# Optimizing a Trainium2 kernel written in Bass

```python
import math
import jax
import jax.numpy as jnp
from jax import lax
import numpy as np
import jax, jax.numpy as jnp

D_MODEL = 2048
BATCH = 1
SEQ = 512
DEPTH = 1

CTX_LEN = 256
GRID_W = 64
N_DIR = 2
D_MIX = D_MODEL
SSD_WIDTH = D_MIX // 2
GDN_WIDTH = D_MIX - SSD_WIDTH
SSD_HEAD_DIM = 64
SSD_HEADS = SSD_WIDTH // SSD_HEAD_DIM
SSD_GROUPS = 2
SSD_HEADS_PER_GROUP = SSD_HEADS // SSD_GROUPS
SSD_STATE = 128
SSD_CONV_DIM = SSD_WIDTH + 2 * SSD_GROUPS * SSD_STATE
GDN_HEAD_DIM = 128
GDN_HEADS = GDN_WIDTH // GDN_HEAD_DIM
GDN_CONV_DIM = 3 * GDN_WIDTH
CONV_K = 5
CHUNK = 128
EPS = 1e-6

OFF_XBC = D_MIX
OFF_DT = OFF_XBC + SSD_CONV_DIM
OFF_QKV = OFF_DT + N_DIR * SSD_HEADS
OFF_BETA = OFF_QKV + GDN_CONV_DIM
OFF_ALPHA = OFF_BETA + N_DIR * GDN_HEADS
IN_DIM = OFF_ALPHA + N_DIR * GDN_HEADS


def rms_norm(x, w):
    xf = x.astype(jnp.float32)
    y = xf * lax.rsqrt(jnp.mean(xf * xf, axis=-1, keepdims=True) + EPS)
    return (y * w.astype(jnp.float32)).astype(x.dtype)

def l2_norm(t):
    return t * lax.rsqrt(jnp.sum(t * t, axis=-1, keepdims=True) + EPS)

def _flip(t):
    return t[:, ::-1]

def _same(t):
    return t

def centred_dwconv(x, w):
    pad = CONV_K // 2
    L = x.shape[1]
    xp = jnp.pad(x, ((0, 0), (pad, pad), (0, 0)))
    out = xp[:, 0:L] * w[0]
    for k in range(1, CONV_K):
        out = out + xp[:, k:k + L] * w[k]
    return out

def conv_latent(x, w):
    bsz, L, ch = x.shape
    rows = L // GRID_W
    y = centred_dwconv(x.reshape(bsz * rows, GRID_W, ch), w)
    return y.reshape(bsz, L, ch)

def _chunks(t):
    return t.reshape(t.shape[0], t.shape[1] // CHUNK, CHUNK, *t.shape[2:])

def ssd_scan(xs, dt, a_neg, bm, cm, h0):
    loga = _chunks(dt * a_neg)
    xdt = _chunks(xs * dt[..., None])
    bmc, cmc = _chunks(bm), _chunks(cm)
    acum = jnp.cumsum(loga, axis=2)
    causal = jnp.tril(jnp.ones((CHUNK, CHUNK), bool))
    a_t = jnp.moveaxis(acum, 2, -1)
    seg = a_t[..., :, None] - a_t[..., None, :]
    lmat = jnp.exp(jnp.where(causal, seg, -jnp.inf))
    cb = jnp.einsum('bcqgn,bcsgn->bcgqs', cmc, bmc)
    y_diag = jnp.einsum('bcgrqs,bcsgrp->bcqgrp', cb[:, :, :, None] * lmat, xdt)
    decay_end = jnp.exp(acum[:, :, -1:] - acum)
    states = jnp.einsum('bcsgn,bcsgrp->bcgrpn', bmc, xdt * decay_end[..., None])
    chunk_decay = jnp.exp(acum[:, :, -1])

    def step(h, inp):
        st, dec = inp
        return h * dec[..., None, None] + st, h

    h_last, h_prev = lax.scan(step, h0, (jnp.moveaxis(states, 1, 0), jnp.moveaxis(chunk_decay, 1, 0)))
    h_prev = jnp.moveaxis(h_prev, 0, 1)
    y_off = jnp.einsum('bcqgn,bcgrpn->bcqgrp', cmc, h_prev) * jnp.exp(acum)[..., None]
    return (y_diag + y_off).reshape(xs.shape), h_last

def gdn_scan(q, k, v, g, beta, s0):
    bsz, L, H, V = v.shape

    def heads_first(t):
        return jnp.moveaxis(_chunks(t), 3, 1)

    q, k, v, g, beta = (heads_first(t) for t in (q, k, v, g, beta))
    gcum = jnp.cumsum(g, axis=-1)
    incl = jnp.tril(jnp.ones((CHUNK, CHUNK), bool))
    strict = jnp.tril(jnp.ones((CHUNK, CHUNK), bool), -1)
    decay = jnp.exp(jnp.where(incl, gcum[..., :, None] - gcum[..., None, :], -jnp.inf))
    k_beta = k * beta[..., None]
    a_strict = jnp.where(strict, jnp.einsum('bhcik,bhcjk->bhcij', k_beta, k) * decay, 0.0)
    rhs = jnp.concatenate([v * beta[..., None], k_beta * jnp.exp(gcum)[..., None]], axis=-1)
    sol = lax.linalg.triangular_solve(a_strict, rhs, left_side=True, lower=True, unit_diagonal=True)
    u, w = sol[..., :V], sol[..., V:]
    attn = jnp.einsum('bhcik,bhcjk->bhcij', q, k) * decay
    q_dec = q * jnp.exp(gcum)[..., None]
    k_end = k * jnp.exp(gcum[..., -1:] - gcum)[..., None]
    chunk_decay = jnp.exp(gcum[..., -1])

    def step(S, inp):
        qd, ke, ui, wi, ai, dec = inp
        v_new = ui - jnp.einsum('bhqk,bhkv->bhqv', wi, S)
        o = jnp.einsum('bhqk,bhkv->bhqv', qd, S) + jnp.einsum('bhqs,bhsv->bhqv', ai, v_new)
        S = S * dec[..., None, None] + jnp.einsum('bhsk,bhsv->bhkv', ke, v_new)
        return S, o

    xs = tuple(jnp.moveaxis(t, 2, 0) for t in (q_dec, k_end, u, w, attn, chunk_decay))
    s_last, o = lax.scan(step, s0, xs)
    o = jnp.moveaxis(jnp.moveaxis(o, 0, 2), 1, 3).reshape(bsz, L, H, V)
    return o, s_last

def ssd_mixer(xbc_c, dt_c, xbc_l, dt_l, a_log, dt_bias, d_skip):
    G, R, P, N = SSD_GROUPS, SSD_HEADS_PER_GROUP, SSD_HEAD_DIM, SSD_STATE
    a_neg = -jnp.exp(a_log.astype(jnp.float32)).reshape(N_DIR, G, R)
    bias = dt_bias.astype(jnp.float32).reshape(N_DIR, G, R)

    def unpack(xbc, dt_raw):
        bsz, L = xbc.shape[:2]
        xbc = xbc.astype(jnp.float32)
        xs = xbc[..., :SSD_WIDTH].reshape(bsz, L, G, R, P)
        bm = xbc[..., SSD_WIDTH:SSD_WIDTH + G * N].reshape(bsz, L, G, N)
        cm = xbc[..., SSD_WIDTH + G * N:].reshape(bsz, L, G, N)
        dt = jax.nn.softplus(dt_raw.astype(jnp.float32).reshape(bsz, L, N_DIR, G, R) + bias)
        return xs, bm, cm, dt

    xc, bc, cc, dtc = unpack(xbc_c, dt_c)
    xl, bl, cl, dtl = unpack(xbc_l, dt_l)
    dsk = d_skip.astype(jnp.float32).reshape(G, R)[..., None]
    y_c, y_l = xc * dsk, xl * dsk
    h0 = jnp.zeros((xc.shape[0], G, R, P, N), jnp.float32)
    for d in range(N_DIR):
        f = _flip if d else _same
        yc_d, h_ctx = ssd_scan(f(xc), f(dtc[:, :, d]), a_neg[d], f(bc), f(cc), h0)
        yl_d, _ = ssd_scan(f(xl), f(dtl[:, :, d]), a_neg[d], f(bl), f(cl), h_ctx)
        y_c = y_c + f(yc_d)
        y_l = y_l + f(yl_d)
    return y_c.reshape(*xc.shape[:2], SSD_WIDTH), y_l.reshape(*xl.shape[:2], SSD_WIDTH)

def gdn_mixer(qkv_c, b_c, a_c, qkv_l, b_l, a_l, a_log, dt_bias):
    H, K = GDN_HEADS, GDN_HEAD_DIM
    rate = jnp.exp(a_log.astype(jnp.float32))
    bias = dt_bias.astype(jnp.float32)

    def unpack(qkv, b_raw, a_raw):
        bsz, L = qkv.shape[:2]
        qkv = qkv.astype(jnp.float32).reshape(bsz, L, 3, H, K)
        q = l2_norm(qkv[:, :, 0]) * (K ** -0.5)
        k = l2_norm(qkv[:, :, 1])
        v = qkv[:, :, 2]
        beta = jax.nn.sigmoid(b_raw.astype(jnp.float32).reshape(bsz, L, N_DIR, H))
        g = -rate * jax.nn.softplus(a_raw.astype(jnp.float32).reshape(bsz, L, N_DIR, H) + bias)
        return q, k, v, beta, g

    qc, kc, vc, bec, gc = unpack(qkv_c, b_c, a_c)
    ql, kl, vl, bel, gl = unpack(qkv_l, b_l, a_l)
    s0 = jnp.zeros((qc.shape[0], H, K, K), jnp.float32)
    o_c = jnp.zeros_like(vc)
    o_l = jnp.zeros_like(vl)
    for d in range(N_DIR):
        f = _flip if d else _same
        oc_d, s_ctx = gdn_scan(f(qc), f(kc), f(vc), f(gc[:, :, d]), f(bec[:, :, d]), s0)
        ol_d, _ = gdn_scan(f(ql), f(kl), f(vl), f(gl[:, :, d]), f(bel[:, :, d]), s_ctx)
        o_c = o_c + f(oc_d)
        o_l = o_l + f(ol_d)
    return o_c, o_l

def ssd_out_norm(y, z, w):
    bsz, L = y.shape[:2]
    yg = (y * jax.nn.silu(z.astype(jnp.float32))).reshape(bsz, L, SSD_GROUPS, SSD_WIDTH // SSD_GROUPS)
    yg = yg * lax.rsqrt(jnp.mean(yg * yg, axis=-1, keepdims=True) + EPS)
    return yg.reshape(bsz, L, SSD_WIDTH) * w.astype(jnp.float32)

def gdn_out_norm(o, z, w):
    bsz, L = o.shape[:2]
    o = o * lax.rsqrt(jnp.mean(o * o, axis=-1, keepdims=True) + EPS) * w.astype(jnp.float32)
    return o.reshape(bsz, L, GDN_WIDTH) * jax.nn.silu(z.astype(jnp.float32))

def _split_proj(p):
    return (p[..., :OFF_XBC], p[..., OFF_XBC:OFF_DT], p[..., OFF_DT:OFF_QKV],
            p[..., OFF_QKV:OFF_BETA], p[..., OFF_BETA:OFF_ALPHA], p[..., OFF_ALPHA:IN_DIM])

def hybrid_layer(h_lat, h_ctx, mod_lat, mod_ctx, pre_w, post_w, w_in, conv_ssd_w, conv_ssd_b,
                 conv_gdn_w, ssd_a_log, ssd_dt_bias, ssd_d, ssd_norm_w, gdn_a_log, gdn_dt_bias,
                 gdn_norm_w, w_out, update_ctx):
    shift_l, scale_l, gate_l = jnp.split(mod_lat, 3, axis=-1)
    shift_c, scale_c, gate_c = jnp.split(mod_ctx, 3, axis=-1)
    u_l = rms_norm(h_lat, pre_w) * (1 + scale_l[:, None]) + shift_l[:, None]
    u_c = rms_norm(h_ctx, pre_w) * (1 + scale_c) + shift_c
    z_l, xbc_l, dt_l, qkv_l, b_l, a_l = _split_proj(u_l @ w_in)
    z_c, xbc_c, dt_c, qkv_c, b_c, a_c = _split_proj(u_c @ w_in)
    xbc_l = jax.nn.silu(conv_latent(xbc_l, conv_ssd_w) + conv_ssd_b)
    xbc_c = jax.nn.silu(centred_dwconv(xbc_c, conv_ssd_w) + conv_ssd_b)
    qkv_l = jax.nn.silu(conv_latent(qkv_l, conv_gdn_w))
    qkv_c = jax.nn.silu(centred_dwconv(qkv_c, conv_gdn_w))
    ssd_c, ssd_l = ssd_mixer(xbc_c, dt_c, xbc_l, dt_l, ssd_a_log, ssd_dt_bias, ssd_d)
    gdn_c, gdn_l = gdn_mixer(qkv_c, b_c, a_c, qkv_l, b_l, a_l, gdn_a_log, gdn_dt_bias)

    def merge(ssd_y, gdn_o, z, dtype):
        y = jnp.concatenate([ssd_out_norm(ssd_y, z[..., :SSD_WIDTH], ssd_norm_w),
                             gdn_out_norm(gdn_o, z[..., SSD_WIDTH:], gdn_norm_w)], axis=-1)
        return rms_norm(y.astype(dtype) @ w_out, post_w)

    h_lat = h_lat + gate_l[:, None] * merge(ssd_l, gdn_l, z_l, h_lat.dtype)
    if update_ctx:
        h_ctx = h_ctx + gate_c * merge(ssd_c, gdn_c, z_c, h_ctx.dtype)
    return h_lat, h_ctx

def _dt_bias_init(key, shape):
    dt = jnp.exp(jax.random.uniform(key, shape, jnp.float32, math.log(1e-3), math.log(1e-1)))
    return dt + jnp.log(-jnp.expm1(-dt))

def first_inputs(seed: int = 0) -> dict:
    key = jax.random.key(seed)
    ks = jax.random.split(key, 20)
    f32 = jnp.float32

    def nrm(k, shape, s):
        return jax.random.normal(k, shape, f32) * s

    return {
        'x': nrm(ks[0], (BATCH, SEQ, D_MODEL), 1.0),
        'c': nrm(ks[1], (BATCH, D_MODEL), 1.0),
        'ctx': nrm(ks[2], (BATCH, CTX_LEN, D_MODEL), 1.0),
        'c_ctx': nrm(ks[3], (D_MODEL,), 1.0),
        'w_ada': nrm(ks[4], (DEPTH, D_MODEL, 3 * D_MODEL), 0.5 * D_MODEL ** -0.5),
        'b_ada': nrm(ks[5], (DEPTH, 3 * D_MODEL), 0.01),
        'pre_norm_w': 1.0 + nrm(ks[6], (DEPTH, D_MODEL), 0.05),
        'post_norm_w': 1.0 + nrm(ks[7], (DEPTH, D_MODEL), 0.05),
        'w_in': nrm(ks[8], (DEPTH, D_MODEL, IN_DIM), D_MODEL ** -0.5),
        'conv_ssd_w': nrm(ks[9], (DEPTH, CONV_K, SSD_CONV_DIM), CONV_K ** -0.5),
        'conv_ssd_b': nrm(ks[10], (DEPTH, SSD_CONV_DIM), 0.02),
        'conv_gdn_w': nrm(ks[11], (DEPTH, CONV_K, GDN_CONV_DIM), CONV_K ** -0.5),
        'ssd_a_log': jnp.log(jax.random.uniform(ks[12], (DEPTH, N_DIR, SSD_HEADS), f32, 1.0, 16.0)),
        'ssd_dt_bias': _dt_bias_init(ks[13], (DEPTH, N_DIR, SSD_HEADS)),
        'ssd_d': 1.0 + nrm(ks[14], (DEPTH, SSD_HEADS), 0.1),
        'ssd_norm_w': 1.0 + nrm(ks[15], (DEPTH, SSD_WIDTH), 0.05),
        'gdn_a_log': jnp.log(jax.random.uniform(ks[16], (DEPTH, N_DIR, GDN_HEADS), f32, 1.0, 16.0)),
        'gdn_dt_bias': _dt_bias_init(ks[17], (DEPTH, N_DIR, GDN_HEADS)),
        'gdn_norm_w': 1.0 + nrm(ks[18], (DEPTH, GDN_HEAD_DIM), 0.05),
        'w_out': nrm(ks[19], (DEPTH, D_MIX, D_MODEL), D_MIX ** -0.5),
    }

def first_block(x, c, ctx, c_ctx, w_ada, b_ada, pre_norm_w, post_norm_w, w_in, conv_ssd_w, conv_ssd_b,
              conv_gdn_w, ssd_a_log, ssd_dt_bias, ssd_d, ssd_norm_w, gdn_a_log, gdn_dt_bias,
              gdn_norm_w, w_out):
    h_lat, h_ctx = x, ctx
    c_act = jax.nn.silu(c)
    cc_act = jax.nn.silu(c_ctx)
    for l in range(DEPTH):
        mod_lat = c_act @ w_ada[l] + b_ada[l]
        mod_ctx = cc_act @ w_ada[l] + b_ada[l]
        h_lat, h_ctx = hybrid_layer(
            h_lat, h_ctx, mod_lat, mod_ctx, pre_norm_w[l], post_norm_w[l], w_in[l],
            conv_ssd_w[l], conv_ssd_b[l], conv_gdn_w[l], ssd_a_log[l], ssd_dt_bias[l], ssd_d[l],
            ssd_norm_w[l], gdn_a_log[l], gdn_dt_bias[l], gdn_norm_w[l], w_out[l],
            update_ctx=(l < DEPTH - 1))
    return h_lat


DEPTH_2 = 2

PLE_DIM = 256
N_EVEN = (DEPTH_2 + 1) // 2
N_ODD = DEPTH_2 // 2
CHUNK_2 = 64
CONV_W = 4
A_DK = 128
A_WIDTH = D_MODEL // 2
A_HEADS = A_WIDTH // A_DK
A_DV = A_WIDTH // A_HEADS
A_QK = A_HEADS * A_DK
B_WIDTH = D_MODEL // 2
B_BLOCK = 128
B_BLOCKS = B_WIDTH // B_BLOCK
LRU_C = 8.0
C_DK = 128
C_DV = 256
C_WIDTH = D_MODEL
C_HEADS = C_WIDTH // C_DV
C_QK = C_HEADS * C_DK
EVEN_IN = 2 * A_QK + 2 * A_WIDTH + 2 * B_WIDTH
EVEN_MIX = A_WIDTH + B_WIDTH
ODD_IN = 2 * C_QK + 3 * C_WIDTH + 2 * C_HEADS
ODD_MIX = C_WIDTH


def rmsnorm(x, g):
    xf = x.astype(jnp.float32)
    y = xf * lax.rsqrt(jnp.mean(xf * xf, axis=-1, keepdims=True) + EPS)
    return (y * g.astype(jnp.float32)).astype(x.dtype)

def head_rmsnorm(y, g):
    b, s, h, d = y.shape
    yn = y * lax.rsqrt(jnp.mean(y * y, axis=-1, keepdims=True) + EPS)
    return (yn * g.astype(jnp.float32).reshape(h, d)).reshape(b, s, h * d)

def causal_conv(u, w, bias):
    k_w = w.shape[0]
    s = u.shape[1]
    up = jnp.pad(u, ((0, 0), (k_w - 1, 0), (0, 0)))
    out = bias
    for k in range(k_w):
        out = out + up[:, k:k + s, :] * w[k]
    return out

def to_chunks(t):
    b, s = t.shape[:2]
    t = t.reshape((b, s // CHUNK_2, CHUNK_2) + t.shape[2:])
    return jnp.moveaxis(t, (1, 3), (0, 2))

def from_chunks(t):
    nc, b, h, c, d = t.shape
    return t.transpose(1, 0, 3, 2, 4).reshape(b, nc * c, h, d)

def hgrn2(q_pre, f_pre, v, lb):
    bsz, s, h, dk = q_pre.shape
    dv = v.shape[-1]
    lb = lb.reshape(h, dk)
    fp = f_pre.astype(jnp.float32)
    q = jax.nn.silu(q_pre.astype(jnp.float32))
    f = lb + (1.0 - lb) * jax.nn.sigmoid(fp)
    log_f = jnp.log(f)
    k = (1.0 - lb) * jax.nn.sigmoid(-fp)
    causal = jnp.tril(jnp.ones((CHUNK_2, CHUNK_2), dtype=bool))

    def step(state, inp):
        qc, kc, vc, gc = inp
        b = jnp.cumsum(gc, axis=2)
        diff = b[:, :, :, None, :] - b[:, :, None, :, :]
        w = jnp.exp(jnp.where(causal[:, :, None], diff, -jnp.inf))
        attn = jnp.einsum('bhtd,bhsd,bhtsd->bhts', qc, kc, w)
        o = (jnp.einsum('bhtd,bhde->bhte', qc * jnp.exp(b), state)
             + jnp.einsum('bhts,bhse->bhte', attn, vc))
        b_last = b[:, :, -1:, :]
        new_state = (jnp.exp(b_last[:, :, 0, :, None]) * state
                     + jnp.einsum('bhsd,bhse->bhde', kc * jnp.exp(b_last - b), vc))
        return new_state, o

    s0 = jnp.zeros((bsz, h, dk, dv), jnp.float32)
    xs = (to_chunks(q), to_chunks(k), to_chunks(v.astype(jnp.float32)), to_chunks(log_f))
    _, o = lax.scan(step, s0, xs)
    return from_chunks(o)

def rg_lru(xc, w_r, b_r, w_i, b_i, lam):
    bsz, s, wdt = xc.shape
    xf = xc.astype(jnp.float32)
    xh = xf.reshape(bsz, s, B_BLOCKS, B_BLOCK)
    r = jax.nn.sigmoid(jnp.einsum('bsnc,ncd->bsnd', xh, w_r.astype(jnp.float32)).reshape(bsz, s, wdt)
                       + b_r.astype(jnp.float32))
    ig = jax.nn.sigmoid(jnp.einsum('bsnc,ncd->bsnd', xh, w_i.astype(jnp.float32)).reshape(bsz, s, wdt)
                        + b_i.astype(jnp.float32))
    log_a = -LRU_C * r * jax.nn.softplus(-lam.astype(jnp.float32))
    a = jnp.exp(log_a)
    u = jnp.sqrt(-jnp.expm1(2.0 * log_a)) * (ig * xf)

    def combine(left, right):
        a1, b1 = left
        a2, b2 = right
        return a1 * a2, a2 * b1 + b2

    _, hs = lax.associative_scan(combine, (a, u), axis=1)
    return hs

def mlstm(q, k, v, li, lf):
    bsz, s, h, dk = q.shape
    dv = v.shape[-1]
    q = q.astype(jnp.float32) * (dk ** -0.5)
    causal = jnp.tril(jnp.ones((CHUNK_2, CHUNK_2), dtype=bool))

    def step(carry, inp):
        c_st, n_st, m_st = carry
        qc, kc, vc, lic, lfc = inp
        b = jnp.cumsum(lfc, axis=-1)
        dmat = jnp.where(causal, b[..., :, None] - b[..., None, :] + lic[..., None, :], -jnp.inf)
        inter = b + m_st[..., None]
        m_t = jnp.maximum(jnp.max(dmat, axis=-1), inter)
        wts = jnp.exp(dmat - m_t[..., None])
        g_inter = jnp.exp(inter - m_t)
        sc = jnp.einsum('bhtd,bhsd->bhts', qc, kc) * wts
        num = (g_inter[..., None] * jnp.einsum('bhtd,bhde->bhte', qc, c_st)
               + jnp.einsum('bhts,bhse->bhte', sc, vc))
        den = g_inter * jnp.einsum('bhtd,bhd->bht', qc, n_st) + jnp.sum(sc, axis=-1)
        hout = num / jnp.maximum(jnp.abs(den), jnp.exp(-m_t))[..., None]
        b_last = b[..., -1]
        logw = b_last[..., None] - b + lic
        m_new = jnp.maximum(b_last + m_st, jnp.max(logw, axis=-1))
        decay = jnp.exp(b_last + m_st - m_new)
        kw = kc * jnp.exp(logw - m_new[..., None])[..., None]
        c_new = decay[..., None, None] * c_st + jnp.einsum('bhsd,bhse->bhde', kw, vc)
        n_new = decay[..., None] * n_st + jnp.sum(kw, axis=2)
        return (c_new, n_new, m_new), hout

    init = (jnp.zeros((bsz, h, dk, dv), jnp.float32),
            jnp.zeros((bsz, h, dk), jnp.float32),
            jnp.zeros((bsz, h), jnp.float32))
    xs = (to_chunks(q), to_chunks(k.astype(jnp.float32)), to_chunks(v.astype(jnp.float32)),
          to_chunks(li), to_chunks(lf))
    _, hs = lax.scan(step, init, xs)
    return from_chunks(hs)

def second_inputs(seed: int = 0) -> dict:
    key = jax.random.key(seed)
    ks = jax.random.split(key, 32)

    def nrm(k, shape, scale):
        return jax.random.normal(k, shape, jnp.float32) * scale

    u = jax.random.uniform(ks[12], (N_EVEN, B_WIDTH), jnp.float32, minval=0.9, maxval=0.999)
    a0 = u ** (1.0 / LRU_C)
    return {
        "x": nrm(ks[0], (BATCH, SEQ, D_MODEL), 1.0),
        "p": nrm(ks[1], (DEPTH_2, BATCH, SEQ, PLE_DIM), 1.0),
        "e_norm": 1.0 + nrm(ks[2], (N_EVEN, D_MODEL), 0.02),
        "e_w_in": nrm(ks[3], (N_EVEN, D_MODEL, EVEN_IN), D_MODEL ** -0.5),
        "a_lb_logits": nrm(ks[4], (N_EVEN + 1, A_QK), 0.1),
        "a_norm": 1.0 + nrm(ks[5], (N_EVEN, A_WIDTH), 0.02),
        "b_conv_w": nrm(ks[6], (N_EVEN, CONV_W, B_WIDTH), CONV_W ** -0.5),
        "b_conv_b": nrm(ks[7], (N_EVEN, B_WIDTH), 0.01),
        "b_w_r": nrm(ks[8], (N_EVEN, B_BLOCKS, B_BLOCK, B_BLOCK), B_BLOCK ** -0.5),
        "b_b_r": nrm(ks[9], (N_EVEN, B_WIDTH), 0.1),
        "b_w_i": nrm(ks[10], (N_EVEN, B_BLOCKS, B_BLOCK, B_BLOCK), B_BLOCK ** -0.5),
        "b_b_i": nrm(ks[11], (N_EVEN, B_WIDTH), 0.1),
        "b_lambda": jnp.log(a0) - jnp.log1p(-a0),
        "e_w_out": nrm(ks[13], (N_EVEN, EVEN_MIX, D_MODEL), EVEN_MIX ** -0.5),
        "o_norm": 1.0 + nrm(ks[14], (N_ODD, D_MODEL), 0.02),
        "o_w_in": nrm(ks[15], (N_ODD, D_MODEL, ODD_IN), D_MODEL ** -0.5),
        "c_conv_w": nrm(ks[16], (N_ODD, CONV_W, 2 * C_QK), CONV_W ** -0.5),
        "c_conv_b": nrm(ks[17], (N_ODD, 2 * C_QK), 0.01),
        "c_b_i": nrm(ks[18], (N_ODD, C_HEADS), 0.1),
        "c_b_f": jnp.linspace(3.0, 6.0, C_HEADS, dtype=jnp.float32)[None, :] + nrm(ks[19], (N_ODD, C_HEADS), 0.1),
        "c_norm": 1.0 + nrm(ks[20], (N_ODD, C_WIDTH), 0.02),
        "o_w_out": nrm(ks[21], (N_ODD, ODD_MIX, D_MODEL), ODD_MIX ** -0.5),
        "ple_w": nrm(ks[22], (DEPTH_2, PLE_DIM, D_MODEL), PLE_DIM ** -0.5),
        "ple_norm": 1.0 + nrm(ks[23], (DEPTH_2, D_MODEL), 0.02),
        "ple_gate_w": nrm(ks[24], (DEPTH_2, D_MODEL, D_MODEL), D_MODEL ** -0.5),
        "final_norm": 1.0 + nrm(ks[25], (D_MODEL,), 0.02),
    }

def second_block(x, p, e_norm, e_w_in, a_lb_logits, a_norm, b_conv_w, b_conv_b, b_w_r, b_b_r,
              b_w_i, b_b_i, b_lambda, e_w_out, o_norm, o_w_in, c_conv_w, c_conv_b, c_b_i,
              c_b_f, c_norm, o_w_out, ple_w, ple_norm, ple_gate_w, final_norm):
    bsz, s, _ = x.shape
    lbs = jnp.cumsum(jax.nn.softmax(a_lb_logits.astype(jnp.float32), axis=0), axis=0)
    h = x
    for i in range(DEPTH_2):
        j = i // 2
        hn = rmsnorm(h, e_norm[j] if i % 2 == 0 else o_norm[j])
        if i % 2 == 0:
            u = hn @ e_w_in[j]
            o0 = 0
            qa = u[..., o0:o0 + A_QK]; o0 += A_QK
            fa = u[..., o0:o0 + A_QK]; o0 += A_QK
            ia = u[..., o0:o0 + A_WIDTH]; o0 += A_WIDTH
            za = u[..., o0:o0 + A_WIDTH]; o0 += A_WIDTH
            xb = u[..., o0:o0 + B_WIDTH]; o0 += B_WIDTH
            zb = u[..., o0:o0 + B_WIDTH]
            ya = hgrn2(qa.reshape(bsz, s, A_HEADS, A_DK), fa.reshape(bsz, s, A_HEADS, A_DK),
                       ia.reshape(bsz, s, A_HEADS, A_DV), lbs[j])
            ya = head_rmsnorm(ya, a_norm[j]) * jax.nn.silu(za.astype(jnp.float32))
            xc = causal_conv(xb, b_conv_w[j], b_conv_b[j])
            yb = rg_lru(xc, b_w_r[j], b_b_r[j], b_w_i[j], b_b_i[j], b_lambda[j])
            yb = yb * jax.nn.silu(zb.astype(jnp.float32))
            y = jnp.concatenate([ya, yb], axis=-1).astype(h.dtype)
            mix = y @ e_w_out[j]
        else:
            u = hn @ o_w_in[j]
            o0 = 0
            qk = u[..., o0:o0 + 2 * C_QK]; o0 += 2 * C_QK
            v = u[..., o0:o0 + C_WIDTH]; o0 += C_WIDTH
            og = u[..., o0:o0 + C_WIDTH]; o0 += C_WIDTH
            z = u[..., o0:o0 + C_WIDTH]; o0 += C_WIDTH
            ig = u[..., o0:o0 + C_HEADS]; o0 += C_HEADS
            fg = u[..., o0:o0 + C_HEADS]
            qk = jax.nn.silu(causal_conv(qk, c_conv_w[j], c_conv_b[j]))
            q = qk[..., :C_QK].reshape(bsz, s, C_HEADS, C_DK)
            k = qk[..., C_QK:].reshape(bsz, s, C_HEADS, C_DK)
            li = ig.astype(jnp.float32) + c_b_i[j].astype(jnp.float32)
            lf = jax.nn.log_sigmoid(fg.astype(jnp.float32) + c_b_f[j].astype(jnp.float32))
            yc = mlstm(q, k, v.reshape(bsz, s, C_HEADS, C_DV), li, lf)
            yc = (head_rmsnorm(yc, c_norm[j]) * jax.nn.sigmoid(og.astype(jnp.float32))
                  * jax.nn.silu(z.astype(jnp.float32)))
            mix = yc.astype(h.dtype) @ o_w_out[j]
        h = h + mix
        pl = rmsnorm(p[i].astype(h.dtype) @ ple_w[i], ple_norm[i])
        h = h + jax.nn.sigmoid(h @ ple_gate_w[i]) * pl
    return rmsnorm(h, final_norm)


def setup_inputs(seed=0):
    out = dict(first_inputs(seed))
    for name, value in second_inputs(seed + 1).items():
        if name != "x":
            out[name + "_2"] = value
    return out


def reference(
    x, c, ctx, c_ctx, w_ada, b_ada, pre_norm_w, post_norm_w, w_in, conv_ssd_w, conv_ssd_b,
    conv_gdn_w, ssd_a_log, ssd_dt_bias, ssd_d, ssd_norm_w, gdn_a_log, gdn_dt_bias, gdn_norm_w,
    w_out, p_2, e_norm_2, e_w_in_2, a_lb_logits_2, a_norm_2, b_conv_w_2, b_conv_b_2, b_w_r_2,
    b_b_r_2, b_w_i_2, b_b_i_2, b_lambda_2, e_w_out_2, o_norm_2, o_w_in_2, c_conv_w_2,
    c_conv_b_2, c_b_i_2, c_b_f_2, c_norm_2, o_w_out_2, ple_w_2, ple_norm_2, ple_gate_w_2,
    final_norm_2,
):
    x = first_block(
        x, c, ctx, c_ctx, w_ada, b_ada, pre_norm_w, post_norm_w, w_in, conv_ssd_w, conv_ssd_b,
        conv_gdn_w, ssd_a_log, ssd_dt_bias, ssd_d, ssd_norm_w, gdn_a_log, gdn_dt_bias,
        gdn_norm_w, w_out,
    )
    return second_block(
        x, p_2, e_norm_2, e_w_in_2, a_lb_logits_2, a_norm_2, b_conv_w_2, b_conv_b_2, b_w_r_2,
        b_b_r_2, b_w_i_2, b_b_i_2, b_lambda_2, e_w_out_2, o_norm_2, o_w_in_2, c_conv_w_2,
        c_conv_b_2, c_b_i_2, c_b_f_2, c_norm_2, o_w_out_2, ple_w_2, ple_norm_2, ple_gate_w_2,
        final_norm_2,
    )


_drawn_inputs = setup_inputs


def setup_inputs(seed=0):
    import zlib

    import numpy as np

    out = dict(_drawn_inputs(seed))
    spreads = {}
    factors = {'ctx': 3.457,
     'c_ctx': 4.806,
     'b_ada': 4.068,
     'post_norm_w': 3.183,
     'conv_ssd_b': 6.318,
     'ssd_d': 4.496,
     'ssd_norm_w': 3.596,
     'gdn_norm_w': 6.105,
     'e_norm_2': 4.794,
     'a_lb_logits_2': 8.0,
     'a_norm_2': 8.0,
     'b_conv_b_2': 3.45,
     'b_b_r_2': 8.0,
     'b_b_i_2': 5.551,
     'o_norm_2': 6.565,
     'c_conv_b_2': 200.0,
     'c_b_i_2': 64.0,
     'c_norm_2': 30.631,
     'ple_norm_2': 39.088,
     'final_norm_2': 20.534}
    for name, (base, spread) in spreads.items():
        noise = np.random.default_rng([zlib.crc32(name.encode()), seed]).standard_normal(out[name].shape)
        drawn = base * np.exp(spread * noise) if base else spread * noise
        out[name] = jnp.asarray(drawn.astype(out[name].dtype))
    for name, factor in factors.items():
        out[name] = (out[name] * factor).astype(out[name].dtype)
    return out
```

```python
from contextlib import ExitStack

import numpy as np
import concourse.bass as bass
from concourse import mybir

F32 = mybir.dt.float32
F32R = mybir.dt.float32r
ALU = mybir.AluOpType
ACT = mybir.ActivationFunctionType
AX = mybir.AxisListType
EXP_LN = "natural_log_exp_and_others"

P = 128
D = 2048
KD = D // P
LAT = 512
CTX = 256
TOK = CTX + LAT
GRID_W = 64
EPS = 1e-6
CHUNKS = TOK // P
CTX_CHUNKS = CTX // P
NEG = -1.0e30
LEVELS = 7
WCOLS = 256


def stage(build):
    def run(nc, *args, **kwargs):
        before = nc.snapshot_sems()
        build(nc, *args, **kwargs)
        nc.clear_and_free_semaphores(nc.allocated_since(before))
        nc.all_engine_barrier()
    return run


class Sig:

    def __init__(self, sem, per=1, base=0):
        self.sem, self.per, self.base = sem, per, base

    def value(self, it, n):
        return it * self.per + (self.base + n)


class Chain(Sig):

    def __init__(self, sem, per=1, base=0):
        super().__init__(sem, per, base)
        self.n = 0

    def step(self, ins):
        self.n += 1
        return ins.then_inc(self.sem, 1)

    def close(self):
        assert self.n == self.per, f"this loop's chain has {self.n} steps, not {self.per}"
        self.n = 0


def chain_links(eng, chain, it):
    def settle():
        eng.wait_ge(chain.sem, chain.value(it, chain.n))
    return chain.step, settle


def constants():
    r = np.arange(P)
    ident = np.eye(P, dtype=np.float32)
    causal = np.stack([r[:, None] <= r[None, :], r[:, None] >= r[None, :]]).astype(np.float32)
    neg = np.where(causal > 0, 0.0, NEG).astype(np.float32)
    low = []
    for lev in range(LEVELS):
        b = 1 << lev
        blk, half = r // (2 * b), (r // b) % 2
        low.append((blk[:, None] == blk[None, :]) & (half[:, None] == 1) & (half[None, :] == 0))
    low = np.stack(low).astype(np.float32)
    pair = np.stack([low, low.transpose(0, 2, 1)], axis=1)
    scan = np.concatenate([low.transpose(0, 2, 1), ident[None]])
    chunk_start = np.ones((P, LAT), np.float32)
    chunk_start[:, ::P] = 0.0
    last_row = np.zeros((P, P), np.float32)
    last_row[P - 1] = 1.0
    return {
        "c_ident": ident,
        "c_ones": np.ones((P, P), np.float32),
        "c_causal": np.ascontiguousarray(causal.transpose(1, 0, 2)).reshape(P, 2 * P),
        "c_neg": np.ascontiguousarray(neg.transpose(1, 0, 2)).reshape(P, 2 * P),
        "c_pair": np.ascontiguousarray(pair.transpose(2, 0, 1, 3)).reshape(P, LEVELS * 2 * P),
        "c_scan": np.ascontiguousarray(scan.transpose(1, 0, 2)).reshape(P, (LEVELS + 1) * P),
        "c_start": chunk_start,
        "c_last": last_row,
    }


GDN_H = 8
GDN_TABS = 5


@stage
def gdn_stage(nc, consts, qkvT, tabs, gnorm, zT, yT):
    PROB = 2 * CHUNKS
    ORDER = [list(range(CHUNKS)), [1, 0, 5, 4, 3, 2]]
    ident, ones, neg, pair = consts["ident"], consts["ones"], consts["neg"], consts["pair"]
    with ExitStack() as ctx:
        def sb(name, *shape):
            return ctx.enter_context(nc.sbuf_tensor("gdn_" + name, [P, *shape], F32))

        def sig(name, per=1, base=0):
            return Sig(nc.alloc_semaphore("gdn_" + name), per, base)

        raw_q, raw_k, raw_v = sb("raw_q", LAT), sb("raw_k", TOK), sb("raw_v", TOK)
        z_in = sb("z_in", LAT)
        sq_k, sq_q = sb("sq_k", TOK), sb("sq_q", LAT)
        k_n, q_n = sb("k_n", TOK), sb("q_n", LAT)
        k_tok, v_tok = sb("k_tok", CHUNKS, P), sb("v_tok", CHUNKS, P)
        tab = sb("tab", GDN_TABS, CHUNKS, 2)
        ncum = sb("ncum", CHUNKS, 2)
        dec = sb("dec", CHUNKS, 2, P)
        qdec = sb("qdec", CHUNKS - CTX_CHUNKS, 2, P)
        a_t = sb("a_t", CHUNKS, 2, P)
        attn = sb("attn", CHUNKS - CTX_CHUNKS, 2, P)
        x_m, y_m = sb("x_m", CHUNKS, 2, P), sb("y_m", CHUNKS, 2, P)
        t1 = sb("t1", CHUNKS, 2, P)
        k_grow, k_end = sb("k_grow", CHUNKS, 2, P), sb("k_end", CHUNKS, 2, P)
        w_neg = sb("w_neg", CHUNKS, 2, P)
        state, v_new = sb("state", 2, P), sb("v_new", 2, P)
        o_dir, o_sum, o_sq, y_out = sb("o_dir", 2, LAT), sb("o_sum", LAT), sb("o_sq", LAT), sb("y_out", LAT)
        eps, ln_scale = sb("eps", 1), sb("ln_scale", 1)
        bank = [ctx.enter_context(nc.psum_tensor(f"gdn_bank{i}", [P, 512], F32)) for i in range(8)]

        def quad(i):
            return bank[i][:, :].rearrange("p (c d q) -> p c d q", c=2, d=2)

        loaded = sig("loaded", 64)
        head_done = sig("head_done", 1, 1)
        stored = sig("stored", 16, 16)
        consts_set = sig("consts_set")
        staged = sig("staged", 2)
        squared = sig("squared", 2)
        sums = sig("sums", 3)
        inv_norm = sig("inv_norm", 3)
        normed = sig("normed", 2)
        v_turned, v_copied = sig("v_turned"), sig("v_copied", 2)
        k_turned, k_copied = sig("k_turned"), sig("k_copied", 2)
        dmat, dec_read = sig("dmat", 3), sig("dec_read", 3)
        emat, qdec_set = sig("emat", 2), sig("qdec_set", 2)
        q_decayed = sig("q_decayed", 1)
        products, a_set, attn_set = sig("products", 3), sig("a_set", 3), sig("attn_set", 2)
        first_m, first_t, first_set = sig("first_m", 3), sig("first_t", 3), sig("first_set", 3)
        t1_ready, t1_set = sig("t1_ready", 18), sig("t1_set", 18)
        t2_ready, xy_set = sig("t2_ready", 18), sig("xy_set", 18)
        k_scaled = sig("k_scaled", 2)
        w_ready, w_set = sig("w_ready", 3), sig("w_set", 3)
        v_ready, v_set = sig("v_ready", 12), sig("v_set", 12)
        o_ready, o_set = sig("o_ready", 8), sig("o_set", 8)
        s_ready, s_set = sig("s_ready", 10), sig("s_set", 10)
        o_squared, o_sums, o_inv = sig("o_squared"), sig("o_sums"), sig("o_inv")
        act_chain = Chain(sig("act_chain").sem, 4)
        dve_chain = Chain(sig("dve_chain").sem, 5)

        block = ctx.enter_context(nc.Block())

        @block.sync
        def _(sp):
            def load_qkv(h):
                sp.dma_start(raw_q[:], qkvT[h, :, CTX:TOK]).then_inc(loaded.sem, 16)
                sp.dma_start(raw_k[:], qkvT[h + GDN_H]).then_inc(loaded.sem, 16)
                sp.dma_start(raw_v[:], qkvT[h + 2 * GDN_H]).then_inc(loaded.sem, 16)

            load_qkv(0)
            sp.dma_start(z_in[:], zT[0]).then_inc(loaded.sem, 16)
            with sp.Fori(1, GDN_H) as h:
                sp.wait_ge(normed.sem, normed.value(h - 1, 2))
                load_qkv(h)
                sp.wait_ge(head_done.sem, head_done.value(h - 1, 1))
                sp.dma_start(z_in[:], zT[h]).then_inc(loaded.sem, 16)
                sp.dma_start(yT[h - 1], y_out[:]).then_inc(stored.sem, 16)
            sp.wait_ge(head_done.sem, head_done.value(GDN_H - 1, 1))
            sp.dma_start(yT[GDN_H - 1], y_out[:]).then_inc(stored.sem, 16)
            sp.wait_ge(stored.sem, stored.value(GDN_H, 0))

        @block.tensor
        def _(pe):
            with pe.Fori(0, GDN_H) as h:
                pe.wait_ge(head_done.sem, head_done.value(h, 0))
                pe.wait_ge(squared.sem, squared.value(h, 1))
                pe.matmul(bank[0][:, :], ones[:], sq_k[:, 0:512], start=True, stop=True).then_inc(sums.sem, 1)
                pe.matmul(bank[1][:, 0:256], ones[:], sq_k[:, 512:TOK], start=True, stop=True).then_inc(sums.sem, 1)
                pe.wait_ge(squared.sem, squared.value(h, 2))
                pe.matmul(bank[2][:, :], ones[:], sq_q[:], start=True, stop=True).then_inc(sums.sem, 1)
                pe.wait_ge(loaded.sem, loaded.value(h, 64))
                for c in range(CHUNKS):
                    last = pe.transpose(bank[5 + c // 4][:, (c % 4) * P:(c % 4 + 1) * P],
                                        raw_v[:, c * P:(c + 1) * P], ident[:])
                last.then_inc(v_turned.sem, 1)
                pe.wait_ge(staged.sem, staged.value(h, 2))
                for b, i in enumerate((3, 4, 7)):
                    for c in range(2):
                        for d in range(2):
                            pe.matmul(quad(i)[:, c, d, :], tab[:, 4, 2 * b + c, d:d + 1].to_broadcast([P, P]),
                                      ident[:], start=(c == 0 and d == 0), stop=False)
                    last = pe.matmul(quad(i), ident[:], neg[:].unsqueeze(1).to_broadcast([P, 2, 2, P]),
                                     start=False, stop=True)
                    last.then_inc(dmat.sem, 1)
                for b, i in enumerate((0, 1)):
                    pe.wait_ge(inv_norm.sem, inv_norm.value(h, 2))
                    for c in range(2):
                        for d in range(2):
                            last = pe.matmul(quad(i)[:, c, d, :],
                                             tab[:, 4, 2 * b + 2 + c, d:d + 1].to_broadcast([P, P]),
                                             ident[:], start=True, stop=True)
                    last.then_inc(emat.sem, 1)
                pe.wait_ge(normed.sem, normed.value(h, 1))
                pe.wait_ge(v_copied.sem, v_copied.value(h, 2))
                for c in range(CHUNKS):
                    last = pe.transpose(bank[5 + c // 4][:, (c % 4) * P:(c % 4 + 1) * P],
                                        k_n[:, c * P:(c + 1) * P], ident[:])
                last.then_inc(k_turned.sem, 1)
                pe.wait_ge(inv_norm.sem, inv_norm.value(h, 3))
                for c in range(CHUNKS):
                    if c == 4:
                        pe.wait_ge(dec_read.sem, dec_read.value(h, 1))
                    kc = k_n[:, c * P:(c + 1) * P]
                    last = pe.matmul(bank[2 + c // 4][:, (c % 4) * P:(c % 4 + 1) * P], kc, kc, start=True, stop=True)
                    if c in (3, 5):
                        last.then_inc(products.sem, 1)
                pe.wait_ge(dec_read.sem, dec_read.value(h, 2))
                pe.wait_ge(normed.sem, normed.value(h, 2))
                for c in range(CTX_CHUNKS, CHUNKS):
                    j = c - CTX_CHUNKS
                    last = pe.matmul(bank[4][:, j * P:(j + 1) * P], k_n[:, c * P:(c + 1) * P],
                                     q_n[:, j * P:(j + 1) * P], start=True, stop=True)
                last.then_inc(products.sem, 1)
                for b in range(3):
                    pe.wait_ge(first_m.sem, first_m.value(h, b + 1))
                    if b < 2:
                        pe.wait_ge(qdec_set.sem, qdec_set.value(h, b + 1))
                    else:
                        pe.wait_ge(a_set.sem, a_set.value(h, 3))
                    for c in range(2):
                        for d in range(2):
                            last = pe.matmul(quad(b)[:, c, d, :], t1[:, 2 * b + c, d, :], ident[:],
                                             start=True, stop=True)
                    last.then_inc(first_t.sem, 1)
                n = 0
                for lev in range(1, LEVELS):
                    for b in range(3):
                        if lev == 1:
                            pe.wait_ge(first_set.sem, first_set.value(h, b + 1))
                        else:
                            pe.wait_ge(xy_set.sem, xy_set.value(h, n - 3 + b + 1))
                        for c in range(2):
                            for d in range(2):
                                p = 2 * b + c
                                last = pe.matmul(quad(b)[:, c, d, :], a_t[:, p, d, :], x_m[:, p, d, :],
                                                 start=True, stop=True)
                        last.then_inc(t1_ready.sem, 1)
                    for b in range(3):
                        pe.wait_ge(t1_set.sem, t1_set.value(h, n + b + 1))
                        if lev == 1 and b == 0:
                            pe.wait_ge(a_set.sem, a_set.value(h, 3))
                        if lev == 1 and b == 1:
                            pe.wait_ge(attn_set.sem, attn_set.value(h, 2))
                        if lev == 1 and b == 2:
                            pe.wait_ge(k_copied.sem, k_copied.value(h, 2))
                        for c in range(2):
                            for d in range(2):
                                p = 2 * b + c
                                last = pe.matmul(quad(3 + b)[:, c, d, :], t1[:, p, d, :], y_m[:, p, d, :],
                                                 start=True, stop=True)
                                if lev < LEVELS - 1:
                                    last = pe.matmul(quad(b)[:, c, d, :], y_m[:, p, d, :], t1[:, p, d, :],
                                                     start=True, stop=True)
                        last.then_inc(t2_ready.sem, 1)
                    n += 3
                pe.wait_ge(k_scaled.sem, k_scaled.value(h, 1))
                for b in range(3):
                    pe.wait_ge(xy_set.sem, xy_set.value(h, 15 + b + 1))
                    for c in range(2):
                        for d in range(2):
                            p = 2 * b + c
                            last = pe.matmul(quad(b)[:, c, d, :], k_grow[:, p, d, :], y_m[:, p, d, :],
                                             start=True, stop=True)
                    last.then_inc(w_ready.sem, 1)
                pe.wait_ge(w_set.sem, w_set.value(h, 3))
                pe.wait_ge(k_scaled.sem, k_scaled.value(h, 2))
                pe.wait_ge(q_decayed.sem, q_decayed.value(h, 1))
                n_o = 0
                for j in range(CHUNKS):
                    for d in range(2):
                        c = ORDER[d][j]
                        if j > 0:
                            pe.wait_ge(s_set.sem, s_set.value(h, 2 * j - 1 + d))
                        mm = pe.matmul(bank[3 + d][:, 0:P], y_m[:, c, d, :], v_tok[:, c, :],
                                       start=True, stop=(j == 0))
                        if j > 0:
                            mm = pe.matmul(bank[3 + d][:, 0:P], w_neg[:, c, d, :], state[:, d, :],
                                           start=False, stop=True)
                        mm.then_inc(v_ready.sem, 1)
                    for d in range(2):
                        c = ORDER[d][j]
                        pe.wait_ge(v_set.sem, v_set.value(h, 2 * j + d + 1))
                        if j < CHUNKS - 1:
                            pe.matmul(bank[7 * (1 - d)][:, 0:P], k_end[:, c, d, :], v_new[:, d, :],
                                      start=True, stop=True).then_inc(s_ready.sem, 1)
                        if c >= CTX_CHUNKS:
                            if n_o >= 2:
                                pe.wait_ge(o_set.sem, o_set.value(h, n_o - 1))
                            pe.matmul(bank[5 + d][:, 0:P], state[:, d, :], qdec[:, c - 2, d, :],
                                      start=True, stop=False)
                            pe.matmul(bank[5 + d][:, 0:P], v_new[:, d, :], attn[:, c - 2, d, :],
                                      start=False, stop=True).then_inc(o_ready.sem, 1)
                            n_o += 1
                pe.wait_ge(o_squared.sem, o_squared.value(h, 1))
                pe.matmul(bank[1][:, :], ones[:], o_sq[:], start=True, stop=True).then_inc(o_sums.sem, 1)

        @block.scalar
        def _(act):
            act.preload_act_table_set(EXP_LN)
            act.wait_ge(consts_set.sem, 2)
            with act.Fori(0, GDN_H) as h:
                do, settle = chain_links(act, act_chain, h)
                act.wait_ge(head_done.sem, head_done.value(h, 0))
                act.wait_ge(loaded.sem, loaded.value(h, 64))
                act.activation(sq_k[:], raw_k[:], ACT.Square).then_inc(squared.sem, 1)
                act.activation(sq_q[:], raw_q[:], ACT.Square).then_inc(squared.sem, 1)
                for n, (i, dst) in enumerate(((0, sq_k[:, 0:512]), (1, sq_k[:, 512:TOK]), (2, sq_q[:]))):
                    act.wait_ge(sums.sem, sums.value(h, n + 1))
                    do(act.activation(dst, bank[i][:, 0:dst.shape[1]], ACT.Ln, bias=eps[:, 0:1]))
                    settle()
                    bias = ln_scale[:, 0:1] if n == 2 else 0.0
                    act.activation(dst, dst, ACT.Exp, scale=-0.5, bias=bias).then_inc(inv_norm.sem, 1)
                act.wait_ge(v_turned.sem, v_turned.value(h, 1))
                act.activation(v_tok[:, 0:4, :], bank[5][:, :].rearrange("p (c q) -> p c q", c=4),
                               ACT.Copy).then_inc(v_copied.sem, 1)
                act.activation(v_tok[:, 4:6, :], bank[6][:, 0:256].rearrange("p (c q) -> p c q", c=2),
                               ACT.Copy).then_inc(v_copied.sem, 1)
                act.wait_ge(staged.sem, staged.value(h, 2))
                for b, i in enumerate((3, 4, 7)):
                    act.wait_ge(dmat.sem, dmat.value(h, b + 1))
                    for c in range(2):
                        for d in range(2):
                            ins = act.activation(dec[:, 2 * b + c, d, :], quad(i)[:, c, d, :], ACT.Exp,
                                                 bias=ncum[:, 2 * b + c, d:d + 1])
                    ins.then_inc(dec_read.sem, 1)
                for b in range(2):
                    act.wait_ge(emat.sem, emat.value(h, b + 1))
                    act.activation(qdec[:, 2 * b:2 * b + 2, :, :], quad(b), ACT.Exp).then_inc(qdec_set.sem, 1)
                act.wait_ge(k_turned.sem, k_turned.value(h, 1))
                act.activation(k_tok[:, 0:4, :], bank[5][:, :].rearrange("p (c q) -> p c q", c=4),
                               ACT.Copy).then_inc(k_copied.sem, 1)
                act.activation(k_tok[:, 4:6, :], bank[6][:, 0:256].rearrange("p (c q) -> p c q", c=2),
                               ACT.Copy).then_inc(k_copied.sem, 1)
                for b in range(3):
                    act.wait_ge(w_ready.sem, w_ready.value(h, b + 1))
                    act.activation(w_neg[:, 2 * b:2 * b + 2, :, :], quad(b), ACT.Copy, scale=-1.0).then_inc(w_set.sem, 1)
                n_o = 0
                for j in range(CHUNKS):
                    for d in range(2):
                        c = ORDER[d][j]
                        if c >= CTX_CHUNKS:
                            act.wait_ge(o_ready.sem, o_ready.value(h, n_o + 1))
                            act.activation(o_dir[:, d, (c - 2) * P:(c - 1) * P], bank[5 + d][:, 0:P],
                                           ACT.Copy).then_inc(o_set.sem, 1)
                            n_o += 1
                act.wait_ge(o_sums.sem, o_sums.value(h, 1))
                do(act.activation(o_sq[:], bank[1][:, :], ACT.Ln, scale=1.0 / P, bias=eps[:, 0:1]))
                settle()
                act.activation(o_sq[:], o_sq[:], ACT.Exp, scale=-0.5).then_inc(o_inv.sem, 1)
                act_chain.close()

        @block.gpsimd
        def _(pool):
            with pool.Fori(0, GDN_H) as h:
                pool.wait_ge(head_done.sem, head_done.value(h, 0))
                pool.wait_ge(staged.sem, staged.value(h, 1))
                pool.wait_ge(normed.sem, normed.value(h, 2))
                pool.wait_ge(qdec_set.sem, qdec_set.value(h, 2))
                pool.tensor_tensor(qdec[:], qdec[:], q_n[:].rearrange("p (c q) -> p c q", c=4).unsqueeze(2)
                                   .to_broadcast([P, 4, 2, P]), ALU.mult).then_inc(q_decayed.sem, 1)
                pool.wait_ge(k_copied.sem, k_copied.value(h, 2))
                k_both = k_tok[:].unsqueeze(2).to_broadcast([P, CHUNKS, 2, P])
                for t, dst in ((1, k_grow), (2, k_end)):
                    pool.tensor_tensor(dst[:], k_both, tab[:, t, :, :].unsqueeze(3).to_broadcast([P, CHUNKS, 2, P]),
                                       ALU.mult).then_inc(k_scaled.sem, 1)

        @block.vector
        def _(dve):
            dve.memset(eps[:], EPS).then_inc(consts_set.sem, 1)
            dve.memset(ln_scale[:], float(-0.5 * np.log(P))).then_inc(consts_set.sem, 1)
            dve.sem_inc(head_done.sem, 1)
            dve.sem_inc(stored.sem, 16)
            with dve.Fori(0, GDN_H) as h:
                do, settle = chain_links(dve, dve_chain, h)
                dve.tensor_copy(tab[:].rearrange("p t c d -> p (t c d)"),
                                   tabs[:].rearrange("p t c d h -> p (t c d) h")[:, :, bass.ds(h, 1)]
                                   .rearrange("p x h -> p (x h)")).then_inc(staged.sem, 1)
                dve.wait_ge(staged.sem, staged.value(h, 1))
                dve.tensor_scalar(ncum[:], tab[:, 4, :, :], -1.0, None, ALU.mult).then_inc(staged.sem, 1)
                dve.wait_ge(inv_norm.sem, inv_norm.value(h, 2))
                dve.tensor_tensor(k_n[:], raw_k[:], sq_k[:], ALU.mult).then_inc(normed.sem, 1)
                dve.wait_ge(inv_norm.sem, inv_norm.value(h, 3))
                dve.wait_ge(v_copied.sem, v_copied.value(h, 2))
                dve.tensor_tensor(q_n[:], raw_q[:], sq_q[:], ALU.mult).then_inc(normed.sem, 1)
                for c in range(CHUNKS):
                    if c in (0, 4):
                        dve.wait_ge(products.sem, products.value(h, 1 + c // 4))
                    if c % 2 == 0:
                        dve.wait_ge(dec_read.sem, dec_read.value(h, 1 + c // 2))
                    for d in range(2):
                        ins = dve.scalar_tensor_tensor(a_t[:, c, d, :], bank[2 + c // 4][:, (c % 4) * P:(c % 4 + 1) * P],
                                                       tab[:, 0, c, d:d + 1], dec[:, c, d, :], ALU.mult, ALU.mult)
                    if c % 2 == 1:
                        ins.then_inc(a_set.sem, 1)
                dve.wait_ge(products.sem, products.value(h, 3))
                kq = bank[4][:, :].rearrange("p (c q) -> p c q", c=4)
                for b in range(2):
                    dve.tensor_tensor(attn[:, 2 * b:2 * b + 2, :, :],
                                      kq[:, 2 * b:2 * b + 2, :].unsqueeze(2).to_broadcast([P, 2, 2, P]),
                                      dec[:, 2 * b + 2:2 * b + 4, :, :], ALU.mult).then_inc(attn_set.sem, 1)
                corner = pair[:, 0, :, :]
                ident4 = ident[:].unsqueeze(1).unsqueeze(1).to_broadcast([P, 2, 2, P])
                for b in range(3):
                    s = slice(2 * b, 2 * b + 2)
                    dve.wait_ge(a_set.sem, a_set.value(h, b + 1))
                    for d in range(2):
                        ins = dve.tensor_tensor(t1[:, s, d, :], a_t[:, s, d, :],
                                                corner[:, 1 - d, :].unsqueeze(1).to_broadcast([P, 2, P]), ALU.mult)
                    ins.then_inc(first_m.sem, 1)
                for b in range(3):
                    s = slice(2 * b, 2 * b + 2)
                    dve.wait_ge(first_m.sem, first_m.value(h, b + 1))
                    do(dve.tensor_tensor(y_m[:, s, :, :], ident4, t1[:, s, :, :], ALU.subtract))
                    dve.wait_ge(first_t.sem, first_t.value(h, b + 1))
                    dve.tensor_tensor(x_m[:, s, :, :], ident4, quad(b), ALU.subtract).then_inc(first_set.sem, 1)
                n = 0
                for lev in range(1, LEVELS):
                    for b in range(3):
                        s = slice(2 * b, 2 * b + 2)
                        dve.wait_ge(t1_ready.sem, t1_ready.value(h, n + b + 1))
                        dve.tensor_tensor(t1[:, s, :, :], quad(b),
                                          pair[:, lev, :, :].unsqueeze(1).to_broadcast([P, 2, 2, P]),
                                          ALU.mult).then_inc(t1_set.sem, 1)
                    for b in range(3):
                        s = slice(2 * b, 2 * b + 2)
                        dve.wait_ge(t2_ready.sem, t2_ready.value(h, n + b + 1))
                        ins = dve.tensor_tensor(y_m[:, s, :, :], y_m[:, s, :, :], quad(3 + b), ALU.subtract)
                        if lev < LEVELS - 1:
                            ins = dve.tensor_tensor(x_m[:, s, :, :], x_m[:, s, :, :], quad(b), ALU.subtract)
                        ins.then_inc(xy_set.sem, 1)
                    n += 3
                for j in range(CHUNKS):
                    for d in range(2):
                        c = ORDER[d][j]
                        dve.wait_ge(v_ready.sem, v_ready.value(h, 2 * j + d + 1))
                        dve.tensor_scalar(v_new[:, d, :], bank[3 + d][:, 0:P], tab[:, 0, c, d:d + 1], None,
                                          ALU.mult).then_inc(v_set.sem, 1)
                    if j == CHUNKS - 1:
                        break
                    for d in range(2):
                        c = ORDER[d][j]
                        dve.wait_ge(s_ready.sem, s_ready.value(h, 2 * j + d + 1))
                        if c >= CTX_CHUNKS:
                            dve.wait_ge(o_ready.sem, o_ready.value(h, 2 * (j - 2) + d + 1))
                        s_new = bank[7 * (1 - d)][:, 0:P]
                        if j == 0:
                            dve.tensor_copy(state[:, d, :], s_new).then_inc(s_set.sem, 1)
                        else:
                            dve.scalar_tensor_tensor(state[:, d, :], state[:, d, :], tab[:, 3, c, d:d + 1], s_new,
                                                     ALU.mult, ALU.add).then_inc(s_set.sem, 1)
                dve.wait_ge(o_set.sem, o_set.value(h, 8))
                do(dve.tensor_tensor(o_sum[:], o_dir[:, 0, :], o_dir[:, 1, :], ALU.add))
                settle()
                dve.tensor_tensor(o_sq[:], o_sum[:], o_sum[:], ALU.mult).then_inc(o_squared.sem, 1)
                dve.wait_ge(o_inv.sem, o_inv.value(h, 1))
                do(dve.tensor_tensor(o_sum[:], o_sum[:], o_sq[:], ALU.mult))
                settle()
                dve.wait_ge(stored.sem, stored.value(h, 0))
                dve.scalar_tensor_tensor(y_out[:], o_sum[:], gnorm, z_in[:], ALU.mult,
                                         ALU.mult).then_inc(head_done.sem, 1)
                dve_chain.close()


SSD_H = 16
SSD_G = 2
HPG = SSD_H // SSD_G
SSD_P = 64
GW = HPG * SSD_P
GB = GW // P
SSD_TABS = 4


@stage
def ssd_stage(nc, consts, xbcT, tabs, skip, norm_w, zT, yT):
    LC = CHUNKS - CTX_CHUNKS
    ORDER = [list(range(CHUNKS)), [1, 0, 5, 4, 3, 2]]
    EXPO_BANK = [0, 1, 5, 6]
    ident, ones, neg = consts["ident"], consts["ones"], consts["neg"]
    with ExitStack() as ctx:
        def sb(name, *shape):
            return ctx.enter_context(nc.sbuf_tensor("ssd_" + name, [P, *shape], F32))

        def sig(name, per=1, base=0):
            return Sig(nc.alloc_semaphore("ssd_" + name), per, base)

        x_in, b_in, c_in, z_in = sb("x_in", GB, TOK), sb("b_in", TOK), sb("c_in", TOK), sb("z_in", GB, LAT)
        x_tok, b_tok = sb("x_tok", CHUNKS, GW), sb("b_tok", CHUNKS, P)
        cb = sb("cb", LC, P)
        tab, ncum = sb("tab", SSD_TABS, CHUNKS, 2, HPG), sb("ncum", CHUNKS, 2, HPG)
        sk, nw = sb("sk", GB), sb("nw", GB)
        x_w = sb("x_w", 2, GW)
        x_dt = sb("x_dt", LC, 2, GW)
        h_state = sb("h_state", 2, CHUNKS - 1, GW)
        grow, expo = sb("grow", 2, 4, P), sb("expo", 2, 4, P)
        c_grow, dec = sb("c_grow", 2, 4, 4, P), sb("dec", 2, 4, 4, P)
        y_g, y_sq, inv = sb("y_g", GB, LAT), sb("y_sq", GB, LAT), sb("inv", LAT)
        eps = sb("eps", 1)
        bank = [ctx.enter_context(nc.psum_tensor(f"ssd_bank{i}", [P, 512], F32)) for i in range(8)]

        NB = 4 * LC
        group_done = sig("group_done", GB, GB)
        loaded = sig("loaded", 64)
        stored = sig("stored", 16, 16)
        consts_set = sig("consts_set")
        staged = sig("staged", 4)
        turned, copied = sig("turned", CHUNKS + 2), sig("copied", CHUNKS + 2)
        cb_ready, cb_set = sig("cb_ready"), sig("cb_set")
        xw_set, add_ready, h_set = sig("xw_set", 10), sig("add_ready", 10), sig("h_set", 10)
        h_decayed = sig("h_decayed", 8)
        xdt_set = sig("xdt_set", LC)
        cum_ready, grow_set, expo_set = sig("cum_ready", NB), sig("grow_set", NB), sig("expo_set", NB)
        dec_exp, dec_set, cgrow_set = sig("dec_exp", NB), sig("dec_set", NB), sig("cgrow_set", NB)
        y_mms = sig("y_mms", LC)
        y_skip, y_gated, squares = sig("y_skip", LC), sig("y_gated", LC), sig("squares")
        sums, inv_ln, inv_set = sig("sums"), sig("inv_ln"), sig("inv_set")

        block = ctx.enter_context(nc.Block())

        @block.sync
        def _(sp):
            with sp.Fori(0, SSD_G) as g:
                sp.wait_ge(group_done.sem, group_done.value(g, 0))
                sp.dma_start(x_in[:], xbcT[bass.ds(g * GB, GB)].rearrange("b p t -> p b t")).then_inc(loaded.sem, 16)
                sp.dma_start(b_in[:], xbcT[g + 8]).then_inc(loaded.sem, 16)
                sp.dma_start(c_in[:], xbcT[g + 10]).then_inc(loaded.sem, 16)
                sp.dma_start(z_in[:], zT[bass.ds(g * GB, GB)].rearrange("b p t -> p b t")).then_inc(loaded.sem, 16)
                sp.wait_ge(group_done.sem, group_done.value(g, GB))
                sp.dma_start(yT[bass.ds(g * GB, GB)].rearrange("b p t -> p b t"), y_g[:]).then_inc(stored.sem, 16)
            sp.wait_ge(stored.sem, stored.value(SSD_G, 0))

        @block.tensor
        def _(pe):
            with pe.Fori(0, SSD_G) as g:
                pe.wait_ge(group_done.sem, group_done.value(g, 0))
                pe.wait_ge(loaded.sem, loaded.value(g, 64))
                for r in range(CHUNKS + 2):
                    if r >= 4:
                        pe.wait_ge(copied.sem, copied.value(g, r - 3))
                    for i in range(4):
                        if r < CHUNKS:
                            src = x_in[:, i, r * P:(r + 1) * P]
                        elif 4 * (r - CHUNKS) + i < CHUNKS:
                            c = 4 * (r - CHUNKS) + i
                            src = b_in[:, c * P:(c + 1) * P]
                        else:
                            break
                        last = pe.transpose(bank[r % 4][:, i * P:(i + 1) * P], src, ident[:])
                    last.then_inc(turned.sem, 1)
                for c in range(CTX_CHUNKS, CHUNKS):
                    j = c - CTX_CHUNKS
                    last = pe.matmul(bank[4][:, j * P:(j + 1) * P], b_in[:, c * P:(c + 1) * P],
                                     c_in[:, c * P:(c + 1) * P], start=True, stop=True)
                last.then_inc(cb_ready.sem, 1)
                pe.wait_ge(copied.sem, copied.value(g, CHUNKS + 2))
                for j in range(CHUNKS - 1):
                    for d in range(2):
                        pe.wait_ge(xw_set.sem, xw_set.value(g, 2 * j + d + 1))
                        if j > 0:
                            pe.wait_ge(h_set.sem, h_set.value(g, 2 * j + d - 1))
                        pe.matmul(bank[5 + d][:, :], b_tok[:, ORDER[d][j], :], x_w[:, d, :],
                                  start=True, stop=True).then_inc(add_ready.sem, 1)
                pe.wait_ge(staged.sem, staged.value(g, 4))

                def exponents(c):
                    for m in range(4):
                        n = 4 * c + m
                        if c == 0 and m >= 2:
                            pe.wait_ge(h_set.sem, h_set.value(g, 10))
                        if c > 0:
                            pe.wait_ge(expo_set.sem, expo_set.value(g, n - 3))
                        for i in range(4):
                            r = (m % 2) * 4 + i
                            last = pe.matmul(bank[EXPO_BANK[m]][:, i * P:(i + 1) * P],
                                             tab[:, 3, c + CTX_CHUNKS, m // 2, r:r + 1].to_broadcast([P, P]),
                                             ident[:], start=True, stop=True)
                        last.then_inc(cum_ready.sem, 1)

                exponents(0)
                pe.wait_ge(xdt_set.sem, xdt_set.value(g, LC))
                for c in range(LC):
                    if c < LC - 1:
                        exponents(c + 1)
                    if c >= 2:
                        pe.wait_ge(y_skip.sem, y_skip.value(g, c - 1))
                    pe.wait_ge(dec_set.sem, dec_set.value(g, 4 * c + 4))
                    pe.wait_ge(cgrow_set.sem, cgrow_set.value(g, 4 * c + 4))
                    for r in range(HPG):
                        out = bank[2 + c % 2][(r % 2) * SSD_P:(r % 2 + 1) * SSD_P, (r // 2) * P:(r // 2 + 1) * P]
                        cols = slice(r * SSD_P, (r + 1) * SSD_P)
                        for d in range(2):
                            j = ORDER[d].index(c + CTX_CHUNKS)
                            m = 2 * d + r // 4
                            pe.matmul(out, x_dt[:, c, d, cols], dec[:, c % 2, m, r % 4, :],
                                      start=(d == 0), stop=False)
                            last = pe.matmul(out, h_state[:, d, j - 1, cols], c_grow[:, c % 2, m, r % 4, :],
                                             start=False, stop=(d == 1))
                    last.then_inc(y_mms.sem, 1)
                pe.wait_ge(squares.sem, squares.value(g, 1))
                for b in range(GB):
                    last = pe.matmul(bank[7][:, :], ones[:], y_sq[:, b, :], start=(b == 0), stop=(b == GB - 1))
                last.then_inc(sums.sem, 1)

        @block.scalar
        def _(act):
            act.preload_act_table_set(EXP_LN)
            act.wait_ge(consts_set.sem, 1)
            with act.Fori(0, SSD_G) as g:
                act.wait_ge(group_done.sem, group_done.value(g, 0))
                for r in range(CHUNKS + 2):
                    act.wait_ge(turned.sem, turned.value(g, r + 1))
                    if r < CHUNKS:
                        ins = act.activation(x_tok[:, r, :], bank[r % 4][:, :], ACT.Copy)
                    else:
                        lo = 4 * (r - CHUNKS)
                        n = min(4, CHUNKS - lo)
                        ins = act.activation(b_tok[:, lo:lo + n, :].rearrange("p c q -> p (c q)"),
                                             bank[r % 4][:, 0:n * P], ACT.Copy)
                    ins.then_inc(copied.sem, 1)
                act.wait_ge(cb_ready.sem, cb_ready.value(g, 1))
                act.activation(cb[:].rearrange("p c q -> p (c q)"), bank[4][:, :], ACT.Copy).then_inc(cb_set.sem, 1)
                act.wait_ge(staged.sem, staged.value(g, 2))

                def growth(n):
                    act.wait_ge(cum_ready.sem, cum_ready.value(g, n + 1))
                    if n >= 2:
                        act.wait_ge(cgrow_set.sem, cgrow_set.value(g, n - 1))
                    act.activation(grow[:, n % 2].rearrange("p i q -> p (i q)"), bank[EXPO_BANK[n % 4]][:, :],
                                   ACT.Exp).then_inc(grow_set.sem, 1)

                growth(0)
                for n in range(NB):
                    c, m = n // 4, n % 4
                    if n < NB - 1:
                        growth(n + 1)
                    act.wait_ge(expo_set.sem, expo_set.value(g, n + 1))
                    if c >= 2 and m == 0:
                        act.wait_ge(y_mms.sem, y_mms.value(g, c - 1))
                    for i in range(4):
                        r = (m % 2) * 4 + i
                        ins = act.activation(dec[:, c % 2, m, i, :], expo[:, n % 2, i, :], ACT.Exp,
                                             bias=ncum[:, c + CTX_CHUNKS, m // 2, r:r + 1])
                    ins.then_inc(dec_exp.sem, 1)
                act.wait_ge(y_gated.sem, y_gated.value(g, LC))
                act.activation(y_sq[:], y_g[:], ACT.Square).then_inc(squares.sem, 1)
                act.wait_ge(sums.sem, sums.value(g, 1))
                act.activation(inv[:], bank[7][:, :], ACT.Ln, scale=1.0 / GW, bias=eps[:, 0:1]).then_inc(inv_ln.sem, 1)
                act.wait_ge(inv_ln.sem, inv_ln.value(g, 1))
                act.activation(inv[:], inv[:], ACT.Exp, scale=-0.5).then_inc(inv_set.sem, 1)

        @block.gpsimd
        def _(pool):
            with pool.Fori(0, SSD_G) as g:
                pool.wait_ge(group_done.sem, group_done.value(g, 0))
                pool.wait_ge(staged.sem, staged.value(g, 1))
                for j in range(CHUNKS - 1):
                    for d in range(2):
                        c = ORDER[d][j]
                        pool.wait_ge(copied.sem, copied.value(g, c + 1))
                        if j > 0:
                            pool.wait_ge(add_ready.sem, add_ready.value(g, 2 * j + d - 1))
                        pool.tensor_tensor(x_w[:, d, :].rearrange("p (r f) -> p r f", r=HPG),
                                           x_tok[:, c, :].rearrange("p (r f) -> p r f", r=HPG),
                                           tab[:, 1, c, d, :].unsqueeze(2).to_broadcast([P, HPG, SSD_P]),
                                           ALU.mult).then_inc(xw_set.sem, 1)
                for c in range(LC):
                    for d in range(2):
                        ins = pool.tensor_tensor(x_dt[:, c, d, :].rearrange("p (r f) -> p r f", r=HPG),
                                                 x_tok[:, c + CTX_CHUNKS, :].rearrange("p (r f) -> p r f", r=HPG),
                                                 tab[:, 0, c + CTX_CHUNKS, d, :].unsqueeze(2)
                                                 .to_broadcast([P, HPG, SSD_P]), ALU.mult)
                    ins.then_inc(xdt_set.sem, 1)
                for n in range(NB):
                    c, m = n // 4, n % 4
                    pool.wait_ge(grow_set.sem, grow_set.value(g, n + 1))
                    if c >= 2 and m == 0:
                        pool.wait_ge(y_mms.sem, y_mms.value(g, c - 1))
                    pool.tensor_tensor(c_grow[:, c % 2, m, :, :], grow[:, n % 2, :, :],
                                       c_in[:, (c + CTX_CHUNKS) * P:(c + CTX_CHUNKS + 1) * P].unsqueeze(1)
                                       .to_broadcast([P, 4, P]), ALU.mult).then_inc(cgrow_set.sem, 1)

        @block.vector
        def _(dve):
            dve.memset(eps[:], EPS).then_inc(consts_set.sem, 1)
            dve.sem_inc(group_done.sem, GB)
            dve.sem_inc(stored.sem, 16)
            with dve.Fori(0, SSD_G) as g:
                dve.wait_ge(group_done.sem, group_done.value(g, 0))
                heads = bass.ds(g * HPG, HPG)
                dve.tensor_copy(tab[:].rearrange("p t c d r -> p (t c d) r"),
                                tabs[:].rearrange("p t c d r -> p (t c d) r")[:, :, heads]).then_inc(staged.sem, 1)
                dve.wait_ge(staged.sem, staged.value(g, 1))
                dve.tensor_scalar(ncum[:], tab[:, 3, :, :, :], -1.0, None, ALU.mult).then_inc(staged.sem, 1)
                dve.tensor_copy(sk[:], skip[:, bass.ds(g * GB, GB)]).then_inc(staged.sem, 1)
                dve.tensor_copy(nw[:], norm_w[:, bass.ds(g * GB, GB)]).then_inc(staged.sem, 1)
                n_decayed = 0
                for j in range(CHUNKS - 1):
                    for d in range(2):
                        c = ORDER[d][j]
                        if j > 0:
                            dve.wait_ge(h_set.sem, h_set.value(g, 2 * j + d - 1))
                            n_decayed += 1
                            dve.tensor_tensor(h_state[:, d, j, :].rearrange("p (r f) -> p r f", r=HPG),
                                              h_state[:, d, j - 1, :].rearrange("p (r f) -> p r f", r=HPG),
                                              tab[:, 2, c, d, :].unsqueeze(2).to_broadcast([P, HPG, SSD_P]),
                                              ALU.mult).then_inc(h_decayed.sem, 1)
                            dve.wait_ge(h_decayed.sem, h_decayed.value(g, n_decayed))
                        dve.wait_ge(add_ready.sem, add_ready.value(g, 2 * j + d + 1))
                        if j == 0:
                            dve.tensor_copy(h_state[:, d, j, :], bank[5 + d][:, :]).then_inc(h_set.sem, 1)
                        else:
                            dve.tensor_tensor(h_state[:, d, j, :], h_state[:, d, j, :], bank[5 + d][:, :],
                                              ALU.add).then_inc(h_set.sem, 1)
                dve.wait_ge(cb_set.sem, cb_set.value(g, 1))
                dve.wait_ge(stored.sem, stored.value(g, 0))

                def masked(n):
                    d = (n % 4) // 2
                    dve.wait_ge(grow_set.sem, grow_set.value(g, n + 1))
                    if n >= 2:
                        dve.wait_ge(dec_exp.sem, dec_exp.value(g, n - 1))
                    dve.tensor_tensor(expo[:, n % 2, :, :], bank[EXPO_BANK[n % 4]][:, :].rearrange("p (i q) -> p i q", i=4),
                                      neg[:, d, :].unsqueeze(1).to_broadcast([P, 4, P]), ALU.add).then_inc(expo_set.sem, 1)

                masked(0)
                for c in range(LC):
                    for m in range(4):
                        n = 4 * c + m
                        if n < NB - 1:
                            masked(n + 1)
                        dve.wait_ge(dec_exp.sem, dec_exp.value(g, n + 1))
                        dve.tensor_tensor(dec[:, c % 2, m, :, :], dec[:, c % 2, m, :, :],
                                          cb[:, c, :].unsqueeze(1).to_broadcast([P, 4, P]), ALU.mult).then_inc(dec_set.sem, 1)
                    cols = slice(c * P, (c + 1) * P)
                    dve.wait_ge(y_mms.sem, y_mms.value(g, c + 1))
                    for b in range(GB):
                        ins = dve.scalar_tensor_tensor(y_g[:, b, cols], x_in[:, b, CTX + c * P:CTX + (c + 1) * P],
                                                       sk[:, b:b + 1], bank[2 + c % 2][:, b * P:(b + 1) * P],
                                                       ALU.mult, ALU.add)
                    ins.then_inc(y_skip.sem, 1)
                    dve.wait_ge(y_skip.sem, y_skip.value(g, c + 1))
                    dve.tensor_tensor(y_g[:, :, cols], y_g[:, :, cols], z_in[:, :, cols], ALU.mult).then_inc(y_gated.sem, 1)
                dve.wait_ge(inv_set.sem, inv_set.value(g, 1))
                for b in range(GB):
                    dve.scalar_tensor_tensor(y_g[:, b, :], y_g[:, b, :], nw[:, b:b + 1], inv[:],
                                             ALU.mult, ALU.mult).then_inc(group_done.sem, 1)


HG_H = 8
HG_CH = LAT // P
F_FLOOR = float(2.0 ** -63)


@stage
def hgrn_stage(nc, consts, qT, sigT, sig_negT, v_tok_dram, lower, norm_w, zT, yT):
    ident, ones, scan_masks, start = consts["ident"], consts["ones"], consts["scan"], consts["start"]
    with ExitStack() as ctx:
        def sb(name, *shape):
            return ctx.enter_context(nc.sbuf_tensor("hg_" + name, [P, *shape], F32))

        def sig(name, per=1, base=0):
            return Sig(nc.alloc_semaphore("hg_" + name), per, base)

        q_in, s_in, n_in, z_in = sb("q_in", LAT), sb("s_in", LAT), sb("n_in", LAT), sb("z_in", LAT)
        v_tok = sb("v_tok", HG_CH, P)
        lb, rest, nw = sb("lb", 1), sb("rest", 1), sb("nw", 1)
        q, f, k, cum = sb("q", LAT), sb("f", LAT), sb("k", LAT), sb("cum", LAT)
        diff, q_arg, k_arg = sb("diff", 2, LAT), sb("q_arg", 2, LAT), sb("k_arg", 2, LAT)
        q_lev, k_lev = sb("q_lev", 2, LAT), sb("k_lev", 2, LAT)
        part, attn = sb("part", 2, HG_CH, P), sb("attn", HG_CH, P)
        q_grow, k_end, k_end_tok = sb("q_grow", LAT), sb("k_end", LAT), sb("k_end_tok", HG_CH, P)
        to_end, decay_end = sb("to_end", LAT), sb("decay_end", HG_CH)
        state = sb("state", HG_CH - 1, P)
        o, o_sq, y_out = sb("o", LAT), sb("o_sq", LAT), sb("y_out", LAT)
        eps = sb("eps", 1)
        bank = [ctx.enter_context(nc.psum_tensor(f"hg_bank{i}", [P, 512], F32)) for i in range(7)]

        loaded = sig("loaded", 80)
        stored = sig("stored", 16, 16)
        head_done = sig("head_done", 1, 1)
        consts_set = sig("consts_set")
        staged = sig("staged", 3)
        f_set, f_ln, cum_set, k_set, q_set = sig("f_set", 2), sig("f_ln"), sig("cum_set"), sig("k_set"), sig("q_set")
        diff_set, args_set = sig("diff_set", LEVELS), sig("args_set", LEVELS)
        exp_set = sig("exp_set", 2 * LEVELS)
        q_lev_set, k_lev_set = sig("q_lev_set", LEVELS), sig("k_lev_set", LEVELS)
        scores, part_set, attn_set = sig("scores", LEVELS + 1), sig("part_set", LEVELS + 1), sig("attn_set", LEVELS)
        grow_exp, grow_set = sig("grow_exp"), sig("grow_set")
        end_arg, end_exp, end_set = sig("end_arg"), sig("end_exp"), sig("end_set")
        dec_exp = sig("dec_exp")
        turned, turned_copied = sig("turned"), sig("turned_copied")
        add_ready, state_set = sig("add_ready", 3), sig("state_set", 3)
        o_ready, o_set, o_squared = sig("o_ready"), sig("o_set"), sig("o_squared")
        sums, inv_ln, inv_set, o_normed = sig("sums"), sig("inv_ln"), sig("inv_set"), sig("o_normed")

        block = ctx.enter_context(nc.Block())

        @block.sync
        def _(sp):
            with sp.Fori(0, HG_H) as h:
                sp.wait_ge(head_done.sem, head_done.value(h, 0))
                for src, dst in ((sigT, s_in), (sig_negT, n_in), (qT, q_in), (zT, z_in)):
                    sp.dma_start(dst[:], src[h]).then_inc(loaded.sem, 16)
                sp.dma_start(v_tok[:], v_tok_dram.rearrange("(c p) f -> p c f", p=P)[:, :, bass.ts(h, P)]
                             ).then_inc(loaded.sem, 16)
                sp.wait_ge(head_done.sem, head_done.value(h, 1))
                sp.dma_start(yT[h], y_out[:]).then_inc(stored.sem, 16)
            sp.wait_ge(stored.sem, stored.value(HG_H, 0))

        @block.tensor
        def _(pe):
            with pe.Fori(0, HG_H) as h:
                pe.wait_ge(head_done.sem, head_done.value(h, 0))
                pe.wait_ge(k_set.sem, k_set.value(h, 1))
                for n in range(LEVELS + 1):
                    lev = (n - 1) % (LEVELS + 1)
                    if n >= 2:
                        pe.wait_ge(part_set.sem, part_set.value(h, n - 1))
                    if n >= 1:
                        pe.wait_ge(q_lev_set.sem, q_lev_set.value(h, n))
                        pe.wait_ge(k_lev_set.sem, k_lev_set.value(h, n))
                    else:
                        pe.wait_ge(loaded.sem, loaded.value(h, 80))
                    for c in range(HG_CH):
                        cols = slice(c * P, (c + 1) * P)
                        ks = k[:, cols] if n == 0 else k_lev[:, lev % 2, cols]
                        qs = q_in[:, cols] if n == 0 else q_lev[:, lev % 2, cols]
                        last = pe.matmul(bank[n % 2][:, cols], ks, qs, start=True, stop=True)
                    last.then_inc(scores.sem, 1)
                    if n == 1:
                        pe.wait_ge(end_set.sem, end_set.value(h, 1))
                        for c in range(HG_CH - 1):
                            last = pe.transpose(bank[3][:, c * P:(c + 1) * P], k_end[:, c * P:(c + 1) * P], ident[:])
                        last.then_inc(turned.sem, 1)
                    if n == 3:
                        pe.wait_ge(turned_copied.sem, turned_copied.value(h, 1))
                        for c in range(HG_CH - 1):
                            last = pe.matmul(bank[4][:, c * P:(c + 1) * P], k_end_tok[:, c, :], v_tok[:, c, :],
                                             start=True, stop=True)
                        last.then_inc(add_ready.sem, 3)
                pe.wait_ge(grow_set.sem, grow_set.value(h, 1))
                pe.wait_ge(state_set.sem, state_set.value(h, 3))
                pe.wait_ge(attn_set.sem, attn_set.value(h, LEVELS))
                for c in range(HG_CH):
                    cols = slice(c * P, (c + 1) * P)
                    if c > 0:
                        pe.matmul(bank[2][:, cols], state[:, c - 1, :], q_grow[:, cols], start=True, stop=False)
                    last = pe.matmul(bank[2][:, cols], v_tok[:, c, :], attn[:, c, :], start=(c == 0), stop=True)
                last.then_inc(o_ready.sem, 1)
                pe.wait_ge(o_squared.sem, o_squared.value(h, 1))
                pe.matmul(bank[6][:, :], ones[:], o_sq[:], start=True, stop=True).then_inc(sums.sem, 1)

        @block.scalar
        def _(act):
            act.preload_act_table_set(EXP_LN)
            act.wait_ge(consts_set.sem, 1)
            with act.Fori(0, HG_H) as h:
                act.wait_ge(head_done.sem, head_done.value(h, 0))
                act.wait_ge(f_set.sem, f_set.value(h, 2))
                act.activation(f[:], f[:], ACT.Ln).then_inc(f_ln.sem, 1)
                act.wait_ge(end_arg.sem, end_arg.value(h, 1))
                act.activation(to_end[:], to_end[:], ACT.Exp).then_inc(end_exp.sem, 1)
                act.activation(decay_end[:], cum[:].rearrange("p (c t) -> p c t", c=HG_CH)[:, :, P - 1],
                               ACT.Exp).then_inc(dec_exp.sem, 1)
                for lev in range(LEVELS):
                    act.wait_ge(args_set.sem, args_set.value(h, lev + 1))
                    act.activation(q_arg[:, lev % 2, :], q_arg[:, lev % 2, :], ACT.Exp).then_inc(exp_set.sem, 1)
                    act.activation(k_arg[:, lev % 2, :], k_arg[:, lev % 2, :], ACT.Exp, scale=-1.0).then_inc(exp_set.sem, 1)
                    if lev == 0:
                        act.activation(q_grow[:], cum[:], ACT.Exp).then_inc(grow_exp.sem, 1)
                    if lev == 1:
                        act.wait_ge(turned.sem, turned.value(h, 1))
                        act.activation(k_end_tok[:, 0:HG_CH - 1, :].rearrange("p c q -> p (c q)"),
                                       bank[3][:, 0:(HG_CH - 1) * P], ACT.Copy).then_inc(turned_copied.sem, 1)
                act.wait_ge(o_ready.sem, o_ready.value(h, 1))
                act.activation(o[:], bank[2][:, :], ACT.Copy).then_inc(o_set.sem, 1)
                act.activation(o_sq[:], bank[2][:, :], ACT.Square).then_inc(o_squared.sem, 1)
                act.wait_ge(sums.sem, sums.value(h, 1))
                act.activation(o_sq[:], bank[6][:, :], ACT.Ln, scale=1.0 / P, bias=eps[:, 0:1]).then_inc(inv_ln.sem, 1)
                act.wait_ge(inv_ln.sem, inv_ln.value(h, 1))
                act.activation(o_sq[:], o_sq[:], ACT.Exp, scale=-0.5).then_inc(inv_set.sem, 1)

        @block.gpsimd
        def _(pool):
            with pool.Fori(0, HG_H) as h:
                pool.wait_ge(head_done.sem, head_done.value(h, 0))
                pool.wait_ge(k_set.sem, k_set.value(h, 1))
                pool.wait_ge(end_exp.sem, end_exp.value(h, 1))
                pool.tensor_tensor(k_end[:], k[:], to_end[:], ALU.mult).then_inc(end_set.sem, 1)
                for lev in range(LEVELS):
                    pool.wait_ge(exp_set.sem, exp_set.value(h, 2 * lev + 2))
                    if lev >= 2:
                        pool.wait_ge(scores.sem, scores.value(h, lev))
                    pool.tensor_tensor(k_lev[:, lev % 2, :], k[:], k_arg[:, lev % 2, :], ALU.mult).then_inc(k_lev_set.sem, 1)
                    if lev == 0:
                        pool.wait_ge(grow_exp.sem, grow_exp.value(h, 1))
                        pool.tensor_tensor(q_grow[:], q_grow[:], q_in[:], ALU.mult).then_inc(grow_set.sem, 1)
                    pool.wait_ge(part_set.sem, part_set.value(h, lev + 2))
                    if lev > 0:
                        pool.wait_ge(attn_set.sem, attn_set.value(h, lev))
                    first = part[:, 0] if lev == 0 else attn[:]
                    pool.tensor_tensor(attn[:], first, part[:, (lev + 1) % 2], ALU.add).then_inc(attn_set.sem, 1)

        @block.vector
        def _(dve):
            dve.memset(eps[:], EPS).then_inc(consts_set.sem, 1)
            dve.sem_inc(head_done.sem, 1)
            dve.sem_inc(stored.sem, 16)
            with dve.Fori(0, HG_H) as h:
                dve.wait_ge(head_done.sem, head_done.value(h, 0))
                dve.tensor_copy(lb[:], lower[:, bass.ds(h, 1)]).then_inc(staged.sem, 1)
                dve.tensor_copy(nw[:], norm_w[:, bass.ds(h, 1)]).then_inc(staged.sem, 1)
                dve.wait_ge(staged.sem, staged.value(h, 2))
                dve.tensor_scalar(rest[:], lb[:], -1.0, 1.0, ALU.mult, ALU.add).then_inc(staged.sem, 1)
                dve.wait_ge(staged.sem, staged.value(h, 3))
                dve.wait_ge(loaded.sem, loaded.value(h, 80))
                dve.tensor_scalar(f[:], s_in[:], rest[:, 0:1], lb[:, 0:1], ALU.mult, ALU.add).then_inc(f_set.sem, 1)
                dve.wait_ge(f_set.sem, f_set.value(h, 1))
                dve.tensor_scalar(f[:], f[:], F_FLOOR, None, ALU.max).then_inc(f_set.sem, 1)
                dve.tensor_scalar(k[:], n_in[:], rest[:, 0:1], None, ALU.mult).then_inc(k_set.sem, 1)
                dve.wait_ge(f_ln.sem, f_ln.value(h, 1))
                dve.tensor_tensor_scan(cum[:], start[:], f[:], 0.0, ALU.mult, ALU.add).then_inc(cum_set.sem, 1)
                dve.wait_ge(cum_set.sem, cum_set.value(h, 1))
                chunks = cum[:].rearrange("p (c t) -> p c t", c=HG_CH)
                dve.tensor_tensor(to_end[:].rearrange("p (c t) -> p c t", c=HG_CH),
                                  chunks[:, :, P - 1:P].to_broadcast([P, HG_CH, P]), chunks,
                                  ALU.subtract).then_inc(end_arg.sem, 1)

                def exponents(lev):
                    half = 1 << lev
                    blocks = cum[:].rearrange("p (b t) -> p b t", t=2 * half)
                    if lev >= 2:
                        dve.wait_ge(k_lev_set.sem, k_lev_set.value(h, lev - 1))
                        dve.wait_ge(q_lev_set.sem, q_lev_set.value(h, lev - 1))
                    dve.tensor_tensor(diff[:, lev % 2, :].rearrange("p (b t) -> p b t", t=2 * half), blocks,
                                      blocks[:, :, half - 1:half].to_broadcast([P, LAT // (2 * half), 2 * half]),
                                      ALU.subtract).then_inc(diff_set.sem, 1)
                    dve.wait_ge(diff_set.sem, diff_set.value(h, lev + 1))
                    dve.tensor_scalar(q_arg[:, lev % 2, :], diff[:, lev % 2, :], 0.0, None, ALU.min)
                    dve.tensor_scalar(k_arg[:, lev % 2, :], diff[:, lev % 2, :], 0.0, None, ALU.max).then_inc(args_set.sem, 1)

                def masked(n):
                    lev = (n - 1) % (LEVELS + 1)
                    dve.wait_ge(scores.sem, scores.value(h, n + 1))
                    if n >= 2:
                        dve.wait_ge(attn_set.sem, attn_set.value(h, max(1, n - 2)))
                    dve.tensor_tensor(part[:, n % 2], bank[n % 2][:, :].rearrange("p (c t) -> p c t", c=HG_CH),
                                      scan_masks[:, lev, :].unsqueeze(1).to_broadcast([P, HG_CH, P]),
                                      ALU.mult).then_inc(part_set.sem, 1)

                exponents(0)
                masked(0)
                for lev in range(LEVELS):
                    if lev < LEVELS - 1:
                        exponents(lev + 1)
                    dve.wait_ge(exp_set.sem, exp_set.value(h, 2 * lev + 1))
                    if lev >= 2:
                        dve.wait_ge(scores.sem, scores.value(h, lev))
                    dve.tensor_tensor(q_lev[:, lev % 2, :], q_in[:], q_arg[:, lev % 2, :], ALU.mult).then_inc(q_lev_set.sem, 1)
                    masked(lev + 1)
                    if 3 <= lev < 6:
                        c = lev - 3
                        dve.wait_ge(add_ready.sem, add_ready.value(h, 3))
                        if c == 0:
                            dve.wait_ge(dec_exp.sem, dec_exp.value(h, 1))
                            dve.tensor_copy(state[:, 0, :], bank[4][:, 0:P]).then_inc(state_set.sem, 1)
                        else:
                            dve.wait_ge(state_set.sem, state_set.value(h, c))
                            dve.scalar_tensor_tensor(state[:, c, :], state[:, c - 1, :], decay_end[:, c:c + 1],
                                                     bank[4][:, c * P:(c + 1) * P], ALU.mult, ALU.add
                                                     ).then_inc(state_set.sem, 1)
                dve.wait_ge(o_set.sem, o_set.value(h, 1))
                dve.wait_ge(inv_set.sem, inv_set.value(h, 1))
                dve.tensor_tensor(o[:], o[:], o_sq[:], ALU.mult).then_inc(o_normed.sem, 1)
                dve.wait_ge(o_normed.sem, o_normed.value(h, 1))
                dve.wait_ge(stored.sem, stored.value(h, 0))
                dve.scalar_tensor_tensor(y_out[:], o[:], nw[:, 0:1], z_in[:], ALU.mult, ALU.mult).then_inc(head_done.sem, 1)


ML_H = 8
ML_CH = LAT // P
ML_E = 2
ML_TABS = 8


@stage
def mlstm_gates_stage(nc, consts, ig, fg, bias_i, bias_f, tabs):
    ident, start, last_row = consts["ident"], consts["start"], consts["last"]
    LN_SCALE = float(-0.5 * np.log(P))
    with ExitStack() as ctx:
        def sb(name, *shape):
            return ctx.enter_context(nc.sbuf_tensor("mg_" + name, list(shape), F32))

        def sem(name):
            return nc.alloc_semaphore("mg_" + name)

        li, x, e, lf = sb("li", 8, LAT), sb("x", 8, LAT), sb("e", 8, LAT), sb("lf", 8, LAT)
        cum, m = sb("cum", 8, LAT), sb("m", 8, LAT)
        rows = sb("rows", 8, 3, LAT)
        turned = ctx.enter_context(nc.psum_tensor("mg_turned", [P, 3, ML_CH, 8], F32))
        ends = ctx.enter_context(nc.psum_tensor("mg_ends", [P, 3, ML_CH, 8], F32))
        dve_n, act_n = sem("dve_n"), sem("act_n")
        rows_set, turned_set, cols_set, ends_set = sem("rows_set"), sem("turned_set"), sem("cols_set"), sem("ends_set")
        block = ctx.enter_context(nc.Block())

        @block.vector
        def _(dve):
            done = [0]

            def link(ins):
                done[0] += 1
                ins.then_inc(dve_n, 1)
                dve.wait_ge(dve_n, done[0])

            link(dve.tensor_scalar(li[:], ig, bias_i, None, ALU.add))
            link(dve.tensor_scalar(x[:], fg, bias_f, None, ALU.add))
            dve.wait_ge(act_n, 3)
            link(dve.tensor_scalar(x[:], x[:], 0.0, None, ALU.min))
            link(dve.tensor_tensor(lf[:], x[:], e[:], ALU.subtract))
            link(dve.tensor_tensor_scan(cum[:], start[0:8, :], lf[:], 0.0, ALU.mult, ALU.add))
            link(dve.tensor_tensor_scan(m[:], lf[:], li[:], 0.0, ALU.add, ALU.max))
            link(dve.tensor_tensor(rows[:, 0, :], cum[:], m[:], ALU.subtract))
            link(dve.tensor_tensor(rows[:, 1, :], li[:], cum[:], ALU.subtract))
            dve.tensor_copy(rows[:, 2, :], m[:]).then_inc(rows_set, 1)
            dve.wait_ge(turned_set, 1)
            dve.tensor_copy(tabs[:, 0:3, :, :], turned[:]).then_inc(cols_set, 1)
            dve.wait_ge(cols_set, 1)
            dve.wait_ge(ends_set, 1)
            link(dve.memset(tabs[:, 3, 0, :], 0.0))
            link(dve.tensor_copy(tabs[:, 3, 1:ML_CH, :], ends[:, 2, 0:ML_CH - 1, :]))
            link(dve.tensor_tensor(tabs[:, 4, :, :], tabs[:, 1, :, :], ends[:, 0, :, :], ALU.add))
            link(dve.tensor_tensor(tabs[:, 5, :, :], tabs[:, 3, :, :], ends[:, 0, :, :], ALU.add))
            link(dve.tensor_scalar(tabs[:, 6, :, :], tabs[:, 1, :, :], LN_SCALE, None, ALU.add))
            link(dve.tensor_scalar(tabs[:, 7, :, :], tabs[:, 3, :, :], LN_SCALE, None, ALU.add))

        @block.scalar
        def _(act):
            act.preload_act_table_set(EXP_LN)
            act.wait_ge(dve_n, 2)
            act.activation(e[:], x[:], ACT.Abs).then_inc(act_n, 1)
            act.wait_ge(act_n, 1)
            act.activation(e[:], e[:], ACT.Exp, scale=-1.0).then_inc(act_n, 1)
            act.wait_ge(act_n, 2)
            act.activation(e[:], e[:], ACT.Ln, bias=1.0).then_inc(act_n, 1)
            act.wait_ge(dve_n, 14)
            act.activation(tabs[:, 4:6, :, :], tabs[:, 4:6, :, :], ACT.Exp).then_inc(act_n, 1)

        @block.tensor
        def _(pe):
            pe.wait_ge(rows_set, 1)
            for t in range(3):
                for c in range(ML_CH):
                    last = pe.transpose(turned[:, t, c, :], rows[:, t, c * P:(c + 1) * P], ident[0:8, 0:8])
            last.then_inc(turned_set, 1)
            pe.wait_ge(cols_set, 1)
            pe.matmul(ends[:], last_row[:], tabs[:, 0:3, :, :], start=True, stop=True).then_inc(ends_set, 1)


@stage
def mlstm_stage(nc, consts, qkT, v_tok_dram, tabs, norm_w, ogT, zT, yT):
    ident, ones, neg = consts["ident"], consts["ones"], consts["neg"]
    SW = (ML_E + 1) * P
    with ExitStack() as ctx:
        def sb(name, *shape):
            return ctx.enter_context(nc.sbuf_tensor("ml_" + name, [P, *shape], F32))

        def sig(name, per=1, base=0):
            return Sig(nc.alloc_semaphore("ml_" + name), per, base)

        q_in, k_in, v_tok = sb("q_in", LAT), sb("k_in", LAT), sb("v_tok", ML_CH, ML_E * P)
        og_in, z_in, gate = sb("og_in", ML_E, LAT), sb("z_in", ML_E, LAT), sb("gate", ML_E, LAT)
        tab, nw = sb("tab", ML_TABS, ML_CH), sb("nw", ML_E)
        grow, expo, w, floor = sb("grow", ML_CH, P), sb("expo", ML_CH, P), sb("w", ML_CH, P), sb("floor", LAT)
        q_grow, score = sb("q_grow", LAT), sb("score", ML_CH, P)
        k_w, state = sb("k_w", ML_CH, P), sb("state", ML_CH - 1, SW)
        den, o, o_sq, inv, y_out = sb("den", LAT), sb("o", ML_E, LAT), sb("o_sq", ML_E, LAT), sb("inv", LAT), sb("y_out", ML_E, LAT)
        eps = sb("eps", 1)
        bank = [ctx.enter_context(nc.psum_tensor(f"ml_bank{i}", [P, 512], F32)) for i in range(8)]

        loaded = sig("loaded", 80)
        stored, head_done = sig("stored", 16, 16), sig("head_done", 1, 1)
        consts_set = sig("consts_set")
        staged = sig("staged", 2)
        cum_ready, m_ready, kq_ready, k_turned = sig("cum_ready"), sig("m_ready"), sig("kq_ready"), sig("k_turned")
        grow_set, floor_set, expo_set, w_set = sig("grow_set"), sig("floor_set"), sig("expo_set"), sig("w_set")
        q_grown, gate_set = sig("q_grown"), sig("gate_set")
        score_set, k_w_set = sig("score_set"), sig("k_w_set")
        add_ready, state_set = sig("add_ready", 3), sig("state_set", 3)
        num_ready, den_ready = sig("num_ready", ML_E), sig("den_ready")
        den_abs, den_max, den_inv = sig("den_abs"), sig("den_max"), sig("den_inv")
        o_set, o_squared, sums = sig("o_set", ML_E), sig("o_squared"), sig("sums")
        inv_ln, inv_set, y_normed = sig("inv_ln"), sig("inv_set"), sig("y_normed")

        block = ctx.enter_context(nc.Block())

        @block.sync
        def _(sp):
            with sp.Fori(0, ML_H) as h:
                sp.wait_ge(head_done.sem, head_done.value(h, 0))
                sp.dma_start(k_in[:], qkT[h + ML_H]).then_inc(loaded.sem, 16)
                sp.dma_start(q_in[:], qkT[h]).then_inc(loaded.sem, 16)
                sp.dma_start(v_tok[:], v_tok_dram.rearrange("(c p) f -> p c f", p=P)[:, :, bass.ts(h, ML_E * P)]
                             ).then_inc(loaded.sem, 16)
                pair_of = bass.ds(h * ML_E, ML_E)
                sp.dma_start(og_in[:], ogT[pair_of].rearrange("b p t -> p b t")).then_inc(loaded.sem, 16)
                sp.dma_start(z_in[:], zT[pair_of].rearrange("b p t -> p b t")).then_inc(loaded.sem, 16)
                sp.wait_ge(head_done.sem, head_done.value(h, 1))
                sp.dma_start(yT[pair_of].rearrange("b p t -> p b t"), y_out[:]).then_inc(stored.sem, 16)
            sp.wait_ge(stored.sem, stored.value(ML_H, 0))

        @block.tensor
        def _(pe):
            with pe.Fori(0, ML_H) as h:
                pe.wait_ge(head_done.sem, head_done.value(h, 0))
                pe.wait_ge(staged.sem, staged.value(h, 2))
                for i, t, ready in ((0, 0, cum_ready), (1, 2, m_ready)):
                    for c in range(ML_CH):
                        last = pe.matmul(bank[i][:, c * P:(c + 1) * P], tab[:, t, c:c + 1].to_broadcast([P, P]),
                                         ident[:], start=True, stop=True)
                    last.then_inc(ready.sem, 1)
                pe.wait_ge(loaded.sem, loaded.value(h, 80))
                for c in range(ML_CH):
                    last = pe.transpose(bank[3][:, c * P:(c + 1) * P], k_in[:, c * P:(c + 1) * P], ident[:])
                last.then_inc(k_turned.sem, 1)
                for c in range(ML_CH):
                    cols = slice(c * P, (c + 1) * P)
                    last = pe.matmul(bank[2][:, cols], k_in[:, cols], q_in[:, cols], start=True, stop=True)
                last.then_inc(kq_ready.sem, 1)
                pe.wait_ge(k_w_set.sem, k_w_set.value(h, 1))
                for c in range(ML_CH - 1):
                    pe.matmul(bank[4 + c][:, 0:ML_E * P], k_w[:, c, :], v_tok[:, c, :], start=True, stop=True)
                    pe.matmul(bank[4 + c][:, ML_E * P:SW], k_w[:, c, :], ones[:], start=True, stop=True
                              ).then_inc(add_ready.sem, 1)
                pe.wait_ge(score_set.sem, score_set.value(h, 1))
                pe.wait_ge(q_grown.sem, q_grown.value(h, 1))
                pe.wait_ge(state_set.sem, state_set.value(h, 3))
                pe.wait_ge(expo_set.sem, expo_set.value(h, 1))
                pe.wait_ge(floor_set.sem, floor_set.value(h, 1))
                for i, e, ready in ((0, ML_E, den_ready), (7, 0, num_ready), (1, 1, num_ready)):
                    for c in range(ML_CH):
                        cols = slice(c * P, (c + 1) * P)
                        if c > 0:
                            pe.matmul(bank[i][:, cols], state[:, c - 1, e * P:(e + 1) * P], q_grow[:, cols],
                                      start=True, stop=False)
                        values = ones[:] if e == ML_E else v_tok[:, c, e * P:(e + 1) * P]
                        last = pe.matmul(bank[i][:, cols], values, score[:, c, :], start=(c == 0), stop=True)
                    last.then_inc(ready.sem, 1)
                pe.wait_ge(o_squared.sem, o_squared.value(h, 1))
                for e in range(ML_E):
                    last = pe.matmul(bank[2][:, :], ones[:], o_sq[:, e, :], start=(e == 0), stop=(e == ML_E - 1))
                last.then_inc(sums.sem, 1)

        @block.scalar
        def _(act):
            act.preload_act_table_set(EXP_LN)
            act.wait_ge(consts_set.sem, 1)
            with act.Fori(0, ML_H) as h:
                act.wait_ge(head_done.sem, head_done.value(h, 0))
                act.wait_ge(cum_ready.sem, cum_ready.value(h, 1))
                for c in range(ML_CH):
                    ins = act.activation(grow[:, c, :], bank[0][:, c * P:(c + 1) * P], ACT.Exp, bias=tab[:, 7, c:c + 1])
                ins.then_inc(grow_set.sem, 1)
                act.wait_ge(m_ready.sem, m_ready.value(h, 1))
                act.activation(floor[:], bank[1][:, :], ACT.Exp, scale=-1.0).then_inc(floor_set.sem, 1)
                act.wait_ge(expo_set.sem, expo_set.value(h, 1))
                for c in range(ML_CH):
                    ins = act.activation(w[:, c, :], expo[:, c, :], ACT.Exp, bias=tab[:, 6, c:c + 1])
                ins.then_inc(w_set.sem, 1)
                act.wait_ge(den_ready.sem, den_ready.value(h, 1))
                act.activation(den[:], bank[0][:, :], ACT.Abs).then_inc(den_abs.sem, 1)
                act.wait_ge(o_set.sem, o_set.value(h, ML_E))
                act.activation(o_sq[:], o[:], ACT.Square).then_inc(o_squared.sem, 1)
                act.wait_ge(sums.sem, sums.value(h, 1))
                act.activation(inv[:], bank[2][:, :], ACT.Ln, scale=1.0 / (ML_E * P), bias=eps[:, 0:1]).then_inc(inv_ln.sem, 1)
                act.wait_ge(inv_ln.sem, inv_ln.value(h, 1))
                act.activation(inv[:], inv[:], ACT.Exp, scale=-0.5).then_inc(inv_set.sem, 1)

        @block.gpsimd
        def _(pool):
            with pool.Fori(0, ML_H) as h:
                pool.wait_ge(loaded.sem, loaded.value(h, 80))
                pool.wait_ge(grow_set.sem, grow_set.value(h, 1))
                pool.tensor_tensor(q_grow[:], q_in[:], grow[:].rearrange("p c t -> p (c t)"), ALU.mult).then_inc(q_grown.sem, 1)
                pool.tensor_tensor(gate[:], og_in[:], z_in[:], ALU.mult).then_inc(gate_set.sem, 1)

        @block.vector
        def _(dve):
            dve.memset(eps[:], EPS).then_inc(consts_set.sem, 1)
            dve.sem_inc(head_done.sem, 1)
            dve.sem_inc(stored.sem, 16)
            with dve.Fori(0, ML_H) as h:
                dve.wait_ge(head_done.sem, head_done.value(h, 0))
                dve.tensor_copy(tab[:].rearrange("p t c -> p (t c)"),
                                tabs[:].rearrange("p t c h -> p (t c) h")[:, :, bass.ds(h, 1)]
                                .rearrange("p x h -> p (x h)")).then_inc(staged.sem, 1)
                dve.tensor_copy(nw[:], norm_w[:, bass.ds(h * ML_E, ML_E)]).then_inc(staged.sem, 1)
                dve.wait_ge(staged.sem, staged.value(h, 2))
                dve.wait_ge(grow_set.sem, grow_set.value(h, 1))
                dve.tensor_tensor(expo[:], bank[0][:, :].rearrange("p (c t) -> p c t", c=ML_CH),
                                  neg[:, 0, :].unsqueeze(1).to_broadcast([P, ML_CH, P]), ALU.add).then_inc(expo_set.sem, 1)
                dve.wait_ge(k_turned.sem, k_turned.value(h, 1))
                dve.tensor_tensor(k_w[:], bank[3][:, :].rearrange("p (c t) -> p c t", c=ML_CH),
                                  tab[:, 4, :].unsqueeze(2).to_broadcast([P, ML_CH, P]), ALU.mult).then_inc(k_w_set.sem, 1)
                dve.wait_ge(kq_ready.sem, kq_ready.value(h, 1))
                dve.wait_ge(w_set.sem, w_set.value(h, 1))
                dve.tensor_tensor(score[:], bank[2][:, :].rearrange("p (c t) -> p c t", c=ML_CH), w[:],
                                  ALU.mult).then_inc(score_set.sem, 1)
                for c in range(ML_CH - 1):
                    dve.wait_ge(add_ready.sem, add_ready.value(h, c + 1))
                    if c == 0:
                        ins = dve.tensor_copy(state[:, 0, :], bank[4][:, 0:SW])
                    else:
                        dve.wait_ge(state_set.sem, state_set.value(h, c))
                        ins = dve.scalar_tensor_tensor(state[:, c, :], state[:, c - 1, :], tab[:, 5, c:c + 1],
                                                       bank[4 + c][:, 0:SW], ALU.mult, ALU.add)
                    ins.then_inc(state_set.sem, 1)
                dve.wait_ge(den_abs.sem, den_abs.value(h, 1))
                dve.tensor_tensor(den[:], den[:], floor[:], ALU.max).then_inc(den_max.sem, 1)
                dve.wait_ge(den_max.sem, den_max.value(h, 1))
                dve.reciprocal(den[:], den[:]).then_inc(den_inv.sem, 1)
                dve.wait_ge(den_inv.sem, den_inv.value(h, 1))
                for e, i in ((0, 7), (1, 1)):
                    dve.wait_ge(num_ready.sem, num_ready.value(h, e + 1))
                    dve.tensor_tensor(o[:, e, :], bank[i][:, :], den[:], ALU.mult).then_inc(o_set.sem, 1)
                dve.wait_ge(inv_set.sem, inv_set.value(h, 1))
                dve.wait_ge(stored.sem, stored.value(h, 0))
                for e in range(ML_E):
                    ins = dve.scalar_tensor_tensor(y_out[:, e, :], o[:, e, :], nw[:, e:e + 1], inv[:], ALU.mult, ALU.mult)
                ins.then_inc(y_normed.sem, 1)
                dve.wait_ge(y_normed.sem, y_normed.value(h, 1))
                dve.wait_ge(gate_set.sem, gate_set.value(h, 1))
                dve.tensor_tensor(y_out[:], y_out[:], gate[:], ALU.mult).then_inc(head_done.sem, 1)


ROWS = [
    [("b_ada", 48), ("pre_norm_w", 16), ("post_norm_w", 16), ("conv_ssd_b", 12), ("ssd_norm_w", 8), ("gdn_norm_w", 1)],
    [("conv_ssd_w", 60), ("c_conv_w_2", 64)],
    [("conv_gdn_w", 120)],
    [("e_norm_2", 16), ("o_norm_2", 16), ("final_norm_2", 16), ("ple_norm_2", 32), ("a_norm_2", 8), ("c_norm_2", 16),
     ("b_conv_b_2", 8), ("b_b_r_2", 8), ("b_b_i_2", 8)],
    [("b_conv_w_2", 32), ("b_lambda_2", 8), ("a_lb_logits_2", 16), ("c_conv_b_2", 16)],
]
CONSTS = {"ident": (P,), "ones": (P,), "causal": (2, P), "neg": (2, P), "pair": (LEVELS, 2, P),
          "scan": (LEVELS + 1, P), "start": (LAT,), "last": (P,)}
Z_BLOCKS = D // P
XBC_BLOCKS, QKV_BLOCKS = 12, 24
OFF_XBC, OFF_DT = D, D + XBC_BLOCKS * P
OFF_QKV = OFF_DT + 2 * SSD_H
OFF_BETA = OFF_QKV + QKV_BLOCKS * P
GATES = 2 * SSD_H + 4 * GDN_H


def flat(ap):
    names = "abcdef"[:len(ap.shape) - 1]
    return ap if len(names) == 1 else ap.rearrange(f"p {' '.join(names)} -> p ({' '.join(names)})")


def columns(cols, name, lo=0, n=None):
    for t, tile in enumerate(ROWS):
        at = 0
        for key, rows in tile:
            if key == name:
                return cols[:, t, at + lo:at + (rows if n is None else lo + n)]
            at += rows
    raise KeyError(name)


@stage
def setup_stage(nc, a, consts, cols, x_all, h_dram):
    TILES = TOK // P
    with ExitStack() as ctx:
        def sem(name):
            return nc.alloc_semaphore("set_" + name)

        rows = ctx.enter_context(nc.sbuf_tensor("set_rows", [P, len(ROWS), P], F32))
        tok = ctx.enter_context(nc.sbuf_tensor("set_tok", [P, 2, D], F32))
        turned_p = [ctx.enter_context(nc.psum_tensor(f"set_turned{i}", [P, 4, P], F32)) for i in range(4)]
        cols_p = [ctx.enter_context(nc.psum_tensor(f"set_cols{i}", [P, P], F32)) for i in range(2)]
        ident_in, others_in, rows_in, tok_in = sem("ident_in"), sem("others_in"), sem("rows_in"), [sem("tok_in0"), sem("tok_in1")]
        cleared = sem("cleared")
        turned, copied = sem("turned"), sem("copied")
        cols_ready, cols_set = sem("cols_ready"), sem("cols_set")
        h_stored = sem("h_stored")
        n_rows = sum(len(t) for t in ROWS)
        block = ctx.enter_context(nc.Block())

        def tokens(i):
            return a["ctx"][0, i * P:(i + 1) * P, :] if i < CTX_CHUNKS else \
                a["x"][0, (i - CTX_CHUNKS) * P:(i - CTX_CHUNKS + 1) * P, :]

        @block.sync
        def _(sp):
            sp.dma_start(consts["ident"][:], a["c_ident"]).then_inc(ident_in, 16)
            for i in range(TILES):
                if i >= 2:
                    sp.wait_ge(copied, 4 * (i - 1))
                sp.dma_start(tok[:, i % 2, :], tokens(i)).then_inc(tok_in[i % 2], 16)

        @block.tensor
        def _(pe):
            pe.wait_ge(ident_in, 16)
            for i in range(TILES):
                pe.wait_ge(tok_in[i % 2], 16 * (i // 2 + 1))
                for g in range(4):
                    n = 4 * i + g
                    if n >= 4:
                        pe.wait_ge(copied, n - 3)
                    for k in range(4):
                        f = 4 * g + k
                        last = pe.transpose(turned_p[n % 4][:, k, :], tok[:, i % 2, f * P:(f + 1) * P], consts["ident"][:])
                    last.then_inc(turned, 1)
            pe.wait_ge(rows_in, 16 * n_rows)
            for t in range(len(ROWS)):
                if t >= 2:
                    pe.wait_ge(cols_set, t - 1)
                pe.transpose(cols_p[t % 2][:], rows[:, t, :], consts["ident"][:]).then_inc(cols_ready, 1)

        @block.vector
        def _(dve):
            dve.memset(rows[:], 0.0).then_inc(cleared, 1)
            for n in range(4 * TILES):
                i, g = n // 4, n % 4
                dve.wait_ge(turned, n + 1)
                dve.tensor_copy(x_all[:, 4 * g:4 * g + 4, i * P:(i + 1) * P], turned_p[n % 4][:]).then_inc(copied, 1)
            for t in range(len(ROWS)):
                dve.wait_ge(cols_ready, t + 1)
                dve.tensor_copy(cols[:, t, :], cols_p[t % 2][:]).then_inc(cols_set, 1)

        @block.scalar
        def _(act):
            act.wait_ge(cleared, 1)
            for t, tile in enumerate(ROWS):
                at = 0
                for key, n in tile:
                    src = a[key]
                    names = "abcdef"[:len(src.shape)]
                    src = src if len(names) == 1 else src.rearrange(f"{' '.join(names)} -> ({' '.join(names)})")
                    act.dma_start(rows[at:at + n, t, :], src.rearrange("(r f) -> r f", f=P)).then_inc(rows_in, 16)
                    at += n
            for key in CONSTS:
                if key != "ident":
                    act.dma_start(flat(consts[key][:]), a["c_" + key]).then_inc(others_in, 16)
            for g in range(4):
                act.wait_ge(copied, 4 * TILES - 3 + g)
                act.dma_start(h_dram[4 * g:4 * g + 4].rearrange("k p t -> p k t"),
                              x_all[:, 4 * g:4 * g + 4, CTX:TOK]).then_inc(h_stored, 16)
            act.wait_ge(others_in, 16 * (len(CONSTS) - 1))
            act.wait_ge(h_stored, 64)


@stage
def modulation_stage(nc, a, cols, mod, vec):
    MB = 3 * KD
    GROUP = 2
    with ExitStack() as ctx:
        def sb(name, *shape):
            return ctx.enter_context(nc.sbuf_tensor("mod_" + name, [P, *shape], F32))

        def sem(name):
            return nc.alloc_semaphore("mod_" + name)

        c_in, c_act = sb("c_in", 2, KD), sb("c_act", KD, 2)
        w = [sb(f"w{i}", KD, GROUP * P) for i in range(2)]
        t0, t1, t2 = sb("t0", 8), sb("t1", 8), sb("t2", 8)
        acc = [ctx.enter_context(nc.psum_tensor(f"mod_acc{i}", [P, GROUP, 2], F32)) for i in range(2)]
        c_loaded, c_set, w_in = sem("c_loaded"), sem("c_set"), [sem("w_in0"), sem("w_in1")]
        group_ready, group_used = sem("group_ready"), sem("group_used")
        dve_n, act_n = sem("dve_n"), sem("act_n")
        HALF = MB // GROUP // 2
        ready, used = Sig(group_ready, 2), Sig(group_used, 2, 2)
        loads = [Sig(s, 16) for s in w_in]
        w_v = a["w_ada"].rearrange("l (p k) n -> (l p) k n", k=KD)
        block = ctx.enter_context(nc.Block())

        @block.sync
        def _(sp):
            sp.dma_start(c_in[:, 0, :], a["c"].rearrange("b (p k) -> (b p) k", k=KD)).then_inc(c_loaded, 16)
            sp.dma_start(c_in[:, 1, :], a["c_ctx"].rearrange("(p k) -> p k", k=KD)).then_inc(c_loaded, 16)
            with sp.Fori(0, HALF) as it:
                for s in range(2):
                    sp.wait_ge(used.sem, used.value(it, s - 1))
                    sp.dma_start(w[s][:], w_v[:, :, bass.ds(it * (2 * GROUP * P) + s * GROUP * P, GROUP * P)]
                                 ).then_inc(w_in[s], 16)

        @block.tensor
        def _(pe):
            pe.wait_ge(c_set, 1)
            with pe.Fori(0, HALF) as it:
                for s in range(2):
                    pe.wait_ge(w_in[s], loads[s].value(it, 16))
                    pe.wait_ge(used.sem, used.value(it, s - 1))
                    for b in range(GROUP):
                        for k in range(KD):
                            last = pe.matmul(acc[s][:, b, :], w[s][:, k, b * P:(b + 1) * P], c_act[:, k, :],
                                             start=(k == 0), stop=(k == KD - 1))
                    last.then_inc(ready.sem, 1)

        @block.scalar
        def _(act):
            act.wait_ge(c_loaded, 32)
            act.activation(c_act[:].rearrange("p k w -> p w k"), c_in[:], ACT.Silu).then_inc(c_set, 1)
            act.preload_act_table_set(EXP_LN)
            act.activation(t0[:], columns(cols, "b_lambda_2"), ACT.Abs).then_inc(act_n, 1)
            act.wait_ge(act_n, 1)
            act.activation(t0[:], t0[:], ACT.Exp, scale=-1.0).then_inc(act_n, 1)
            act.wait_ge(act_n, 2)
            act.activation(t0[:], t0[:], ACT.Ln, bias=1.0).then_inc(act_n, 1)
            act.wait_ge(dve_n, 4)
            act.activation(vec["lower"], t1[:], ACT.Exp).then_inc(act_n, 1)
            act.activation(t2[:], t2[:], ACT.Exp).then_inc(act_n, 1)

        @block.vector
        def _(dve):
            dve.sem_inc(used.sem, 2)
            done = [0]

            def link(ins):
                done[0] += 1
                ins.then_inc(dve_n, 1)
                dve.wait_ge(dve_n, done[0])

            l0, l1 = columns(cols, "a_lb_logits_2", 0, 8), columns(cols, "a_lb_logits_2", 8, 8)
            link(dve.tensor_tensor(t1[:], l0, l1, ALU.max))
            link(dve.tensor_tensor(t2[:], l1, t1[:], ALU.subtract))
            link(dve.tensor_tensor(t1[:], l0, t1[:], ALU.subtract))
            link(dve.tensor_scalar(vec["rate8"], columns(cols, "b_lambda_2"), -1.0, 0.0, ALU.mult, ALU.max))
            dve.wait_ge(act_n, 5)
            link(dve.tensor_tensor(vec["rate8"], vec["rate8"], t0[:], ALU.add))
            link(dve.tensor_scalar(vec["rate8"], vec["rate8"], -8.0, None, ALU.mult))
            link(dve.tensor_scalar(vec["rate16"], vec["rate8"], 2.0, None, ALU.mult))
            link(dve.tensor_tensor(t2[:], t2[:], vec["lower"], ALU.add))
            link(dve.reciprocal(t2[:], t2[:]))
            link(dve.tensor_tensor(vec["lower"], vec["lower"], t2[:], ALU.mult))
            b_ada = columns(cols, "b_ada")
            with dve.Fori(0, HALF) as it:
                for s in range(2):
                    dve.wait_ge(ready.sem, ready.value(it, s + 1))
                    here = bass.ds(it * (2 * GROUP) + s * GROUP, GROUP)
                    dve.tensor_tensor(mod[:, here, :], acc[s][:], b_ada[:, here].unsqueeze(2).to_broadcast([P, GROUP, 2]),
                                      ALU.add).then_inc(used.sem, 1)
            dve.wait_ge(used.sem, used.value(HALF, 0))
            pre, post = columns(cols, "pre_norm_w"), columns(cols, "post_norm_w")
            for w_, out in ((0, vec["gain_l"]), (1, vec["gain_c"])):
                link(dve.tensor_scalar(out, mod[:, KD:2 * KD, w_], 1.0, None, ALU.add))
                link(dve.tensor_tensor(out, out, pre, ALU.mult))
                link(dve.tensor_copy(vec["shift_l" if w_ == 0 else "shift_c"], mod[:, 0:KD, w_]))
            link(dve.tensor_tensor(vec["post_gain"], mod[:, 2 * KD:MB, 0], post, ALU.mult))


@stage
def norm_stage(nc, name, src, regions, dst=None, parts=None, add_to=None, feature_count=D):
    K = feature_count // P
    width = max(t0 + n for t0, n, _, _ in regions)
    with ExitStack() as ctx:
        def sb(nm, *shape):
            return ctx.enter_context(nc.sbuf_tensor(f"{name}_{nm}", [P, *shape], F32))

        def sem(nm):
            return nc.alloc_semaphore(f"{name}_{nm}")

        sq, inv, tmp = sb("sq", 2, width), sb("inv", width), sb("tmp", 2, width)
        eps = sb("eps", 1)
        sums = [ctx.enter_context(nc.psum_tensor(f"{name}_sums{i}", [P, 512], F32)) for i in range(len(regions))]
        eps_set, sq_set, sq_used, sums_ready = sem("eps_set"), sem("sq_set"), sem("sq_used"), sem("sums_ready")
        ln_set, inv_set, out_set, tmp_set, shifted = sem("ln_set"), sem("inv_set"), sem("out_set"), sem("tmp_set"), sem("shifted")
        hi_set, lo_set = sem("hi_set"), sem("lo_set")
        block = ctx.enter_context(nc.Block())

        @block.scalar
        def _(act):
            act.preload_act_table_set(EXP_LN)
            for k in range(K):
                if k >= 2:
                    act.wait_ge(sq_used, k - 1)
                act.activation(sq[:, k % 2, :], src[:, k, 0:width], ACT.Square).then_inc(sq_set, 1)
            act.wait_ge(eps_set, 1)
            act.wait_ge(sums_ready, 1)
            for r, (t0, n, _, _) in enumerate(regions):
                act.activation(inv[:, t0:t0 + n], sums[r][:, 0:n], ACT.Ln, scale=1.0 / feature_count,
                               bias=eps[:, 0:1]).then_inc(ln_set, 1)
            act.wait_ge(ln_set, len(regions))
            act.activation(inv[:], inv[:], ACT.Exp, scale=-0.5).then_inc(inv_set, 1)
            n_out = 0
            for k in range(K if parts is not None else 0):
                for t0, n, _, shift in regions:
                    n_out += 1
                    value = tmp[:, k % 2, t0:t0 + n]
                    act.wait_ge(tmp_set, n_out)
                    if shift is not None:
                        act.activation(value, value, ACT.Identity, bias=shift[:, k:k + 1]).then_inc(shifted, 1)
                        act.wait_ge(shifted, n_out)
                    act.activation(parts[0][:, k, t0:t0 + n], value, ACT.Copy).then_inc(hi_set, 1)

        @block.tensor
        def _(pe):
            for k in range(K):
                pe.wait_ge(sq_set, k + 1)
                for r, (t0, n, _, _) in enumerate(regions):
                    last = pe.matmul(sums[r][:, 0:n], ones_of(nc)[:], sq[:, k % 2, t0:t0 + n],
                                     start=(k == 0), stop=(k == K - 1))
                last.then_inc(sums_ready if k == K - 1 else sq_used, 1)

        @block.vector
        def _(dve):
            dve.memset(eps[:], EPS).then_inc(eps_set, 1)
            dve.wait_ge(inv_set, 1)
            if parts is not None:
                steps = [(k, *region[:3]) for k in range(K) for region in regions]
                lag = len(regions)
                for n_out in range(len(steps) + lag):
                    if n_out < len(steps):
                        k, t0, n, gain = steps[n_out]
                        here = slice(t0, t0 + n)
                        if n_out >= 2 * lag:
                            dve.wait_ge(lo_set, n_out - 2 * lag + 1)
                        dve.scalar_tensor_tensor(tmp[:, k % 2, here], src[:, k, here], gain[:, k:k + 1], inv[:, here],
                                                 ALU.mult, ALU.mult).then_inc(tmp_set, 1)
                    if n_out >= lag:
                        k, t0, n, _ = steps[n_out - lag]
                        here = slice(t0, t0 + n)
                        dve.wait_ge(hi_set, n_out - lag + 1)
                        dve.tensor_tensor(parts[1][:, k, here], tmp[:, k % 2, here], parts[0][:, k, here].bitcast(F32),
                                          ALU.subtract).then_inc(lo_set, 1)
                return
            for k in range(K):
                for t0, n, gain, _ in regions:
                    here = slice(t0, t0 + n)
                    if add_to is None:
                        dve.scalar_tensor_tensor(dst[:, k, here], src[:, k, here], gain[:, k:k + 1], inv[:, here],
                                                 ALU.mult, ALU.mult).then_inc(out_set, 1)
                    else:
                        dve.scalar_tensor_tensor(tmp[:, k % 2, :], src[:, k, here], gain[:, k:k + 1], inv[:, here],
                                                 ALU.mult, ALU.mult).then_inc(tmp_set, 1)
                        dve.wait_ge(tmp_set, k + 1)
                        dve.tensor_tensor(add_to[:, k, here], add_to[:, k, here], tmp[:, k % 2, :],
                                          ALU.add).then_inc(out_set, 1)


class Segment:

    def __init__(self, w, col0, blocks, kind, dst, func=None, taps=None, bias=None, extra=None):
        self.w, self.col0, self.blocks, self.kind, self.dst = w, col0, blocks, kind, dst
        self.func, self.taps, self.bias, self.extra = func, taps, bias, extra
        self.rounds = blocks // 4


@stage
def project_stage(nc, name, x, segments, lat0=0, kd=KD, small=None):
    has_ctx = lat0 > 0
    has_conv = any(s.kind in ("conv5", "conv4") for s in segments)
    C = min(4, kd)
    KC = kd // C
    R = C
    PAIR = 2 * P
    x_hi, x_lo = x
    with ExitStack() as ctx:
        def sb(nm, *shape, dt=F32):
            return ctx.enter_context(nc.sbuf_tensor(f"{name}_{nm}", [P, *shape], dt))

        def sem(nm):
            return nc.alloc_semaphore(f"{name}_{nm}")

        tokens = lat0 + LAT
        w = [sb(f"w{r}", KC, PAIR) for r in range(R)]
        w_hi, w_lo = ([sb(f"w_{part}{r}", KC, PAIR, dt=F32R) for r in range(R)] for part in ("hi", "lo"))
        out_b = [sb(f"out{b}", 2 if any(s.kind == "sig2" for s in segments) else 1, tokens) for b in range(2)]
        raw = [sb(f"raw{b}", tokens) for b in range(2)] if has_conv else None
        mixed = [sb(f"mixed{b}", tokens) for b in range(2)] if has_conv else None
        banks = 2 if has_ctx or any(s.kind == "tok" for s in segments) else 1
        acc = [[[ctx.enter_context(nc.psum_tensor(f"{name}_acc{q}{i}{r}", [P, 512], F32)) for r in range(banks)]
                for i in range(2)] for q in range(2)]
        w_in = [sem(f"w_in{r}") for r in range(R)]
        hi_s, lo_s, done_s, evac_s = sem("w_hi_set"), sem("w_lo_set"), sem("chunk_done"), sem("evacuated")
        tap_s, out_s = sem("taps"), sem("out_set")
        stored_s = [sem("stored0"), sem("stored1")]
        small_in, small_ready, small_set = sem("small_in"), sem("small_ready"), sem("small_set")
        if small:
            w_small = sb("w_small", kd, small["cols"] if small["token_major"] else 32 + small["cols"] // 2)

        plan, blocks_done, taps_done, outs_done, stores_done = [], 0, 0, 0, 0
        for g in segments:
            tap_n = {"conv5": 9, "conv4": 4, "gate": 1}.get(g.kind, 0)
            chunk0 = blocks_done // 2 * C
            plan.append(dict(
                hi=Sig(hi_s, 2 * C, chunk0), lo=Sig(lo_s, 2 * C, chunk0 + R), done=Sig(done_s, 2 * C, chunk0),
                evac=Sig(evac_s, 4, blocks_done + 4), taps=Sig(tap_s, 4 * tap_n, taps_done), tap_n=tap_n,
                out=Sig(out_s, 4, outs_done),
                loads=[Sig(s, 16 * 2 * C // R, 16 * chunk0 // R) for s in w_in],
                stores=[Sig(s, 32 * (2 if g.kind == "sig2" else 1), stores_done + 16) for s in stored_s]))
            blocks_done += g.blocks
            taps_done += g.blocks * tap_n
            outs_done += g.blocks if g.kind in ("conv5", "conv4") else 0
            if g.kind in ("act", "tok", "conv5", "conv4"):
                stores_done += 8 * g.blocks
            if g.kind == "sig2":
                stores_done += 16 * g.blocks
        block = ctx.enter_context(nc.Block())

        def rounds(eng, body):
            for g, pl in zip(segments, plan):
                last = g is segments[-1]
                if g.rounds - last > 0:
                    with eng.Fori(0, g.rounds - last) as it:
                        body(g, pl, it, False)
                if last:
                    body(g, pl, g.rounds - 1, True)

        @block.sync
        def _(sp):
            for g, pl in zip(segments, plan):
                w_v = g.w.rearrange("(k p) n -> p k n", p=P)
                with sp.Fori(0, g.rounds) as it:
                    for j in range(2 * C):
                        q, c = j // C, j % C
                        sp.wait_ge(lo_s, pl["lo"].value(it, j + 1 - R))
                        sp.dma_start(w[j % R][:], w_v[:, c * KC:(c + 1) * KC, bass.ds(it * (2 * PAIR) + (g.col0 + q * PAIR), PAIR)]
                                     ).then_inc(w_in[j % R], 16)

        @block.tensor
        def _(pe):
            if small:
                pe.wait_ge(small_in, 16 * len(small["parts"]))
                if small["token_major"]:
                    for m in range(tokens // P):
                        for k in range(kd):
                            for part in x:
                                last = pe.matmul(acc[1][0][0][:, m * small["cols"]:(m + 1) * small["cols"]],
                                                 part[:, k, m * P:(m + 1) * P].bitcast(F32), w_small[:, k, :],
                                                 start=(k == 0 and part is x_hi), stop=(k == kd - 1 and part is x_lo))
                else:
                    cols = w_small.shape[-1]
                    for k in range(kd):
                        for part in x:
                            last = pe.matmul(acc[1][0][0][0:cols, :], w_small[:, k, :], part[:, k, lat0:tokens].bitcast(F32),
                                             start=(k == 0 and part is x_hi), stop=(k == kd - 1 and part is x_lo))
                last.then_inc(small_ready, 1)
                pe.wait_ge(small_set, 1 if small["token_major"] else 2)

            def body(g, pl, it, final):
                for j in range(2 * C):
                    q, c = j // C, j % C
                    if c == 0:
                        pe.wait_ge(evac_s, pl["evac"].value(it, 2 * q - 2))
                    pe.wait_ge(lo_s, pl["lo"].value(it, j + 1))
                    hi, lo = w_hi[j % R], w_lo[j % R]
                    for kk in range(KC):
                        k = c * KC + kk
                        first, end = k == 0, k == kd - 1
                        if g.kind == "tok":
                            for m in range(LAT // P):
                                out = acc[q][m // 2][m % 2][:, 0:PAIR]
                                here = slice(lat0 + m * P, lat0 + (m + 1) * P)
                                pe.matmul(out, x_hi[:, k, here], hi[:, kk, :], start=first, stop=False)
                                pe.matmul(out, x_hi[:, k, here], lo[:, kk, :], start=False, stop=False)
                                last = pe.matmul(out, x_lo[:, k, here], hi[:, kk, :], start=False, stop=end)
                            continue
                        for i in range(2):
                            wh, wl = hi[:, kk, i * P:(i + 1) * P], lo[:, kk, i * P:(i + 1) * P]
                            lat = acc[q][i][0][:, :]
                            pe.matmul(lat, wh, x_hi[:, k, lat0:tokens], start=first, stop=False)
                            pe.matmul(lat, wh, x_lo[:, k, lat0:tokens], start=False, stop=False)
                            if g.kind == "conv5":
                                context = acc[q][i][1][:, 0:lat0]
                                pe.matmul(context, wh, x_hi[:, k, 0:lat0], start=first, stop=False)
                                pe.matmul(context, wh, x_lo[:, k, 0:lat0], start=False, stop=False)
                                pe.matmul(context, wl, x_hi[:, k, 0:lat0], start=False, stop=end)
                            last = pe.matmul(lat, wl, x_hi[:, k, lat0:tokens], start=False, stop=end)
                    last.then_inc(done_s, 1)

            rounds(pe, body)

        @block.scalar
        def _(act):
            def store(g, pl, it, s):
                b, blk = s % 2, it * 4 + s
                if g.kind in ("conv5", "conv4"):
                    act.wait_ge(out_s, pl["out"].value(it, s + 1))
                elif g.kind in ("act", "sig2", "tok"):
                    act.wait_ge(evac_s, pl["evac"].value(it, s + 1))
                else:
                    return
                if g.kind == "tok":
                    dst = g.dst.rearrange("(m p) f -> p m f", p=P)
                    m = 2 * (s % 2)
                    act.dma_start(dst[:, m:m + 2, bass.ds(it * 512 + (s // 2) * 256, 256)],
                                  out_b[b][:, 0, 0:512].rearrange("p (m f) -> p m f", m=2)).then_inc(stored_s[b], 16)
                elif g.kind == "sig2":
                    for i in range(2):
                        act.dma_start(g.dst[i][blk], out_b[b][:, i, :]).then_inc(stored_s[b], 16)
                elif g.kind == "conv5":
                    act.dma_start(g.dst[blk], out_b[b][:, 0, :]).then_inc(stored_s[b], 16)
                else:
                    act.dma_start(g.dst[blk], out_b[b][:, 0, lat0:tokens]).then_inc(stored_s[b], 16)

            if small:
                act.wait_ge(small_ready, 1)
                if small["token_major"]:
                    act.activation(small["out"][0], acc[1][0][0][:, 0:(tokens // P) * small["cols"]], ACT.Copy).then_inc(small_set, 1)
                else:
                    half = small["cols"] // 2
                    act.activation(small["out"][0], acc[1][0][0][0:half, :], ACT.Copy)
                    act.activation(small["out"][1], acc[1][0][0][32:32 + half, :], ACT.Copy).then_inc(small_set, 1)
            for c in range(C):
                act.wait_ge(w_in[c], 16)
                act.activation(w_hi[c][:], w[c][:], ACT.Copy).then_inc(hi_s, 1)

            def body(g, pl, it, final):
                for q in range(2):
                    for c in range(C if not (final and q == 1) else 0):
                        j = (q + 1) * C + c
                        r = j % R
                        act.wait_ge(w_in[r], pl["loads"][r].value(it, 16 * (j // R + 1)))
                        act.wait_ge(done_s, pl["done"].value(it, j + 1 - R))
                        act.activation(w_hi[r][:], w[r][:], ACT.Copy).then_inc(hi_s, 1)
                    act.wait_ge(done_s, pl["done"].value(it, (q + 1) * C))
                    if g.kind in ("conv5", "conv4"):
                        for b in range(2):
                            if g.kind == "conv5":
                                act.activation(raw[b][:, 0:lat0], acc[q][b][1][:, 0:lat0], ACT.Copy)
                            act.activation(raw[b][:, lat0:tokens], acc[q][b][0][:, :], ACT.Copy).then_inc(evac_s, 1)
                    for b in range(2):
                        s = 2 * q + b
                        blk = it * 4 + s
                        st = pl["stores"][b]
                        per_store = 32 if g.kind == "sig2" else 16
                        if g.kind in ("act", "sig2", "tok", "conv5", "conv4"):
                            act.wait_ge(st.sem, st.value(it, per_store * q))
                        bank = acc[q][b][0]
                        if g.kind == "act":
                            act.activation(out_b[b][:, 0, lat0:tokens], bank[:, :], g.func).then_inc(evac_s, 1)
                        elif g.kind == "sig2":
                            act.activation(out_b[b][:, 0, :], bank[:, :], ACT.Sigmoid)
                            act.activation(out_b[b][:, 1, :], bank[:, :], ACT.Sigmoid, scale=-1.0).then_inc(evac_s, 1)
                        elif g.kind == "tok":
                            act.activation(out_b[b][:, 0, 0:PAIR], bank[:, 0:PAIR], ACT.Copy)
                            act.activation(out_b[b][:, 0, PAIR:2 * PAIR], acc[q][b][1][:, 0:PAIR], ACT.Copy).then_inc(evac_s, 1)
                        elif g.kind in ("conv5", "conv4"):
                            act.wait_ge(tap_s, pl["taps"].value(it, (s + 1) * pl["tap_n"]))
                            bias = g.bias[:, bass.ds(blk, 1)] if g.bias is not None else 0.0
                            act.activation(out_b[b][:, 0, :], mixed[b][:], g.func, bias=bias).then_inc(out_s, 1)
                        elif g.kind == "keep":
                            act.activation(g.dst[:, bass.ds(blk, 1), :].rearrange("p o t -> p (o t)"), bank[:, :],
                                           ACT.Copy).then_inc(evac_s, 1)
                        elif g.kind == "gate":
                            act.wait_ge(out_s, pl["out"].value(it, s - 1) + 2)
                            act.activation(out_b[b][:, 0, :], bank[:, :], ACT.Sigmoid).then_inc(evac_s, 1)
                        store(g, pl, it, s)

            rounds(act, body)
            for b in range(2):
                act.wait_ge(stored_s[b], stores_done + 16)

        @block.vector
        def _(dve):
            dve.sem_inc(lo_s, R)
            dve.sem_inc(evac_s, 4)
            dve.sem_inc(stored_s[0], 16)
            dve.sem_inc(stored_s[1], 16)
            if any(g.kind == "gate" for g in segments):
                dve.sem_inc(out_s, 2)
            for c in range(C):
                dve.wait_ge(hi_s, c + 1)
                dve.tensor_tensor(w_lo[c][:], w[c][:], w_hi[c][:].bitcast(F32), ALU.subtract).then_inc(lo_s, 1)

            def taps(g, pl, it, s):
                b, blk = s % 2, it * 4 + s
                n = s * pl["tap_n"]
                dve.wait_ge(evac_s, pl["evac"].value(it, s + 1))
                main = 2 if g.kind == "conv5" else 3

                def weight(j):
                    return g.taps[:, bass.ds(blk + j * g.extra, 1)]

                dve.tensor_scalar(mixed[b][:], raw[b][:], weight(main), None, ALU.mult).then_inc(tap_s, 1)
                n += 1
                rows = (tokens - lat0) // GRID_W
                for j in (0, 1, 3, 4) if g.kind == "conv5" else (0, 1, 2):
                    off = j - main
                    dve.wait_ge(tap_s, pl["taps"].value(it, n))
                    if g.kind == "conv5":
                        out = slice(max(0, -off), lat0 - max(0, off))
                        src = slice(max(0, off), lat0 - max(0, -off))
                        dve.scalar_tensor_tensor(mixed[b][:, out], raw[b][:, src], weight(j), mixed[b][:, out],
                                                 ALU.mult, ALU.add).then_inc(tap_s, 1)
                        out = slice(max(0, -off), GRID_W - max(0, off))
                        src = slice(max(0, off), GRID_W - max(0, -off))
                        m_v = mixed[b][:, lat0:tokens].rearrange("p (r t) -> p r t", r=rows)
                        r_v = raw[b][:, lat0:tokens].rearrange("p (r t) -> p r t", r=rows)
                        dve.scalar_tensor_tensor(m_v[:, :, out], r_v[:, :, src], weight(j), m_v[:, :, out],
                                                 ALU.mult, ALU.add).then_inc(tap_s, 1)
                        n += 2
                    else:
                        dve.scalar_tensor_tensor(mixed[b][:, -off:LAT], raw[b][:, 0:LAT + off], weight(j),
                                                 mixed[b][:, -off:LAT], ALU.mult, ALU.add).then_inc(tap_s, 1)
                        n += 1

            def body(g, pl, it, final):
                for q in range(2):
                    for c in range(C if not (final and q == 1) else 0):
                        j = (q + 1) * C + c
                        r = j % R
                        dve.wait_ge(hi_s, pl["hi"].value(it, j + 1))
                        dve.tensor_tensor(w_lo[r][:], w[r][:], w_hi[r][:].bitcast(F32), ALU.subtract).then_inc(lo_s, 1)
                    for b in range(2):
                        s = 2 * q + b
                        here = bass.ds(it * 4 + s, 1)
                        if g.kind in ("conv5", "conv4"):
                            taps(g, pl, it, s)
                        elif g.kind == "add":
                            dve.wait_ge(done_s, pl["done"].value(it, (q + 1) * C))
                            here = g.dst[:, here, :].rearrange("p o t -> p (o t)")
                            dve.tensor_tensor(here, here, acc[q][b][0][:, :], ALU.add).then_inc(evac_s, 1)
                        elif g.kind == "gate":
                            dve.wait_ge(evac_s, pl["evac"].value(it, s + 1))
                            dve.tensor_tensor(out_b[b][:, 0, :], out_b[b][:, 0, :],
                                              g.extra[:, here, :].rearrange("p o t -> p (o t)"), ALU.mult).then_inc(tap_s, 1)
                            dve.wait_ge(tap_s, pl["taps"].value(it, s + 1))
                            here = g.dst[:, here, :].rearrange("p o t -> p (o t)")
                            dve.tensor_tensor(here, here, out_b[b][:, 0, :], ALU.add).then_inc(out_s, 1)

            rounds(dve, body)

        @block.gpsimd
        def _(pool):
            if small:
                at = 0
                if not small["token_major"]:
                    pool.memset(w_small[:], 0.0).then_inc(small_set, 1)
                    pool.wait_ge(small_set, 1)
                for part in small["parts"]:
                    n = part.shape[1]
                    pool.dma_start(w_small[:, :, at:at + n], part.rearrange("(k p) n -> p k n", p=P)).then_inc(small_in, 16)
                    at += n if small["token_major"] else 32


@stage
def first_gates_stage(nc, consts, a, raw, gdn_tabs, ssd_tabs):
    NS, NG = 2 * SSD_H, 2 * GDN_H
    N = NS + NG
    with ExitStack() as ctx:
        def sb(name, *shape):
            return ctx.enter_context(nc.sbuf_tensor("fg_" + name, [P, *shape], F32))

        def sem(name):
            return nc.alloc_semaphore("fg_" + name)

        bias, rate = sb("bias", N), sb("rate", N)
        x, e, soft, log_a = sb("x", CHUNKS, N), sb("e", CHUNKS, N), sb("soft", CHUNKS, N), sb("log_a", CHUNKS, N)
        beta = sb("beta", CHUNKS, NG)
        cum, total, to_end = sb("cum", CHUNKS, N), sb("total", CHUNKS, N), sb("to_end", CHUNKS, N)
        cum_p = ctx.enter_context(nc.psum_tensor("fg_cum_p", [P, CHUNKS, N], F32))
        total_p = ctx.enter_context(nc.psum_tensor("fg_total_p", [P, CHUNKS, N], F32))
        loaded, dve_n, act_n, sums_ready = sem("loaded"), sem("dve_n"), sem("act_n"), sem("sums_ready")
        block = ctx.enter_context(nc.Block())

        @block.sync
        def _(sp):
            for dst, ssd, gdn in ((bias, "ssd_dt_bias", "gdn_dt_bias"), (rate, "ssd_a_log", "gdn_a_log")):
                sp.dma_start(dst[:, 0:NS], a[ssd].rearrange("l d h -> l (d h)").to_broadcast([P, NS])).then_inc(loaded, 16)
                sp.dma_start(dst[:, NS:N], a[gdn].rearrange("l d h -> l (d h)").to_broadcast([P, NG])).then_inc(loaded, 16)

        @block.vector
        def _(dve):
            done = [0]

            def link(ins):
                done[0] += 1
                ins.then_inc(dve_n, 1)
                dve.wait_ge(dve_n, done[0])

            dve.wait_ge(loaded, 64)
            link(dve.tensor_tensor(x[:, :, 0:NS], raw[:, :, 0:NS],
                                   bias[:, 0:NS].unsqueeze(1).to_broadcast([P, CHUNKS, NS]), ALU.add))
            link(dve.tensor_tensor(x[:, :, NS:N], raw[:, :, NS + NG:GATES],
                                   bias[:, NS:N].unsqueeze(1).to_broadcast([P, CHUNKS, NG]), ALU.add))
            link(dve.tensor_scalar(soft[:], x[:], 0.0, None, ALU.max))
            dve.wait_ge(act_n, 5)
            link(dve.tensor_tensor(soft[:], soft[:], e[:], ALU.add))
            link(dve.tensor_tensor(log_a[:], soft[:], rate[:].unsqueeze(1).to_broadcast([P, CHUNKS, N]), ALU.mult))
            link(dve.tensor_scalar(log_a[:], log_a[:], -1.0, None, ALU.mult))
            link(dve.tensor_scalar(beta[:], beta[:], 1.0, None, ALU.add))
            link(dve.reciprocal(beta[:], beta[:]))
            dve.wait_ge(sums_ready, 1)
            link(dve.tensor_copy(cum[:], cum_p[:]))
            link(dve.tensor_copy(total[:], total_p[:]))
            link(dve.tensor_tensor(to_end[:], total[:], cum[:], ALU.subtract))
            dve.wait_ge(act_n, 7)

            def ssd(t):
                return ssd_tabs[:, t].rearrange("p c d h -> p c (d h)")

            def gdn(t):
                return gdn_tabs[:, t].rearrange("p c d h -> p c (d h)")

            link(dve.tensor_copy(ssd(0), soft[:, :, 0:NS]))
            link(dve.tensor_tensor(ssd(1), soft[:, :, 0:NS], to_end[:, :, 0:NS], ALU.mult))
            link(dve.tensor_copy(ssd(2), total[:, :, 0:NS]))
            link(dve.tensor_copy(ssd(3), cum[:, :, 0:NS]))
            link(dve.tensor_copy(gdn(0), beta[:]))
            link(dve.tensor_copy(gdn(2), to_end[:, :, NS:N]))
            link(dve.tensor_copy(gdn(3), total[:, :, NS:N]))
            link(dve.tensor_copy(gdn(4), cum[:, :, NS:N]))

        @block.scalar
        def _(act):
            act.preload_act_table_set(EXP_LN)
            act.wait_ge(loaded, 64)
            act.activation(rate[:], rate[:], ACT.Exp).then_inc(act_n, 1)
            act.activation(beta[:], raw[:, :, NS:NS + NG], ACT.Exp, scale=-1.0).then_inc(act_n, 1)
            act.wait_ge(dve_n, 2)
            act.activation(e[:], x[:], ACT.Abs).then_inc(act_n, 1)
            act.wait_ge(act_n, 3)
            act.activation(e[:], e[:], ACT.Exp, scale=-1.0).then_inc(act_n, 1)
            act.wait_ge(act_n, 4)
            act.activation(e[:], e[:], ACT.Ln, bias=1.0).then_inc(act_n, 1)
            act.wait_ge(dve_n, 11)
            act.activation(to_end[:], to_end[:], ACT.Exp).then_inc(act_n, 1)
            act.activation(total[:], total[:], ACT.Exp).then_inc(act_n, 1)
            act.wait_ge(dve_n, 19)
            act.activation(gdn_tabs[:, 1].rearrange("p c d h -> p c (d h)"), cum[:, :, NS:N], ACT.Exp).then_inc(act_n, 1)

        @block.tensor
        def _(pe):
            pe.wait_ge(dve_n, 6)
            for lo, n in ((0, SSD_H), (NS, GDN_H)):
                for d in range(2):
                    cols = slice(lo + d * n, lo + (d + 1) * n)
                    pe.matmul(cum_p[:, :, cols], consts["causal"][:, d, :], log_a[:, :, cols], start=True, stop=True)
            pe.matmul(total_p[:], consts["ones"][:], log_a[:], start=True, stop=True).then_inc(sums_ready, 1)


@stage
def lru_stage(nc, a, cols, vec, xT, zT, yT):
    B = 8
    with ExitStack() as ctx:
        def sb(name, *shape):
            return ctx.enter_context(nc.sbuf_tensor("lru_" + name, [P, *shape], F32))

        def sem(name):
            return nc.alloc_semaphore("lru_" + name)

        x, z, r, i, dec = sb("x", B, LAT), sb("z", B, LAT), sb("r", B, LAT), sb("i", B, LAT), sb("dec", B, LAT)
        sq = sb("sq", B, LAT)
        wr, wi = sb("wr", B, P), sb("wi", B, P)
        acc = [ctx.enter_context(nc.psum_tensor(f"lru_acc{n}", [P, LAT], F32)) for n in range(4)]
        loaded, z_loaded, ready, evacuated = sem("loaded"), sem("z_loaded"), sem("ready"), sem("evacuated")
        a_set, sq_exp, th_set = sem("a_set"), sem("sq_exp"), sem("th_set")
        gap, root, ix, u_set, hs, y_set = sem("gap"), sem("root"), sem("ix"), sem("u_set"), sem("hs"), sem("y_set")
        stored = sem("stored")
        block = ctx.enter_context(nc.Block())

        @block.sync
        def _(sp):
            sp.dma_start(x[:], xT.rearrange("b p t -> p b t")).then_inc(loaded, 16)
            sp.dma_start(wr[:], a["b_w_r_2"].rearrange("l n c d -> c (l n) d")).then_inc(loaded, 16)
            sp.dma_start(wi[:], a["b_w_i_2"].rearrange("l n c d -> c (l n) d")).then_inc(loaded, 16)
            sp.dma_start(z[:], zT.rearrange("b p t -> p b t")).then_inc(z_loaded, 16)
            for b in range(B):
                sp.wait_ge(y_set, b + 1)
                sp.dma_start(yT[b], r[:, b, :]).then_inc(stored, 16)
            sp.wait_ge(stored, 16 * B)

        @block.tensor
        def _(pe):
            pe.wait_ge(loaded, 48)
            for b in range(B):
                for j, w in enumerate((wr, wi)):
                    n = 2 * b + j
                    if n >= 4:
                        pe.wait_ge(evacuated, n - 3)
                    pe.matmul(acc[n % 4][:], w[:, b, :], x[:, b, :], start=True, stop=True).then_inc(ready, 1)

        @block.scalar
        def _(act):
            b_r, b_i = columns(cols, "b_b_r_2"), columns(cols, "b_b_i_2")
            for b in range(B):
                for j, (bias, dst) in enumerate(((b_r, r), (b_i, i))):
                    n = 2 * b + j
                    act.wait_ge(ready, n + 1)
                    act.activation(dst[:, b, :], acc[n % 4][:], ACT.Sigmoid, bias=bias[:, b:b + 1]).then_inc(evacuated, 1)
            act.wait_ge(evacuated, 2 * B)
            for b in range(B):
                act.activation(dec[:, b, :], r[:, b, :], ACT.Exp, scale=vec["rate8"][:, b:b + 1]).then_inc(a_set, 1)
                act.activation(sq[:, b, :], r[:, b, :], ACT.Exp, scale=vec["rate16"][:, b:b + 1]).then_inc(sq_exp, 1)
                act.activation(r[:, b, :], r[:, b, :], ACT.Tanh, scale=vec["rate8"][:, b:b + 1]).then_inc(th_set, 1)
            for b in range(B):
                act.wait_ge(gap, b + 1)
                act.activation(sq[:, b, :], sq[:, b, :], ACT.Sqrt, scale=-1.0).then_inc(root, 1)

        @block.gpsimd
        def _(pool):
            for b in range(B):
                pool.wait_ge(evacuated, 2 * b + 2)
                pool.tensor_tensor(i[:, b, :], i[:, b, :], x[:, b, :], ALU.mult).then_inc(ix, 1)

        @block.vector
        def _(dve):
            for b in range(B):
                dve.wait_ge(sq_exp, b + 1)
                dve.wait_ge(th_set, b + 1)
                dve.scalar_tensor_tensor(sq[:, b, :], sq[:, b, :], 1.0, r[:, b, :], ALU.add, ALU.mult).then_inc(gap, 1)
            dve.wait_ge(z_loaded, 16)
            for b in range(B):
                dve.wait_ge(root, b + 1)
                dve.wait_ge(ix, b + 1)
                dve.tensor_tensor(i[:, b, :], i[:, b, :], sq[:, b, :], ALU.mult).then_inc(u_set, 1)
                dve.wait_ge(u_set, b + 1)
                dve.tensor_tensor_scan(x[:, b, :], dec[:, b, :], i[:, b, :], 0.0, ALU.mult, ALU.add).then_inc(hs, 1)
                dve.wait_ge(hs, b + 1)
                dve.tensor_tensor(r[:, b, :], x[:, b, :], z[:, b, :], ALU.mult).then_inc(y_set, 1)


@stage
def load_stage(nc, name, dst, src):
    loaded = nc.alloc_semaphore(name + "_in")
    with nc.Block() as block:
        @block.sync
        def _(sp):
            half = src.shape[0] // 2
            for i in range(2):
                here = slice(i * half, (i + 1) * half)
                sp.dma_start(dst[:, here, :], src[here].rearrange("b p t -> p b t")).then_inc(loaded, 16)
            sp.wait_ge(loaded, 32)


@stage
def split_stage(nc, name, parts, src):
    from_dram = src.shape[0] != P
    K = src.shape[0] if from_dram else src.shape[1]
    STEP = 2
    with ExitStack() as ctx:
        ring = ctx.enter_context(nc.sbuf_tensor(name + "_ring", [P, 4, STEP, LAT], F32)) if from_dram else None
        loaded = [nc.alloc_semaphore(f"{name}_in{i}") for i in range(4)]
        hi_set, lo_set = nc.alloc_semaphore(name + "_hi_set"), nc.alloc_semaphore(name + "_lo_set")
        block = ctx.enter_context(nc.Block())

        def values(n):
            return ring[:, n % 4] if from_dram else src[:, n * STEP:(n + 1) * STEP, :]

        if from_dram:
            @block.sync
            def _(sp):
                for n in range(K // STEP):
                    if n >= 4:
                        sp.wait_ge(lo_set, n - 3)
                    sp.dma_start(ring[:, n % 4], src[n * STEP:(n + 1) * STEP].rearrange("b p t -> p b t")
                                 ).then_inc(loaded[n % 4], 16)

        @block.scalar
        def _(act):
            for n in range(K // STEP):
                if from_dram:
                    act.wait_ge(loaded[n % 4], 16 * (n // 4 + 1))
                act.activation(parts[0][:, n * STEP:(n + 1) * STEP, :], values(n), ACT.Copy).then_inc(hi_set, 1)

        @block.vector
        def _(dve):
            for n in range(K // STEP):
                here = slice(n * STEP, (n + 1) * STEP)
                dve.wait_ge(hi_set, n + 1)
                dve.tensor_tensor(parts[1][:, here, :], values(n), parts[0][:, here, :].bitcast(F32),
                                  ALU.subtract).then_inc(lo_set, 1)


@stage
def turn_in_stage(nc, name, ident, dst, src):
    F = src.shape[1]
    with ExitStack() as ctx:
        tok = ctx.enter_context(nc.sbuf_tensor(name + "_tok", [P, LAT // P, F], F32))
        turned_p = [ctx.enter_context(nc.psum_tensor(f"{name}_p{i}", [P, LAT], F32)) for i in range(2)]
        loaded, turned, copied = (nc.alloc_semaphore(f"{name}_{s}") for s in ("in", "turned", "copied"))
        block = ctx.enter_context(nc.Block())

        @block.sync
        def _(sp):
            sp.dma_start(tok[:], src.rearrange("(m p) f -> p m f", p=P)).then_inc(loaded, 16)

        @block.tensor
        def _(pe):
            pe.wait_ge(loaded, 16)
            for f in range(F // P):
                if f >= 2:
                    pe.wait_ge(copied, f - 1)
                for m in range(LAT // P):
                    last = pe.transpose(turned_p[f % 2][:, m * P:(m + 1) * P], tok[:, m, f * P:(f + 1) * P], ident)
                last.then_inc(turned, 1)

        @block.vector
        def _(dve):
            for f in range(F // P):
                dve.wait_ge(turned, f + 1)
                dve.tensor_copy(dst[:, f, :], turned_p[f % 2][:]).then_inc(copied, 1)


@stage
def turn_out_stage(nc, ident, src, out):
    with ExitStack() as ctx:
        tok = ctx.enter_context(nc.sbuf_tensor("to_tok", [P, 2, D], F32))
        turned_p = [ctx.enter_context(nc.psum_tensor(f"to_p{i}", [P, 4, P], F32)) for i in range(4)]
        turned, copied = nc.alloc_semaphore("to_turned"), nc.alloc_semaphore("to_copied")
        stored = [nc.alloc_semaphore(f"to_stored{i}") for i in range(2)]
        block = ctx.enter_context(nc.Block())

        @block.tensor
        def _(pe):
            for m in range(LAT // P):
                for g in range(4):
                    n = 4 * m + g
                    if n >= 4:
                        pe.wait_ge(copied, n - 3)
                    for k in range(4):
                        last = pe.transpose(turned_p[n % 4][:, k, :], src[:, 4 * g + k, m * P:(m + 1) * P], ident)
                    last.then_inc(turned, 1)

        @block.vector
        def _(dve):
            for m in range(LAT // P):
                if m >= 2:
                    dve.wait_ge(stored[m % 2], 16 * (m // 2))
                for g in range(4):
                    n = 4 * m + g
                    dve.wait_ge(turned, n + 1)
                    dve.tensor_copy(tok[:, m % 2, g * 512:(g + 1) * 512].rearrange("p (k f) -> p k f", k=4),
                                    turned_p[n % 4][:]).then_inc(copied, 1)

        @block.sync
        def _(sp):
            for m in range(LAT // P):
                sp.wait_ge(copied, 4 * m + 4)
                sp.dma_start(out[m * P:(m + 1) * P, :], tok[:, m % 2, :]).then_inc(stored[m % 2], 16)
            for i in range(2):
                sp.wait_ge(stored[i], 32)


@stage
def bias_stage(nc, a, bias):
    loaded = nc.alloc_semaphore("ml_bias_in")
    with nc.Block() as block:
        @block.sync
        def _(sp):
            sp.dma_start(bias[:, 0:1], a["c_b_i_2"].rearrange("l h -> h l")).then_inc(loaded, 16)
            sp.dma_start(bias[:, 1:2], a["c_b_f_2"].rearrange("l h -> h l")).then_inc(loaded, 16)
            sp.wait_ge(loaded, 32)


@stage
def skip_stage(nc, a, skip):
    loaded, made = nc.alloc_semaphore("skip_in"), nc.alloc_semaphore("skip_set")
    with nc.sbuf_tensor("skip_row", [P, SSD_H], F32) as row, nc.Block() as block:
        @block.sync
        def _(sp):
            sp.dma_start(row[:], a["ssd_d"].to_broadcast([P, SSD_H])).then_inc(loaded, 16)

        @block.vector
        def _(dve):
            dve.wait_ge(loaded, 16)
            for s in range(2):
                part = slice(s * SSD_P, (s + 1) * SSD_P)
                dve.tensor_copy(skip[part, :], row[part, :].rearrange("p (b s) -> p s b", s=2)[:, s, :]).then_inc(made, 1)


def kernel_program(nc, a, out):
    def scratch(name, *shape):
        return nc.dram_tensor("s_" + name, shape, F32).ap()

    w_in = a["w_in"].rearrange("l k n -> (l k) n")
    e_in = a["e_w_in_2"].rearrange("l k n -> (l k) n")
    o_in = a["o_w_in_2"].rearrange("l k n -> (l k) n")

    with ExitStack() as ctx:
        def sb(name, *shape):
            return ctx.enter_context(nc.sbuf_tensor(name, [P, *shape], F32))

        consts = {key: sb("k_" + key, *shape) for key, shape in CONSTS.items()}
        nc_ones[id(nc)] = consts["ones"]
        cols = sb("cols", len(ROWS), P)
        vec_t = sb("vec", 5 * KD + 3 * 8)
        vec = {}
        for n, key in enumerate(("gain_l", "shift_l", "gain_c", "shift_c", "post_gain")):
            vec[key] = vec_t[:, n * KD:(n + 1) * KD]
        for n, key in enumerate(("rate8", "rate16", "lower")):
            vec[key] = vec_t[:, 5 * KD + 8 * n:5 * KD + 8 * (n + 1)]

        def split_pair(owner, name, *shape):
            return [owner.enter_context(nc.sbuf_tensor(f"{name}_{part}", [P, *shape], F32R)) for part in ("hi", "lo")]

        h_dram = scratch("h", KD, P, LAT)
        z1, y1 = scratch("z1", KD, P, LAT), scratch("y1", KD, P, LAT)
        xbc, qkv = scratch("xbc", XBC_BLOCKS, P, TOK), scratch("qkv", QKV_BLOCKS, P, TOK)
        with ExitStack() as first:
            gdn_tabs = first.enter_context(nc.sbuf_tensor("gdn_tabs", [P, GDN_TABS, CHUNKS, 2, GDN_H], F32))
            ssd_tabs = first.enter_context(nc.sbuf_tensor("ssd_tabs", [P, SSD_TABS, CHUNKS, 2, SSD_H], F32))
            raw_gates = first.enter_context(nc.sbuf_tensor("raw_gates", [P, CHUNKS, GATES], F32))
            skip = first.enter_context(nc.sbuf_tensor("skip", [P, 8], F32))
            with ExitStack() as inner:
                u = split_pair(inner, "u1", KD, TOK)
                with nc.sbuf_tensor("x1", [P, KD, TOK], F32) as x_all:
                    setup_stage(nc, a, consts, cols, x_all, h_dram)
                    with nc.sbuf_tensor("mod", [P, 3 * KD, 2], F32) as mod:
                        modulation_stage(nc, a, cols, mod, vec)
                    norm_stage(nc, "pre", x_all, [(0, CTX, vec["gain_c"], vec["shift_c"]),
                                                  (CTX, LAT, vec["gain_l"], vec["shift_l"])], parts=u)
                project_stage(nc, "p1", u, [
                    Segment(w_in, OFF_QKV, QKV_BLOCKS, "conv5", qkv, ACT.Silu, columns(cols, "conv_gdn_w"), None, QKV_BLOCKS),
                    Segment(w_in, OFF_XBC, XBC_BLOCKS, "conv5", xbc, ACT.Silu, columns(cols, "conv_ssd_w"),
                            columns(cols, "conv_ssd_b"), XBC_BLOCKS),
                    Segment(w_in, 0, Z_BLOCKS, "act", z1, ACT.Silu),
                ], lat0=CTX, small=dict(cols=GATES, token_major=True, out=[flat(raw_gates[:])],
                                        parts=[w_in[:, OFF_DT:OFF_QKV], w_in[:, OFF_BETA:OFF_BETA + 4 * GDN_H]]))
            first_gates_stage(nc, consts, a, raw_gates, gdn_tabs, ssd_tabs)
            skip_stage(nc, a, skip)
            gdn_stage(nc, consts, qkv, gdn_tabs, columns(cols, "gdn_norm_w"), z1[8:16], y1[8:16])
            ssd_stage(nc, consts, xbc, ssd_tabs, skip, columns(cols, "ssd_norm_w"), z1[0:8], y1[0:8])
        h = sb("h", KD, LAT)
        with ExitStack() as inner:
            y = split_pair(inner, "y_in1", KD, LAT)
            mix = inner.enter_context(nc.sbuf_tensor("mix1", [P, KD, LAT], F32))
            load_stage(nc, "lh", h, h_dram)
            split_stage(nc, "ly1", y, y1)
            project_stage(nc, "o1", y, [Segment(a["w_out"].rearrange("l k n -> (l k) n"), 0, KD, "keep", mix)])
            norm_stage(nc, "post", mix, [(0, LAT, vec["post_gain"], None)], add_to=h)

        q2, s2, n2 = (scratch(n, 8, P, LAT) for n in ("q2", "s2", "n2"))
        v2, za2, xb2, zb2 = scratch("v2", LAT, 1024), scratch("za2", 8, P, LAT), scratch("xb2", 8, P, LAT), scratch("zb2", 8, P, LAT)
        y2 = scratch("y2", KD, P, LAT)
        with ExitStack() as inner:
            u = split_pair(inner, "u2", KD, LAT)
            norm_stage(nc, "en", h, [(0, LAT, columns(cols, "e_norm_2"), None)], parts=u)
            project_stage(nc, "p2", u, [
                Segment(e_in, 0, 8, "act", q2, ACT.Silu),
                Segment(e_in, 1024, 8, "sig2", (s2, n2)),
                Segment(e_in, 2048, 8, "tok", v2),
                Segment(e_in, 3072, 8, "act", za2, ACT.Silu),
                Segment(e_in, 4096, 8, "conv4", xb2, ACT.Identity, columns(cols, "b_conv_w_2"), columns(cols, "b_conv_b_2"), 8),
                Segment(e_in, 5120, 8, "act", zb2, ACT.Silu),
            ])
        hgrn_stage(nc, consts, q2, s2, n2, v2, vec["lower"], columns(cols, "a_norm_2"), za2, y2[0:8])
        lru_stage(nc, a, cols, vec, xb2, zb2, y2[8:16])
        with ExitStack() as inner:
            y = split_pair(inner, "y_in2", KD, LAT)
            split_stage(nc, "ly2", y, y2)
            project_stage(nc, "o2", y, [Segment(a["e_w_out_2"].rearrange("l k n -> (l k) n"), 0, KD, "add", h)])
        embed_stages(nc, a, consts, cols, h, 0)

        qk3, v3 = scratch("qk3", 16, P, LAT), scratch("v3", LAT, D)
        og3, z3, y3 = scratch("og3", 16, P, LAT), scratch("z3", 16, P, LAT), scratch("y3", 16, P, LAT)
        with ExitStack() as last:
            tabs = last.enter_context(nc.sbuf_tensor("ml_tabs", [P, ML_TABS, ML_CH, ML_H], F32))
            gates = last.enter_context(nc.sbuf_tensor("ml_raw", [ML_H, 2, LAT], F32))
            with ExitStack() as inner:
                u = split_pair(inner, "u3", KD, LAT)
                norm_stage(nc, "on", h, [(0, LAT, columns(cols, "o_norm_2"), None)], parts=u)
                project_stage(nc, "p3", u, [
                    Segment(o_in, 0, 16, "conv4", qk3, ACT.Silu, columns(cols, "c_conv_w_2"), columns(cols, "c_conv_b_2"), 16),
                    Segment(o_in, 2048, 16, "tok", v3),
                    Segment(o_in, 4096, 16, "act", og3, ACT.Sigmoid),
                    Segment(o_in, 6144, 16, "act", z3, ACT.Silu),
                ], small=dict(cols=2 * ML_H, token_major=False, out=[gates[:, 0, :], gates[:, 1, :]],
                              parts=[o_in[:, 8192:8192 + ML_H], o_in[:, 8192 + ML_H:8192 + 2 * ML_H]]))
            bias = last.enter_context(nc.sbuf_tensor("ml_bias", [ML_H, 2], F32))
            bias_stage(nc, a, bias)
            mlstm_gates_stage(nc, consts, gates[:, 0, :], gates[:, 1, :], bias[:, 0:1], bias[:, 1:2], tabs)
            mlstm_stage(nc, consts, qk3, v3, tabs, columns(cols, "c_norm_2"), og3, z3, y3)
        with ExitStack() as inner:
            y = split_pair(inner, "y_in3", KD, LAT)
            split_stage(nc, "ly3", y, y3)
            project_stage(nc, "o3", y, [Segment(a["o_w_out_2"].rearrange("l k n -> (l k) n"), 0, KD, "add", h)])
        embed_stages(nc, a, consts, cols, h, 1)
        with nc.sbuf_tensor("u4", [P, KD, LAT], F32) as u:
            norm_stage(nc, "fn", h, [(0, LAT, columns(cols, "final_norm_2"), None)], dst=u)
            turn_out_stage(nc, consts["ident"][:], u, out.rearrange("b t f -> (b t) f"))


def embed_stages(nc, a, consts, cols, h, i):
    with ExitStack() as ctx:
        def split_pair(owner, name, blocks):
            return [owner.enter_context(nc.sbuf_tensor(f"{name}{i}_{part}", [P, blocks, LAT], F32R)) for part in ("hi", "lo")]

        pl = ctx.enter_context(nc.sbuf_tensor(f"pl{i}", [P, KD, LAT], F32))
        with ExitStack() as inner:
            p_t = inner.enter_context(nc.sbuf_tensor(f"p_t{i}", [P, 2, LAT], F32))
            p_parts = split_pair(inner, "p", 2)
            turn_in_stage(nc, f"ti{i}", consts["ident"][:], p_t, a["p_2"][i, 0])
            split_stage(nc, f"ps{i}", p_parts, p_t)
            project_stage(nc, f"e{i}", p_parts, [Segment(a["ple_w_2"][i], 0, KD, "keep", pl)], kd=2)
        norm_stage(nc, f"pn{i}", pl, [(0, LAT, columns(cols, "ple_norm_2", 16 * i, 16), None)], dst=pl)
        h_parts = split_pair(ctx, "h", KD)
        split_stage(nc, f"hs{i}", h_parts, h)
        project_stage(nc, f"g{i}", h_parts, [Segment(a["ple_gate_w_2"][i], 0, KD, "gate", h, extra=pl)])


nc_ones = {}


def ones_of(nc):
    return nc_ones[id(nc)]


_INS = ["x", "c", "ctx", "c_ctx", "w_ada", "b_ada", "pre_norm_w", "post_norm_w", "w_in", "conv_ssd_w", "conv_ssd_b",
        "conv_gdn_w", "ssd_a_log", "ssd_dt_bias", "ssd_d", "ssd_norm_w", "gdn_a_log", "gdn_dt_bias", "gdn_norm_w",
        "w_out", "p_2", "e_norm_2", "e_w_in_2", "a_lb_logits_2", "a_norm_2", "b_conv_w_2", "b_conv_b_2", "b_w_r_2",
        "b_b_r_2", "b_w_i_2", "b_b_i_2", "b_lambda_2", "e_w_out_2", "o_norm_2", "o_w_in_2", "c_conv_w_2",
        "c_conv_b_2", "c_b_i_2", "c_b_f_2", "c_norm_2", "o_w_out_2", "ple_w_2", "ple_norm_2", "ple_gate_w_2",
        "final_norm_2"]


def kernel(**inputs):
    import numpy as _np
    import concourse.bacc as _bacc
    from concourse import mybir as _mybir
    from concourse.bass_utils import run_bass_kernel_spmd as _run

    nc = _bacc.Bacc("TRN2", target_bir_lowering=False, num_devices=1)
    arrays, args = {}, {}
    for name, value in [(n, inputs[n]) for n in _INS] + list(constants().items()):
        value = _np.ascontiguousarray(value)
        arrays[f"in_{name}_dram"] = value
        args[name] = nc.dram_tensor(f"in_{name}_dram", value.shape, _mybir.dt.from_np(value.dtype), kind="ExternalInput").ap()
    out = nc.dram_tensor("out_0_dram", (1, LAT, D), _mybir.dt.float32, kind="ExternalOutput").ap()
    kernel_program(nc, args, out)
    return _run(nc, [arrays], core_ids=[0]).results[0]["out_0_dram"]
```

```python
from contextlib import ExitStack

import numpy as np
import concourse.bass as bass
from concourse import mybir

F32 = mybir.dt.float32
F32R = mybir.dt.float32r
ALU = mybir.AluOpType
ACT = mybir.ActivationFunctionType
AX = mybir.AxisListType
EXP_LN = "natural_log_exp_and_others"

P = 128
D = 2048
KD = D // P
LAT = 512
CTX = 256
TOK = CTX + LAT
GRID_W = 64
EPS = 1e-6
CHUNKS = TOK // P
CTX_CHUNKS = CTX // P
NEG = -1.0e30
LEVELS = 7


def stage(build):
    def run(nc, *args, **kwargs):
        before = nc.snapshot_sems()
        build(nc, *args, **kwargs)
        nc.clear_and_free_semaphores(nc.allocated_since(before))
        nc.all_engine_barrier()
    return run


class Sig:

    def __init__(self, sem, per=1, base=0):
        self.sem, self.per, self.base = sem, per, base

    def value(self, it, n):
        return it * self.per + (self.base + n)


def constants():
    r = np.arange(P)
    ident = np.eye(P, dtype=np.float32)
    causal = np.stack([r[:, None] <= r[None, :], r[:, None] >= r[None, :]]).astype(np.float32)
    neg = np.where(causal > 0, 0.0, NEG).astype(np.float32)
    low = []
    for lev in range(LEVELS):
        b = 1 << lev
        blk, half = r // (2 * b), (r // b) % 2
        low.append((blk[:, None] == blk[None, :]) & (half[:, None] == 1) & (half[None, :] == 0))
    low = np.stack(low).astype(np.float32)
    pair = np.stack([low, low.transpose(0, 2, 1)], axis=1)
    scan = np.concatenate([low.transpose(0, 2, 1), ident[None]])
    chunk_start = np.ones((P, LAT), np.float32)
    chunk_start[:, ::P] = 0.0
    last_row = np.zeros((P, P), np.float32)
    last_row[P - 1] = 1.0
    return {
        "c_ident": ident,
        "c_ones": np.ones((P, P), np.float32),
        "c_causal": np.ascontiguousarray(causal.transpose(1, 0, 2)).reshape(P, 2 * P),
        "c_neg": np.ascontiguousarray(neg.transpose(1, 0, 2)).reshape(P, 2 * P),
        "c_pair": np.ascontiguousarray(pair.transpose(2, 0, 1, 3)).reshape(P, LEVELS * 2 * P),
        "c_scan": np.ascontiguousarray(scan.transpose(1, 0, 2)).reshape(P, (LEVELS + 1) * P),
        "c_start": chunk_start,
        "c_last": last_row,
    }


GDN_H = 8
GDN_TABS = 5


@stage
def gdn_stage(nc, consts, qkvT, tabs, gnorm, zT, yT):
    PROB = 2 * CHUNKS
    ORDER = [list(range(CHUNKS)), [1, 0, 5, 4, 3, 2]]
    ident, ones, neg, pair = consts["ident"], consts["ones"], consts["neg"], consts["pair"]
    with ExitStack() as ctx:
        def sb(name, *shape):
            return ctx.enter_context(nc.sbuf_tensor("gdn_" + name, [P, *shape], F32))

        def sig(name, per=1, base=0):
            return Sig(nc.alloc_semaphore("gdn_" + name), per, base)

        raw_q, raw_k, raw_v = sb("raw_q", LAT), sb("raw_k", TOK), sb("raw_v", TOK)
        z_in = sb("z_in", LAT)
        sq_k, sq_q = sb("sq_k", TOK), sb("sq_q", LAT)
        k_n, q_n = sb("k_n", TOK), sb("q_n", LAT)
        k_tok, v_tok = sb("k_tok", CHUNKS, P), sb("v_tok", CHUNKS, P)
        tab = sb("tab", GDN_TABS, CHUNKS, 2)
        ncum = sb("ncum", CHUNKS, 2)
        dec = sb("dec", CHUNKS, 2, P)
        qdec = sb("qdec", CHUNKS - CTX_CHUNKS, 2, P)
        a_t = sb("a_t", CHUNKS, 2, P)
        attn = sb("attn", CHUNKS - CTX_CHUNKS, 2, P)
        x_m, y_m = sb("x_m", CHUNKS, 2, P), sb("y_m", CHUNKS, 2, P)
        t1 = sb("t1", CHUNKS, 2, P)
        k_grow, k_end = sb("k_grow", CHUNKS, 2, P), sb("k_end", CHUNKS, 2, P)
        w_neg = sb("w_neg", CHUNKS, 2, P)
        state, v_new = sb("state", 2, P), sb("v_new", 2, P)
        o_dir, o_sum, o_sq, y_out = sb("o_dir", 2, LAT), sb("o_sum", LAT), sb("o_sq", LAT), sb("y_out", LAT)
        eps, ln_scale = sb("eps", 1), sb("ln_scale", 1)
        bank = [ctx.enter_context(nc.psum_tensor(f"gdn_bank{i}", [P, 512], F32)) for i in range(8)]

        def quad(i):
            return bank[i][:, :].rearrange("p (c d q) -> p c d q", c=2, d=2)

        loaded, z_loaded = sig("loaded", 48), sig("z_loaded", 16)
        head_done = sig("head_done", 1, 1)
        y_set = sig("y_set")
        stored = sig("stored", 16, 16)
        consts_set = sig("consts_set")
        staged = sig("staged", 2)
        squared = sig("squared", 2)
        sums = sig("sums", 3)
        norm_ln, inv_norm = sig("norm_ln", 3), sig("inv_norm", 3)
        normed = sig("normed", 2)
        v_turned, v_copied = sig("v_turned"), sig("v_copied", 2)
        k_turned, k_copied = sig("k_turned"), sig("k_copied", 2)
        dmat, dec_read = sig("dmat", 3), sig("dec_read", 3)
        emat, qdec_set = sig("emat", 2), sig("qdec_set", 2)
        q_decayed = sig("q_decayed", 1)
        products, a_set, attn_set = sig("products", 3), sig("a_set", 3), sig("attn_set", 2)
        first_m, first_t, first_set = sig("first_m", 3), sig("first_t", 3), sig("first_set", 3)
        t1_ready, t1_set = sig("t1_ready", 18), sig("t1_set", 18)
        t2_ready, xy_set = sig("t2_ready", 18), sig("xy_set", 18)
        k_scaled = sig("k_scaled", 2)
        w_ready, w_set = sig("w_ready", 3), sig("w_set", 3)
        v_ready, v_set = sig("v_ready", 12), sig("v_set", 12)
        o_ready, o_set = sig("o_ready", 8), sig("o_set", 8)
        s_ready, s_set = sig("s_ready", 10), sig("s_set", 10)
        y_first = sig("y_first", 3)
        o_squared, o_sums, o_ln, o_inv, o_normed = sig("o_squared"), sig("o_sums"), sig("o_ln"), sig("o_inv"), sig("o_normed")

        block = ctx.enter_context(nc.Block())

        def heads(eng, body):
            body(0, True, False)
            with eng.Fori(1, GDN_H - 1) as h:
                body(h, False, False)
            body(GDN_H - 1, False, True)

        @block.sync
        def _(sp):
            def load_qkv(h):
                sp.dma_start(raw_q[:], qkvT[h, :, CTX:TOK]).then_inc(loaded.sem, 16)
                sp.dma_start(raw_k[:], qkvT[h + GDN_H]).then_inc(loaded.sem, 16)

            def load_v(h):
                sp.dma_start(raw_v[:], qkvT[h + 2 * GDN_H]).then_inc(loaded.sem, 16)

            def load_z(h):
                sp.dma_start(z_in[:], zT[h]).then_inc(z_loaded.sem, 16)

            def next_qkv(h):
                sp.wait_ge(normed.sem, normed.value(h - 1, 2))
                load_qkv(h)
                sp.wait_ge(v_copied.sem, v_copied.value(h - 1, 2))
                load_v(h)

            def store(h):
                sp.wait_ge(y_set.sem, y_set.value(h, 1))
                sp.dma_start(yT[h], y_out[:]).then_inc(stored.sem, 16)

            load_qkv(0)
            load_v(0)
            load_z(0)
            next_qkv(1)
            with sp.Fori(2, GDN_H) as h:
                next_qkv(h)
                store(h - 2)
                load_z(h - 1)
            store(GDN_H - 2)
            load_z(GDN_H - 1)
            store(GDN_H - 1)
            sp.wait_ge(stored.sem, stored.value(GDN_H, 0))

        @block.tensor
        def _(pe):
            def norm_k(h):
                pe.wait_ge(squared.sem, squared.value(h, 1))
                pe.matmul(bank[6][:, :], ones[:], sq_k[:, 0:512], start=True, stop=True).then_inc(sums.sem, 1)
                pe.matmul(bank[7][:, 0:256], ones[:], sq_k[:, 512:TOK], start=True, stop=True).then_inc(sums.sem, 1)

            def norm_q(h):
                pe.wait_ge(squared.sem, squared.value(h, 2))
                pe.wait_ge(inv_norm.sem, inv_norm.value(h, 1))
                pe.matmul(bank[6][:, :], ones[:], sq_q[:], start=True, stop=True).then_inc(sums.sem, 1)

            def finish(h):
                pe.wait_ge(o_squared.sem, o_squared.value(h, 1))
                pe.matmul(bank[7][:, :], ones[:], o_sq[:], start=True, stop=True).then_inc(o_sums.sem, 1)

            norm_k(0)
            norm_q(0)

            def body(h, first, last_head):
                pe.wait_ge(head_done.sem, head_done.value(h, 0))
                pe.wait_ge(inv_norm.sem, inv_norm.value(h, 3))
                pe.wait_ge(loaded.sem, loaded.value(h, 48))
                for c in range(CHUNKS):
                    last = pe.transpose(bank[5 + c // 4][:, (c % 4) * P:(c % 4 + 1) * P],
                                        raw_v[:, c * P:(c + 1) * P], ident[:])
                last.then_inc(v_turned.sem, 1)
                pe.wait_ge(staged.sem, staged.value(h, 2))
                for b, i in enumerate((3, 4, 7)):
                    for c in range(2):
                        for d in range(2):
                            pe.matmul(quad(i)[:, c, d, :], tab[:, 4, 2 * b + c, d:d + 1].to_broadcast([P, P]),
                                      ident[:], start=(c == 0 and d == 0), stop=False)
                    last = pe.matmul(quad(i), ident[:], neg[:].unsqueeze(1).to_broadcast([P, 2, 2, P]),
                                     start=False, stop=True)
                    last.then_inc(dmat.sem, 1)
                for b, i in enumerate((0, 1)):
                    for c in range(2):
                        for d in range(2):
                            last = pe.matmul(quad(i)[:, c, d, :],
                                             tab[:, 4, 2 * b + 2 + c, d:d + 1].to_broadcast([P, P]),
                                             ident[:], start=True, stop=True)
                    last.then_inc(emat.sem, 1)
                pe.wait_ge(normed.sem, normed.value(h, 1))
                pe.wait_ge(v_copied.sem, v_copied.value(h, 2))
                for c in range(CHUNKS):
                    last = pe.transpose(bank[5 + c // 4][:, (c % 4) * P:(c % 4 + 1) * P],
                                        k_n[:, c * P:(c + 1) * P], ident[:])
                last.then_inc(k_turned.sem, 1)
                for c in range(CHUNKS):
                    if c == 4:
                        pe.wait_ge(dec_read.sem, dec_read.value(h, 1))
                    kc = k_n[:, c * P:(c + 1) * P]
                    last = pe.matmul(bank[2 + c // 4][:, (c % 4) * P:(c % 4 + 1) * P], kc, kc, start=True, stop=True)
                    if c in (3, 5):
                        last.then_inc(products.sem, 1)
                pe.wait_ge(dec_read.sem, dec_read.value(h, 2))
                pe.wait_ge(normed.sem, normed.value(h, 2))
                for c in range(CTX_CHUNKS, CHUNKS):
                    j = c - CTX_CHUNKS
                    last = pe.matmul(bank[4][:, j * P:(j + 1) * P], k_n[:, c * P:(c + 1) * P],
                                     q_n[:, j * P:(j + 1) * P], start=True, stop=True)
                last.then_inc(products.sem, 1)
                for b in range(3):
                    pe.wait_ge(first_m.sem, first_m.value(h, b + 1))
                    if b < 2:
                        pe.wait_ge(qdec_set.sem, qdec_set.value(h, b + 1))
                    else:
                        pe.wait_ge(a_set.sem, a_set.value(h, 3))
                    for c in range(2):
                        for d in range(2):
                            last = pe.matmul(quad(b)[:, c, d, :], t1[:, 2 * b + c, d, :], ident[:],
                                             start=True, stop=True)
                    last.then_inc(first_t.sem, 1)
                n = 0
                for lev in range(1, LEVELS):
                    for b in range(3):
                        if lev == 1:
                            pe.wait_ge(first_set.sem, first_set.value(h, b + 1))
                        else:
                            pe.wait_ge(xy_set.sem, xy_set.value(h, n - 3 + b + 1))
                        for c in range(2):
                            for d in range(2):
                                p = 2 * b + c
                                last = pe.matmul(quad(b)[:, c, d, :], a_t[:, p, d, :], x_m[:, p, d, :],
                                                 start=True, stop=True)
                        last.then_inc(t1_ready.sem, 1)
                    for b in range(3):
                        pe.wait_ge(t1_set.sem, t1_set.value(h, n + b + 1))
                        if lev == 1 and b == 0:
                            pe.wait_ge(a_set.sem, a_set.value(h, 3))
                        if lev == 1 and b == 1:
                            pe.wait_ge(attn_set.sem, attn_set.value(h, 2))
                        if lev == 1 and b == 2:
                            pe.wait_ge(k_copied.sem, k_copied.value(h, 2))
                        for c in range(2):
                            for d in range(2):
                                p = 2 * b + c
                                last = pe.matmul(quad(3 + b)[:, c, d, :], t1[:, p, d, :], y_m[:, p, d, :],
                                                 start=True, stop=True)
                                if lev < LEVELS - 1:
                                    last = pe.matmul(quad(b)[:, c, d, :], y_m[:, p, d, :], t1[:, p, d, :],
                                                     start=True, stop=True)
                        last.then_inc(t2_ready.sem, 1)
                    n += 3
                    if lev == 2 and not first:
                        pe.wait_ge(dec_read.sem, dec_read.value(h, 3))
                        finish(h - 1)
                    if lev == 3 and not last_head:
                        pe.wait_ge(dec_read.sem, dec_read.value(h, 3))
                        if not first:
                            pe.wait_ge(o_ln.sem, o_ln.value(h - 1, 1))
                        norm_k(h + 1)
                    if lev == 4 and not last_head:
                        norm_q(h + 1)
                pe.wait_ge(k_scaled.sem, k_scaled.value(h, 1))
                for b in range(3):
                    pe.wait_ge(xy_set.sem, xy_set.value(h, 15 + b + 1))
                    for c in range(2):
                        for d in range(2):
                            p = 2 * b + c
                            last = pe.matmul(quad(b)[:, c, d, :], k_grow[:, p, d, :], y_m[:, p, d, :],
                                             start=True, stop=True)
                    last.then_inc(w_ready.sem, 1)
                if last_head:
                    pe.wait_ge(o_ln.sem, o_ln.value(h - 1, 1))
                else:
                    pe.wait_ge(inv_norm.sem, inv_norm.value(h + 1, 3))
                pe.wait_ge(w_set.sem, w_set.value(h, 3))
                pe.wait_ge(k_scaled.sem, k_scaled.value(h, 2))
                pe.wait_ge(q_decayed.sem, q_decayed.value(h, 1))
                n_o = 0
                for j in range(CHUNKS):
                    for d in range(2):
                        c = ORDER[d][j]
                        if j > 0:
                            pe.wait_ge(s_set.sem, s_set.value(h, 2 * j - 1 + d))
                        mm = pe.matmul(bank[3 + d][:, 0:P], y_m[:, c, d, :], v_tok[:, c, :],
                                       start=True, stop=(j == 0))
                        if j > 0:
                            mm = pe.matmul(bank[3 + d][:, 0:P], w_neg[:, c, d, :], state[:, d, :],
                                           start=False, stop=True)
                        mm.then_inc(v_ready.sem, 1)
                    for d in range(2):
                        c = ORDER[d][j]
                        pe.wait_ge(v_set.sem, v_set.value(h, 2 * j + d + 1))
                        if j < CHUNKS - 1:
                            pe.matmul(bank[7 * (1 - d)][:, 0:P], k_end[:, c, d, :], v_new[:, d, :],
                                      start=True, stop=True).then_inc(s_ready.sem, 1)
                        if c >= CTX_CHUNKS:
                            if n_o >= 2:
                                pe.wait_ge(o_set.sem, o_set.value(h, n_o - 1))
                            pe.matmul(bank[5 + d][:, 0:P], state[:, d, :], qdec[:, c - 2, d, :],
                                      start=True, stop=False)
                            pe.matmul(bank[5 + d][:, 0:P], v_new[:, d, :], attn[:, c - 2, d, :],
                                      start=False, stop=True).then_inc(o_ready.sem, 1)
                            n_o += 1

            heads(pe, body)
            finish(GDN_H - 1)

        @block.scalar
        def _(act):
            act.preload_act_table_set(EXP_LN)
            act.wait_ge(consts_set.sem, 2)
            def norm(h, first):
                act.wait_ge(loaded.sem, loaded.value(h, 48))
                if not first:
                    act.wait_ge(normed.sem, normed.value(h - 1, 2))
                act.activation(sq_k[:], raw_k[:], ACT.Square).then_inc(squared.sem, 1)
                act.activation(sq_q[:], raw_q[:], ACT.Square).then_inc(squared.sem, 1)
                for n, (i, dst) in enumerate(((6, sq_k[:, 0:512]), (7, sq_k[:, 512:TOK]), (6, sq_q[:]))):
                    act.wait_ge(sums.sem, sums.value(h, n + 1))
                    act.activation(dst, bank[i][:, 0:dst.shape[1]], ACT.Ln, bias=eps[:, 0:1]).then_inc(norm_ln.sem, 1)
                    act.wait_ge(norm_ln.sem, norm_ln.value(h, n + 1))
                    bias = ln_scale[:, 0:1] if n == 2 else 0.0
                    act.activation(dst, dst, ACT.Exp, scale=-0.5, bias=bias).then_inc(inv_norm.sem, 1)

            def finish(h):
                act.wait_ge(o_sums.sem, o_sums.value(h, 1))
                act.activation(o_sq[:], bank[7][:, :], ACT.Ln, scale=1.0 / P, bias=eps[:, 0:1]).then_inc(o_ln.sem, 1)
                act.wait_ge(o_ln.sem, o_ln.value(h, 1))
                act.activation(o_sq[:], o_sq[:], ACT.Exp, scale=-0.5).then_inc(o_inv.sem, 1)

            norm(0, True)

            def body(h, first, last_head):
                act.wait_ge(head_done.sem, head_done.value(h, 0))
                act.wait_ge(v_turned.sem, v_turned.value(h, 1))
                act.activation(v_tok[:, 0:4, :], bank[5][:, :].rearrange("p (c q) -> p c q", c=4),
                               ACT.Copy).then_inc(v_copied.sem, 1)
                act.activation(v_tok[:, 4:6, :], bank[6][:, 0:256].rearrange("p (c q) -> p c q", c=2),
                               ACT.Copy).then_inc(v_copied.sem, 1)
                act.wait_ge(staged.sem, staged.value(h, 2))
                for b, i in enumerate((3, 4, 7)):
                    act.wait_ge(dmat.sem, dmat.value(h, b + 1))
                    for c in range(2):
                        for d in range(2):
                            ins = act.activation(dec[:, 2 * b + c, d, :], quad(i)[:, c, d, :], ACT.Exp,
                                                 bias=ncum[:, 2 * b + c, d:d + 1])
                    ins.then_inc(dec_read.sem, 1)
                for b in range(2):
                    act.wait_ge(emat.sem, emat.value(h, b + 1))
                    act.activation(qdec[:, 2 * b:2 * b + 2, :, :], quad(b), ACT.Exp).then_inc(qdec_set.sem, 1)
                act.wait_ge(k_turned.sem, k_turned.value(h, 1))
                act.activation(k_tok[:, 0:4, :], bank[5][:, :].rearrange("p (c q) -> p c q", c=4),
                               ACT.Copy).then_inc(k_copied.sem, 1)
                act.activation(k_tok[:, 4:6, :], bank[6][:, 0:256].rearrange("p (c q) -> p c q", c=2),
                               ACT.Copy).then_inc(k_copied.sem, 1)
                if not first:
                    finish(h - 1)
                if not last_head:
                    norm(h + 1, False)
                for b in range(3):
                    act.wait_ge(w_ready.sem, w_ready.value(h, b + 1))
                    act.activation(w_neg[:, 2 * b:2 * b + 2, :, :], quad(b), ACT.Copy, scale=-1.0).then_inc(w_set.sem, 1)
                n_o = 0
                for j in range(CHUNKS):
                    for d in range(2):
                        c = ORDER[d][j]
                        if c >= CTX_CHUNKS:
                            act.wait_ge(o_ready.sem, o_ready.value(h, n_o + 1))
                            act.activation(o_dir[:, d, (c - 2) * P:(c - 1) * P], bank[5 + d][:, 0:P],
                                           ACT.Copy).then_inc(o_set.sem, 1)
                            n_o += 1

            heads(act, body)
            finish(GDN_H - 1)

        @block.gpsimd
        def _(pool):
            with pool.Fori(0, GDN_H) as h:
                pool.wait_ge(head_done.sem, head_done.value(h, 0))
                pool.wait_ge(staged.sem, staged.value(h, 1))
                pool.wait_ge(normed.sem, normed.value(h, 2))
                pool.wait_ge(qdec_set.sem, qdec_set.value(h, 2))
                pool.tensor_tensor(qdec[:], qdec[:], q_n[:].rearrange("p (c q) -> p c q", c=4).unsqueeze(2)
                                   .to_broadcast([P, 4, 2, P]), ALU.mult).then_inc(q_decayed.sem, 1)
                pool.wait_ge(k_copied.sem, k_copied.value(h, 2))
                k_both = k_tok[:].unsqueeze(2).to_broadcast([P, CHUNKS, 2, P])
                for t, dst in ((1, k_grow), (2, k_end)):
                    pool.tensor_tensor(dst[:], k_both, tab[:, t, :, :].unsqueeze(3).to_broadcast([P, CHUNKS, 2, P]),
                                       ALU.mult).then_inc(k_scaled.sem, 1)

        @block.vector
        def _(dve):
            dve.memset(eps[:], EPS).then_inc(consts_set.sem, 1)
            dve.memset(ln_scale[:], float(-0.5 * np.log(P))).then_inc(consts_set.sem, 1)
            dve.sem_inc(head_done.sem, 1)
            dve.sem_inc(stored.sem, 16)

            def norm_k(h):
                dve.wait_ge(inv_norm.sem, inv_norm.value(h, 2))
                dve.tensor_tensor(k_n[:], raw_k[:], sq_k[:], ALU.mult).then_inc(normed.sem, 1)

            def norm_q(h):
                dve.wait_ge(inv_norm.sem, inv_norm.value(h, 3))
                dve.tensor_tensor(q_n[:], raw_q[:], sq_q[:], ALU.mult).then_inc(normed.sem, 1)

            def finish(h):
                dve.wait_ge(o_inv.sem, o_inv.value(h, 1))
                dve.tensor_tensor(o_sum[:], o_sum[:], o_sq[:], ALU.mult).then_inc(o_normed.sem, 1)
                dve.wait_ge(o_normed.sem, o_normed.value(h, 1))
                dve.wait_ge(z_loaded.sem, z_loaded.value(h, 16))
                dve.wait_ge(stored.sem, stored.value(h, 0))
                dve.scalar_tensor_tensor(y_out[:], o_sum[:], gnorm, z_in[:], ALU.mult, ALU.mult).then_inc(y_set.sem, 1)

            norm_k(0)
            norm_q(0)

            def body(h, first, last_head):
                dve.wait_ge(head_done.sem, head_done.value(h, 0))
                dve.tensor_copy(tab[:].rearrange("p t c d -> p (t c d)"),
                                   tabs[:].rearrange("p t c d h -> p (t c d) h")[:, :, bass.ds(h, 1)]
                                   .rearrange("p x h -> p (x h)")).then_inc(staged.sem, 1)
                dve.wait_ge(staged.sem, staged.value(h, 1))
                dve.tensor_scalar(ncum[:], tab[:, 4, :, :], -1.0, None, ALU.mult).then_inc(staged.sem, 1)
                for c in range(CHUNKS):
                    if c in (0, 4):
                        dve.wait_ge(products.sem, products.value(h, 1 + c // 4))
                    if c % 2 == 0:
                        dve.wait_ge(dec_read.sem, dec_read.value(h, 1 + c // 2))
                    for d in range(2):
                        ins = dve.scalar_tensor_tensor(a_t[:, c, d, :], bank[2 + c // 4][:, (c % 4) * P:(c % 4 + 1) * P],
                                                       tab[:, 0, c, d:d + 1], dec[:, c, d, :], ALU.mult, ALU.mult)
                    if c % 2 == 1:
                        ins.then_inc(a_set.sem, 1)
                dve.wait_ge(products.sem, products.value(h, 3))
                kq = bank[4][:, :].rearrange("p (c q) -> p c q", c=4)
                for b in range(2):
                    dve.tensor_tensor(attn[:, 2 * b:2 * b + 2, :, :],
                                      kq[:, 2 * b:2 * b + 2, :].unsqueeze(2).to_broadcast([P, 2, 2, P]),
                                      dec[:, 2 * b + 2:2 * b + 4, :, :], ALU.mult).then_inc(attn_set.sem, 1)
                corner = pair[:, 0, :, :]
                ident4 = ident[:].unsqueeze(1).unsqueeze(1).to_broadcast([P, 2, 2, P])
                for b in range(3):
                    s = slice(2 * b, 2 * b + 2)
                    dve.wait_ge(a_set.sem, a_set.value(h, b + 1))
                    for d in range(2):
                        ins = dve.tensor_tensor(t1[:, s, d, :], a_t[:, s, d, :],
                                                corner[:, 1 - d, :].unsqueeze(1).to_broadcast([P, 2, P]), ALU.mult)
                    ins.then_inc(first_m.sem, 1)
                for b in range(3):
                    s = slice(2 * b, 2 * b + 2)
                    dve.wait_ge(first_m.sem, first_m.value(h, b + 1))
                    dve.tensor_tensor(y_m[:, s, :, :], ident4, t1[:, s, :, :], ALU.subtract).then_inc(y_first.sem, 1)
                    dve.wait_ge(first_t.sem, first_t.value(h, b + 1))
                    dve.tensor_tensor(x_m[:, s, :, :], ident4, quad(b), ALU.subtract).then_inc(first_set.sem, 1)
                n = 0
                for lev in range(1, LEVELS):
                    for b in range(3):
                        s = slice(2 * b, 2 * b + 2)
                        dve.wait_ge(t1_ready.sem, t1_ready.value(h, n + b + 1))
                        dve.tensor_tensor(t1[:, s, :, :], quad(b),
                                          pair[:, lev, :, :].unsqueeze(1).to_broadcast([P, 2, 2, P]),
                                          ALU.mult).then_inc(t1_set.sem, 1)
                    for b in range(3):
                        s = slice(2 * b, 2 * b + 2)
                        dve.wait_ge(t2_ready.sem, t2_ready.value(h, n + b + 1))
                        ins = dve.tensor_tensor(y_m[:, s, :, :], y_m[:, s, :, :], quad(3 + b), ALU.subtract)
                        if lev < LEVELS - 1:
                            ins = dve.tensor_tensor(x_m[:, s, :, :], x_m[:, s, :, :], quad(b), ALU.subtract)
                        ins.then_inc(xy_set.sem, 1)
                    n += 3
                    if lev == 3 and not first:
                        finish(h - 1)
                    if lev == 4 and not last_head:
                        dve.wait_ge(k_turned.sem, k_turned.value(h, 1))
                        norm_k(h + 1)
                    if lev == 5 and not last_head:
                        dve.wait_ge(q_decayed.sem, q_decayed.value(h, 1))
                        norm_q(h + 1)
                for j in range(CHUNKS):
                    for d in range(2):
                        c = ORDER[d][j]
                        dve.wait_ge(v_ready.sem, v_ready.value(h, 2 * j + d + 1))
                        dve.tensor_scalar(v_new[:, d, :], bank[3 + d][:, 0:P], tab[:, 0, c, d:d + 1], None,
                                          ALU.mult).then_inc(v_set.sem, 1)
                    if j == CHUNKS - 1:
                        break
                    for d in range(2):
                        c = ORDER[d][j]
                        dve.wait_ge(s_ready.sem, s_ready.value(h, 2 * j + d + 1))
                        if c >= CTX_CHUNKS:
                            dve.wait_ge(o_ready.sem, o_ready.value(h, 2 * (j - 2) + d + 1))
                        s_new = bank[7 * (1 - d)][:, 0:P]
                        if j == 0:
                            dve.tensor_copy(state[:, d, :], s_new).then_inc(s_set.sem, 1)
                        else:
                            dve.scalar_tensor_tensor(state[:, d, :], state[:, d, :], tab[:, 3, c, d:d + 1], s_new,
                                                     ALU.mult, ALU.add).then_inc(s_set.sem, 1)
                dve.wait_ge(o_set.sem, o_set.value(h, 8))
                dve.tensor_tensor(o_sum[:], o_dir[:, 0, :], o_dir[:, 1, :], ALU.add).then_inc(head_done.sem, 1)
                dve.wait_ge(head_done.sem, head_done.value(h, 1))
                dve.tensor_tensor(o_sq[:], o_sum[:], o_sum[:], ALU.mult).then_inc(o_squared.sem, 1)

            heads(dve, body)
            finish(GDN_H - 1)


SSD_H = 16
SSD_G = 2
HPG = SSD_H // SSD_G
SSD_P = 64
GW = HPG * SSD_P
GB = GW // P
SSD_TABS = 4


@stage
def ssd_stage(nc, consts, xbcT, tabs, skip, norm_w, zT, yT):
    LC = CHUNKS - CTX_CHUNKS
    ORDER = [list(range(CHUNKS)), [1, 0, 5, 4, 3, 2]]
    EXPO_BANK = [0, 1, 5, 6]
    ident, ones, neg = consts["ident"], consts["ones"], consts["neg"]
    with ExitStack() as ctx:
        def sb(name, *shape):
            return ctx.enter_context(nc.sbuf_tensor("ssd_" + name, [P, *shape], F32))

        def sig(name, per=1, base=0):
            return Sig(nc.alloc_semaphore("ssd_" + name), per, base)

        x_in, b_in, c_in, z_in = sb("x_in", GB, TOK), sb("b_in", TOK), sb("c_in", TOK), sb("z_in", GB, LAT)
        x_tok, b_tok = sb("x_tok", CHUNKS, GW), sb("b_tok", CHUNKS, P)
        cb = sb("cb", LC, P)
        tab, ncum = sb("tab", SSD_TABS, CHUNKS, 2, HPG), sb("ncum", CHUNKS, 2, HPG)
        sk, nw = sb("sk", GB), sb("nw", GB)
        x_w = sb("x_w", 2, GW)
        x_dt = sb("x_dt", LC, 2, GW)
        h_state = sb("h_state", 2, CHUNKS - 1, GW)
        grow, expo = sb("grow", 2, 4, P), sb("expo", 2, 4, P)
        c_grow, dec = sb("c_grow", 2, 4, 4, P), sb("dec", 2, 4, 4, P)
        y_g, y_sq, inv = sb("y_g", GB, LAT), sb("y_sq", GB, LAT), sb("inv", LAT)
        eps = sb("eps", 1)
        bank = [ctx.enter_context(nc.psum_tensor(f"ssd_bank{i}", [P, 512], F32)) for i in range(8)]

        NB = 4 * LC
        group_done = sig("group_done", GB, GB)
        loaded = sig("loaded", 64)
        stored = sig("stored", 16, 16)
        consts_set = sig("consts_set")
        staged = sig("staged", 4)
        turned, copied = sig("turned", CHUNKS + 2), sig("copied", CHUNKS + 2)
        cb_ready, cb_set = sig("cb_ready"), sig("cb_set")
        xw_set, add_ready, h_set = sig("xw_set", 10), sig("add_ready", 10), sig("h_set", 10)
        h_decayed = sig("h_decayed", 8)
        xdt_set = sig("xdt_set", LC)
        cum_ready, grow_set, expo_set = sig("cum_ready", NB), sig("grow_set", NB), sig("expo_set", NB)
        dec_exp, dec_set, cgrow_set = sig("dec_exp", NB), sig("dec_set", NB), sig("cgrow_set", NB)
        y_mms = sig("y_mms", LC)
        y_skip, y_gated, squares = sig("y_skip", LC), sig("y_gated", LC), sig("squares")
        sums, inv_ln, inv_set = sig("sums"), sig("inv_ln"), sig("inv_set")

        block = ctx.enter_context(nc.Block())

        @block.sync
        def _(sp):
            with sp.Fori(0, SSD_G) as g:
                sp.wait_ge(group_done.sem, group_done.value(g, 0))
                sp.dma_start(x_in[:], xbcT[bass.ds(g * GB, GB)].rearrange("b p t -> p b t")).then_inc(loaded.sem, 16)
                sp.dma_start(b_in[:], xbcT[g + 8]).then_inc(loaded.sem, 16)
                sp.dma_start(c_in[:], xbcT[g + 10]).then_inc(loaded.sem, 16)
                sp.dma_start(z_in[:], zT[bass.ds(g * GB, GB)].rearrange("b p t -> p b t")).then_inc(loaded.sem, 16)
                sp.wait_ge(group_done.sem, group_done.value(g, GB))
                sp.dma_start(yT[bass.ds(g * GB, GB)].rearrange("b p t -> p b t"), y_g[:]).then_inc(stored.sem, 16)
            sp.wait_ge(stored.sem, stored.value(SSD_G, 0))

        @block.tensor
        def _(pe):
            with pe.Fori(0, SSD_G) as g:
                pe.wait_ge(group_done.sem, group_done.value(g, 0))
                pe.wait_ge(loaded.sem, loaded.value(g, 64))
                for r in range(CHUNKS + 2):
                    if r >= 4:
                        pe.wait_ge(copied.sem, copied.value(g, r - 3))
                    for i in range(4):
                        if r < CHUNKS:
                            src = x_in[:, i, r * P:(r + 1) * P]
                        elif 4 * (r - CHUNKS) + i < CHUNKS:
                            c = 4 * (r - CHUNKS) + i
                            src = b_in[:, c * P:(c + 1) * P]
                        else:
                            break
                        last = pe.transpose(bank[r % 4][:, i * P:(i + 1) * P], src, ident[:])
                    last.then_inc(turned.sem, 1)
                for c in range(CTX_CHUNKS, CHUNKS):
                    j = c - CTX_CHUNKS
                    last = pe.matmul(bank[4][:, j * P:(j + 1) * P], b_in[:, c * P:(c + 1) * P],
                                     c_in[:, c * P:(c + 1) * P], start=True, stop=True)
                last.then_inc(cb_ready.sem, 1)
                pe.wait_ge(copied.sem, copied.value(g, CHUNKS + 2))
                for j in range(CHUNKS - 1):
                    for d in range(2):
                        pe.wait_ge(xw_set.sem, xw_set.value(g, 2 * j + d + 1))
                        if j > 0:
                            pe.wait_ge(h_set.sem, h_set.value(g, 2 * j + d - 1))
                        pe.matmul(bank[5 + d][:, :], b_tok[:, ORDER[d][j], :], x_w[:, d, :],
                                  start=True, stop=True).then_inc(add_ready.sem, 1)
                pe.wait_ge(staged.sem, staged.value(g, 4))

                def exponents(c):
                    for m in range(4):
                        n = 4 * c + m
                        if c == 0 and m >= 2:
                            pe.wait_ge(h_set.sem, h_set.value(g, 10))
                        if c > 0:
                            pe.wait_ge(expo_set.sem, expo_set.value(g, n - 3))
                        for i in range(4):
                            r = (m % 2) * 4 + i
                            last = pe.matmul(bank[EXPO_BANK[m]][:, i * P:(i + 1) * P],
                                             tab[:, 3, c + CTX_CHUNKS, m // 2, r:r + 1].to_broadcast([P, P]),
                                             ident[:], start=True, stop=True)
                        last.then_inc(cum_ready.sem, 1)

                exponents(0)
                pe.wait_ge(xdt_set.sem, xdt_set.value(g, LC))
                for c in range(LC):
                    if c < LC - 1:
                        exponents(c + 1)
                    if c >= 2:
                        pe.wait_ge(y_skip.sem, y_skip.value(g, c - 1))
                    pe.wait_ge(dec_set.sem, dec_set.value(g, 4 * c + 4))
                    pe.wait_ge(cgrow_set.sem, cgrow_set.value(g, 4 * c + 4))
                    for r in range(HPG):
                        out = bank[2 + c % 2][(r % 2) * SSD_P:(r % 2 + 1) * SSD_P, (r // 2) * P:(r // 2 + 1) * P]
                        cols = slice(r * SSD_P, (r + 1) * SSD_P)
                        for d in range(2):
                            j = ORDER[d].index(c + CTX_CHUNKS)
                            m = 2 * d + r // 4
                            pe.matmul(out, x_dt[:, c, d, cols], dec[:, c % 2, m, r % 4, :],
                                      start=(d == 0), stop=False)
                            last = pe.matmul(out, h_state[:, d, j - 1, cols], c_grow[:, c % 2, m, r % 4, :],
                                             start=False, stop=(d == 1))
                    last.then_inc(y_mms.sem, 1)
                pe.wait_ge(squares.sem, squares.value(g, 1))
                for b in range(GB):
                    last = pe.matmul(bank[7][:, :], ones[:], y_sq[:, b, :], start=(b == 0), stop=(b == GB - 1))
                last.then_inc(sums.sem, 1)

        @block.scalar
        def _(act):
            act.preload_act_table_set(EXP_LN)
            act.wait_ge(consts_set.sem, 1)
            with act.Fori(0, SSD_G) as g:
                act.wait_ge(group_done.sem, group_done.value(g, 0))
                for r in range(CHUNKS + 2):
                    act.wait_ge(turned.sem, turned.value(g, r + 1))
                    if r < CHUNKS:
                        ins = act.activation(x_tok[:, r, :], bank[r % 4][:, :], ACT.Copy)
                    else:
                        lo = 4 * (r - CHUNKS)
                        n = min(4, CHUNKS - lo)
                        ins = act.activation(b_tok[:, lo:lo + n, :].rearrange("p c q -> p (c q)"),
                                             bank[r % 4][:, 0:n * P], ACT.Copy)
                    ins.then_inc(copied.sem, 1)
                act.wait_ge(cb_ready.sem, cb_ready.value(g, 1))
                act.activation(cb[:].rearrange("p c q -> p (c q)"), bank[4][:, :], ACT.Copy).then_inc(cb_set.sem, 1)
                act.wait_ge(staged.sem, staged.value(g, 2))

                def growth(n):
                    act.wait_ge(cum_ready.sem, cum_ready.value(g, n + 1))
                    if n >= 2:
                        act.wait_ge(cgrow_set.sem, cgrow_set.value(g, n - 1))
                    act.activation(grow[:, n % 2].rearrange("p i q -> p (i q)"), bank[EXPO_BANK[n % 4]][:, :],
                                   ACT.Exp).then_inc(grow_set.sem, 1)

                growth(0)
                for n in range(NB):
                    c, m = n // 4, n % 4
                    if n < NB - 1:
                        growth(n + 1)
                    act.wait_ge(expo_set.sem, expo_set.value(g, n + 1))
                    if c >= 2 and m == 0:
                        act.wait_ge(y_mms.sem, y_mms.value(g, c - 1))
                    for i in range(4):
                        r = (m % 2) * 4 + i
                        ins = act.activation(dec[:, c % 2, m, i, :], expo[:, n % 2, i, :], ACT.Exp,
                                             bias=ncum[:, c + CTX_CHUNKS, m // 2, r:r + 1])
                    ins.then_inc(dec_exp.sem, 1)
                act.wait_ge(y_gated.sem, y_gated.value(g, LC))
                act.activation(y_sq[:], y_g[:], ACT.Square).then_inc(squares.sem, 1)
                act.wait_ge(sums.sem, sums.value(g, 1))
                act.activation(inv[:], bank[7][:, :], ACT.Ln, scale=1.0 / GW, bias=eps[:, 0:1]).then_inc(inv_ln.sem, 1)
                act.wait_ge(inv_ln.sem, inv_ln.value(g, 1))
                act.activation(inv[:], inv[:], ACT.Exp, scale=-0.5).then_inc(inv_set.sem, 1)

        @block.gpsimd
        def _(pool):
            with pool.Fori(0, SSD_G) as g:
                pool.wait_ge(group_done.sem, group_done.value(g, 0))
                pool.wait_ge(staged.sem, staged.value(g, 1))
                for j in range(CHUNKS - 1):
                    for d in range(2):
                        c = ORDER[d][j]
                        pool.wait_ge(copied.sem, copied.value(g, c + 1))
                        if j > 0:
                            pool.wait_ge(add_ready.sem, add_ready.value(g, 2 * j + d - 1))
                        pool.tensor_tensor(x_w[:, d, :].rearrange("p (r f) -> p r f", r=HPG),
                                           x_tok[:, c, :].rearrange("p (r f) -> p r f", r=HPG),
                                           tab[:, 1, c, d, :].unsqueeze(2).to_broadcast([P, HPG, SSD_P]),
                                           ALU.mult).then_inc(xw_set.sem, 1)
                for c in range(LC):
                    for d in range(2):
                        ins = pool.tensor_tensor(x_dt[:, c, d, :].rearrange("p (r f) -> p r f", r=HPG),
                                                 x_tok[:, c + CTX_CHUNKS, :].rearrange("p (r f) -> p r f", r=HPG),
                                                 tab[:, 0, c + CTX_CHUNKS, d, :].unsqueeze(2)
                                                 .to_broadcast([P, HPG, SSD_P]), ALU.mult)
                    ins.then_inc(xdt_set.sem, 1)
                for n in range(NB):
                    c, m = n // 4, n % 4
                    pool.wait_ge(grow_set.sem, grow_set.value(g, n + 1))
                    if c >= 2 and m == 0:
                        pool.wait_ge(y_mms.sem, y_mms.value(g, c - 1))
                    pool.tensor_tensor(c_grow[:, c % 2, m, :, :], grow[:, n % 2, :, :],
                                       c_in[:, (c + CTX_CHUNKS) * P:(c + CTX_CHUNKS + 1) * P].unsqueeze(1)
                                       .to_broadcast([P, 4, P]), ALU.mult).then_inc(cgrow_set.sem, 1)

        @block.vector
        def _(dve):
            dve.memset(eps[:], EPS).then_inc(consts_set.sem, 1)
            dve.sem_inc(group_done.sem, GB)
            dve.sem_inc(stored.sem, 16)
            with dve.Fori(0, SSD_G) as g:
                dve.wait_ge(group_done.sem, group_done.value(g, 0))
                heads = bass.ds(g * HPG, HPG)
                dve.tensor_copy(tab[:].rearrange("p t c d r -> p (t c d) r"),
                                tabs[:].rearrange("p t c d r -> p (t c d) r")[:, :, heads]).then_inc(staged.sem, 1)
                dve.wait_ge(staged.sem, staged.value(g, 1))
                dve.tensor_scalar(ncum[:], tab[:, 3, :, :, :], -1.0, None, ALU.mult).then_inc(staged.sem, 1)
                dve.tensor_copy(sk[:], skip[:, bass.ds(g * GB, GB)]).then_inc(staged.sem, 1)
                dve.tensor_copy(nw[:], norm_w[:, bass.ds(g * GB, GB)]).then_inc(staged.sem, 1)
                n_decayed = 0
                for j in range(CHUNKS - 1):
                    for d in range(2):
                        c = ORDER[d][j]
                        if j > 0:
                            dve.wait_ge(h_set.sem, h_set.value(g, 2 * j + d - 1))
                            n_decayed += 1
                            dve.tensor_tensor(h_state[:, d, j, :].rearrange("p (r f) -> p r f", r=HPG),
                                              h_state[:, d, j - 1, :].rearrange("p (r f) -> p r f", r=HPG),
                                              tab[:, 2, c, d, :].unsqueeze(2).to_broadcast([P, HPG, SSD_P]),
                                              ALU.mult).then_inc(h_decayed.sem, 1)
                            dve.wait_ge(h_decayed.sem, h_decayed.value(g, n_decayed))
                        dve.wait_ge(add_ready.sem, add_ready.value(g, 2 * j + d + 1))
                        if j == 0:
                            dve.tensor_copy(h_state[:, d, j, :], bank[5 + d][:, :]).then_inc(h_set.sem, 1)
                        else:
                            dve.tensor_tensor(h_state[:, d, j, :], h_state[:, d, j, :], bank[5 + d][:, :],
                                              ALU.add).then_inc(h_set.sem, 1)
                dve.wait_ge(cb_set.sem, cb_set.value(g, 1))
                dve.wait_ge(stored.sem, stored.value(g, 0))

                def masked(n):
                    d = (n % 4) // 2
                    dve.wait_ge(grow_set.sem, grow_set.value(g, n + 1))
                    if n >= 2:
                        dve.wait_ge(dec_exp.sem, dec_exp.value(g, n - 1))
                    dve.tensor_tensor(expo[:, n % 2, :, :], bank[EXPO_BANK[n % 4]][:, :].rearrange("p (i q) -> p i q", i=4),
                                      neg[:, d, :].unsqueeze(1).to_broadcast([P, 4, P]), ALU.add).then_inc(expo_set.sem, 1)

                def gated(c):
                    cols = slice(c * P, (c + 1) * P)
                    dve.wait_ge(y_mms.sem, y_mms.value(g, c + 1))
                    for b in range(GB):
                        ins = dve.scalar_tensor_tensor(y_g[:, b, cols], x_in[:, b, CTX + c * P:CTX + (c + 1) * P],
                                                       sk[:, b:b + 1], bank[2 + c % 2][:, b * P:(b + 1) * P],
                                                       ALU.mult, ALU.add)
                    ins.then_inc(y_skip.sem, 1)
                    dve.wait_ge(y_skip.sem, y_skip.value(g, c + 1))
                    dve.tensor_tensor(y_g[:, :, cols], y_g[:, :, cols], z_in[:, :, cols], ALU.mult).then_inc(y_gated.sem, 1)

                masked(0)
                for c in range(LC):
                    for m in range(4):
                        n = 4 * c + m
                        if n < NB - 1:
                            masked(n + 1)
                        dve.wait_ge(dec_exp.sem, dec_exp.value(g, n + 1))
                        dve.tensor_tensor(dec[:, c % 2, m, :, :], dec[:, c % 2, m, :, :],
                                          cb[:, c, :].unsqueeze(1).to_broadcast([P, 4, P]), ALU.mult).then_inc(dec_set.sem, 1)
                    if c > 0:
                        gated(c - 1)
                gated(LC - 1)
                dve.wait_ge(inv_set.sem, inv_set.value(g, 1))
                for b in range(GB):
                    dve.scalar_tensor_tensor(y_g[:, b, :], y_g[:, b, :], nw[:, b:b + 1], inv[:],
                                             ALU.mult, ALU.mult).then_inc(group_done.sem, 1)


HG_H = 8
HG_CH = LAT // P
HG_SLOTS = 2
F_FLOOR = float(2.0 ** -63)


class HgrnSlot:

    def __init__(self, nc, ctx, g):
        def sb(name, *shape):
            return ctx.enter_context(nc.sbuf_tensor(f"hg{g}_{name}", [P, *shape], F32))

        def sig(name, per=1, base=0):
            return Sig(nc.alloc_semaphore(f"hg{g}_{name}"), per, base)

        self.q_in, self.s_in, self.n_in, self.z_in = sb("q_in", LAT), sb("s_in", LAT), sb("n_in", LAT), sb("z_in", LAT)
        self.v_tok = sb("v_tok", HG_CH, P)
        self.lb, self.rest, self.nw = sb("lb", 1), sb("rest", 1), sb("nw", 1)
        self.f, self.k, self.cum = sb("f", LAT), sb("k", LAT), sb("cum", LAT)
        self.diff, self.q_arg, self.k_arg = sb("diff", 2, LAT), sb("q_arg", 2, LAT), sb("k_arg", 2, LAT)
        self.q_lev, self.k_lev = sb("q_lev", 2, LAT), sb("k_lev", 2, LAT)
        self.part, self.attn = sb("part", 2, HG_CH, P), sb("attn", HG_CH, P)
        self.q_grow, self.k_end, self.k_end_tok = sb("q_grow", LAT), sb("k_end", LAT), sb("k_end_tok", HG_CH, P)
        self.to_end, self.decay_end = sb("to_end", LAT), sb("decay_end", HG_CH)
        self.state = sb("state", HG_CH - 1, P)
        self.o, self.o_sq, self.y_out = sb("o", LAT), sb("o_sq", LAT), sb("y_out", LAT)
        self.score_banks = [ctx.enter_context(nc.psum_tensor(f"hg{g}_scores{i}", [P, 512], F32)) for i in range(2)]
        self.misc_bank = ctx.enter_context(nc.psum_tensor(f"hg{g}_misc_bank", [P, 512], F32))
        self.o_bank = ctx.enter_context(nc.psum_tensor(f"hg{g}_o_bank", [P, 512], F32))

        self.loaded = sig("loaded", 80)
        self.stored = sig("stored", 16, 16)
        self.head_done = sig("head_done", 1, 1)
        self.staged = sig("staged", 3)
        self.f_set, self.f_ln, self.cum_set, self.k_set = sig("f_set", 2), sig("f_ln"), sig("cum_set"), sig("k_set")
        self.diff_set, self.args_set = sig("diff_set", LEVELS), sig("args_set", LEVELS)
        self.exp_set = sig("exp_set", 2 * LEVELS)
        self.q_lev_set, self.k_lev_set = sig("q_lev_set", LEVELS), sig("k_lev_set", LEVELS)
        self.scores, self.part_set, self.attn_set = sig("scores", LEVELS + 1), sig("part_set", LEVELS + 1), sig("attn_set", LEVELS)
        self.grow_exp, self.grow_set = sig("grow_exp"), sig("grow_set")
        self.end_arg, self.end_exp, self.end_set = sig("end_arg"), sig("end_exp"), sig("end_set")
        self.dec_exp = sig("dec_exp")
        self.turned, self.turned_copied = sig("turned"), sig("turned_copied")
        self.add_ready, self.state_set = sig("add_ready", 3), sig("state_set", 3)
        self.o_ready, self.o_set, self.o_squared = sig("o_ready"), sig("o_set"), sig("o_squared")
        self.sums, self.inv_ln, self.inv_set, self.o_normed = sig("sums"), sig("inv_ln"), sig("inv_set"), sig("o_normed")


@stage
def hgrn_stage(nc, consts, qT, sigT, sig_negT, v_tok_dram, lower, norm_w, zT, yT):
    ident, ones, scan_masks, start = consts["ident"], consts["ones"], consts["scan"], consts["start"]
    with ExitStack() as ctx:
        slots = [HgrnSlot(nc, ctx, g) for g in range(HG_SLOTS)]
        eps = ctx.enter_context(nc.sbuf_tensor("hg_eps", [P, 1], F32))
        consts_set = nc.alloc_semaphore("hg_consts_set")
        ROUNDS = HG_H // HG_SLOTS
        block = ctx.enter_context(nc.Block())

        @block.sync
        def _(sp):
            def load(s, h):
                for src, dst in ((sigT, s.s_in), (sig_negT, s.n_in), (qT, s.q_in), (zT, s.z_in)):
                    sp.dma_start(dst[:], src[h]).then_inc(s.loaded.sem, 16)
                sp.dma_start(s.v_tok[:], v_tok_dram.rearrange("(c p) f -> p c f", p=P)[:, :, bass.ts(h, P)]
                             ).then_inc(s.loaded.sem, 16)

            for g, s in enumerate(slots):
                load(s, g)
            with sp.Fori(1, ROUNDS) as it:
                for g, s in enumerate(slots):
                    sp.wait_ge(s.head_done.sem, s.head_done.value(it, 0))
                    load(s, it * HG_SLOTS + g)
                    sp.dma_start(yT[(it - 1) * HG_SLOTS + g], s.y_out[:]).then_inc(s.stored.sem, 16)
            for g, s in enumerate(slots):
                sp.wait_ge(s.head_done.sem, s.head_done.value(ROUNDS, 0))
                sp.dma_start(yT[HG_H - HG_SLOTS + g], s.y_out[:]).then_inc(s.stored.sem, 16)
            for s in slots:
                sp.wait_ge(s.stored.sem, s.stored.value(ROUNDS, 0))

        @block.tensor
        def _(pe):
            def level(s, it, n):
                lev = (n - 1) % (LEVELS + 1)
                if n == 0:
                    pe.wait_ge(s.head_done.sem, s.head_done.value(it, 0))
                    pe.wait_ge(s.k_set.sem, s.k_set.value(it, 1))
                if n >= 2:
                    pe.wait_ge(s.part_set.sem, s.part_set.value(it, n - 1))
                if n >= 1:
                    pe.wait_ge(s.q_lev_set.sem, s.q_lev_set.value(it, n))
                    pe.wait_ge(s.k_lev_set.sem, s.k_lev_set.value(it, n))
                else:
                    pe.wait_ge(s.loaded.sem, s.loaded.value(it, 80))
                for c in range(HG_CH):
                    cols = slice(c * P, (c + 1) * P)
                    ks = s.k[:, cols] if n == 0 else s.k_lev[:, lev % 2, cols]
                    qs = s.q_in[:, cols] if n == 0 else s.q_lev[:, lev % 2, cols]
                    last = pe.matmul(s.score_banks[n % 2][:, cols], ks, qs, start=True, stop=True)
                last.then_inc(s.scores.sem, 1)
                if n == 1:
                    pe.wait_ge(s.end_set.sem, s.end_set.value(it, 1))
                    for c in range(HG_CH - 1):
                        last = pe.transpose(s.misc_bank[:, c * P:(c + 1) * P], s.k_end[:, c * P:(c + 1) * P], ident[:])
                    last.then_inc(s.turned.sem, 1)
                if n == 3:
                    pe.wait_ge(s.turned_copied.sem, s.turned_copied.value(it, 1))
                    for c in range(HG_CH - 1):
                        last = pe.matmul(s.misc_bank[:, c * P:(c + 1) * P], s.k_end_tok[:, c, :], s.v_tok[:, c, :],
                                         start=True, stop=True)
                    last.then_inc(s.add_ready.sem, 3)

            def outputs(s, it):
                pe.wait_ge(s.grow_set.sem, s.grow_set.value(it, 1))
                pe.wait_ge(s.state_set.sem, s.state_set.value(it, 3))
                pe.wait_ge(s.attn_set.sem, s.attn_set.value(it, LEVELS))
                for c in range(HG_CH):
                    cols = slice(c * P, (c + 1) * P)
                    if c > 0:
                        pe.matmul(s.o_bank[:, cols], s.state[:, c - 1, :], s.q_grow[:, cols], start=True, stop=False)
                    last = pe.matmul(s.o_bank[:, cols], s.v_tok[:, c, :], s.attn[:, c, :], start=(c == 0), stop=True)
                last.then_inc(s.o_ready.sem, 1)

            def norm_sums(s, it):
                pe.wait_ge(s.o_squared.sem, s.o_squared.value(it, 1))
                pe.matmul(s.misc_bank[:, :], ones[:], s.o_sq[:], start=True, stop=True).then_inc(s.sums.sem, 1)

            with pe.Fori(0, ROUNDS) as it:
                for n in range(LEVELS + 1):
                    for s in slots:
                        level(s, it, n)
                for s in slots:
                    outputs(s, it)
                for s in slots:
                    norm_sums(s, it)

        @block.scalar
        def _(act):
            act.preload_act_table_set(EXP_LN)
            act.wait_ge(consts_set, 1)
            with act.Fori(0, ROUNDS) as it:
                for s in slots:
                    act.wait_ge(s.head_done.sem, s.head_done.value(it, 0))
                    act.wait_ge(s.f_set.sem, s.f_set.value(it, 2))
                    act.activation(s.f[:], s.f[:], ACT.Ln).then_inc(s.f_ln.sem, 1)
                for s in slots:
                    act.wait_ge(s.end_arg.sem, s.end_arg.value(it, 1))
                    act.activation(s.to_end[:], s.to_end[:], ACT.Exp).then_inc(s.end_exp.sem, 1)
                    act.activation(s.decay_end[:], s.cum[:].rearrange("p (c t) -> p c t", c=HG_CH)[:, :, P - 1],
                                   ACT.Exp).then_inc(s.dec_exp.sem, 1)
                for lev in range(LEVELS):
                    for s in slots:
                        q_arg, k_arg = s.q_arg[:, lev % 2, :], s.k_arg[:, lev % 2, :]
                        act.wait_ge(s.args_set.sem, s.args_set.value(it, lev + 1))
                        act.activation(q_arg, q_arg, ACT.Exp).then_inc(s.exp_set.sem, 1)
                        act.activation(k_arg, k_arg, ACT.Exp, scale=-1.0).then_inc(s.exp_set.sem, 1)
                        if lev == 0:
                            act.activation(s.q_grow[:], s.cum[:], ACT.Exp).then_inc(s.grow_exp.sem, 1)
                        if lev == 1:
                            act.wait_ge(s.turned.sem, s.turned.value(it, 1))
                            act.activation(s.k_end_tok[:, 0:HG_CH - 1, :].rearrange("p c q -> p (c q)"),
                                           s.misc_bank[:, 0:(HG_CH - 1) * P], ACT.Copy).then_inc(s.turned_copied.sem, 1)
                for s in slots:
                    act.wait_ge(s.o_ready.sem, s.o_ready.value(it, 1))
                    act.activation(s.o_sq[:], s.o_bank[:, :], ACT.Square).then_inc(s.o_squared.sem, 1)
                    act.activation(s.o[:], s.o_bank[:, :], ACT.Copy).then_inc(s.o_set.sem, 1)
                for s in slots:
                    act.wait_ge(s.sums.sem, s.sums.value(it, 1))
                    act.activation(s.o_sq[:], s.misc_bank[:, :], ACT.Ln, scale=1.0 / P, bias=eps[:, 0:1]).then_inc(s.inv_ln.sem, 1)
                for s in slots:
                    act.wait_ge(s.inv_ln.sem, s.inv_ln.value(it, 1))
                    act.activation(s.o_sq[:], s.o_sq[:], ACT.Exp, scale=-0.5).then_inc(s.inv_set.sem, 1)

        @block.gpsimd
        def _(pool):
            def add_level(s, it, lev):
                pool.wait_ge(s.part_set.sem, s.part_set.value(it, lev + 2))
                if lev > 0:
                    pool.wait_ge(s.attn_set.sem, s.attn_set.value(it, lev))
                first = s.part[:, 0] if lev == 0 else s.attn[:]
                pool.tensor_tensor(s.attn[:], first, s.part[:, (lev + 1) % 2], ALU.add).then_inc(s.attn_set.sem, 1)

            with pool.Fori(0, ROUNDS) as it:
                for s in slots:
                    pool.wait_ge(s.head_done.sem, s.head_done.value(it, 0))
                    pool.wait_ge(s.k_set.sem, s.k_set.value(it, 1))
                    pool.wait_ge(s.end_exp.sem, s.end_exp.value(it, 1))
                    pool.tensor_tensor(s.k_end[:], s.k[:], s.to_end[:], ALU.mult).then_inc(s.end_set.sem, 1)
                for lev in range(LEVELS):
                    for s in slots:
                        pool.wait_ge(s.exp_set.sem, s.exp_set.value(it, 2 * lev + 2))
                        if lev >= 2:
                            pool.wait_ge(s.scores.sem, s.scores.value(it, lev))
                        pool.tensor_tensor(s.k_lev[:, lev % 2, :], s.k[:], s.k_arg[:, lev % 2, :],
                                           ALU.mult).then_inc(s.k_lev_set.sem, 1)
                        if lev == 0:
                            pool.wait_ge(s.grow_exp.sem, s.grow_exp.value(it, 1))
                            pool.tensor_tensor(s.q_grow[:], s.q_grow[:], s.q_in[:], ALU.mult).then_inc(s.grow_set.sem, 1)
                    if lev > 0:
                        for s in slots:
                            add_level(s, it, lev - 1)
                for s in slots:
                    add_level(s, it, LEVELS - 1)

        @block.vector
        def _(dve):
            dve.memset(eps[:], EPS).then_inc(consts_set, 1)
            for s in slots:
                dve.sem_inc(s.head_done.sem, 1)
                dve.sem_inc(s.stored.sem, 16)

            def exponents(s, it, lev):
                half = 1 << lev
                blocks = s.cum[:].rearrange("p (b t) -> p b t", t=2 * half)
                if lev >= 2:
                    dve.wait_ge(s.k_lev_set.sem, s.k_lev_set.value(it, lev - 1))
                    dve.wait_ge(s.q_lev_set.sem, s.q_lev_set.value(it, lev - 1))
                dve.tensor_tensor(s.diff[:, lev % 2, :].rearrange("p (b t) -> p b t", t=2 * half), blocks,
                                  blocks[:, :, half - 1:half].to_broadcast([P, LAT // (2 * half), 2 * half]),
                                  ALU.subtract).then_inc(s.diff_set.sem, 1)
                dve.wait_ge(s.diff_set.sem, s.diff_set.value(it, lev + 1))
                dve.tensor_scalar(s.q_arg[:, lev % 2, :], s.diff[:, lev % 2, :], 0.0, None, ALU.min)
                dve.tensor_scalar(s.k_arg[:, lev % 2, :], s.diff[:, lev % 2, :], 0.0, None, ALU.max).then_inc(s.args_set.sem, 1)

            def masked(s, it, n):
                lev = (n - 1) % (LEVELS + 1)
                dve.wait_ge(s.scores.sem, s.scores.value(it, n + 1))
                if n >= 2:
                    dve.wait_ge(s.attn_set.sem, s.attn_set.value(it, max(1, n - 2)))
                dve.tensor_tensor(s.part[:, n % 2], s.score_banks[n % 2][:, :].rearrange("p (c t) -> p c t", c=HG_CH),
                                  scan_masks[:, lev, :].unsqueeze(1).to_broadcast([P, HG_CH, P]),
                                  ALU.mult).then_inc(s.part_set.sem, 1)

            with dve.Fori(0, ROUNDS) as it:
                for g, s in enumerate(slots):
                    h = it * HG_SLOTS + g
                    dve.wait_ge(s.head_done.sem, s.head_done.value(it, 0))
                    dve.tensor_copy(s.lb[:], lower[:, bass.ds(h, 1)]).then_inc(s.staged.sem, 1)
                    dve.tensor_copy(s.nw[:], norm_w[:, bass.ds(h, 1)]).then_inc(s.staged.sem, 1)
                for s in slots:
                    dve.wait_ge(s.staged.sem, s.staged.value(it, 2))
                    dve.tensor_scalar(s.rest[:], s.lb[:], -1.0, 1.0, ALU.mult, ALU.add).then_inc(s.staged.sem, 1)
                for s in slots:
                    dve.wait_ge(s.staged.sem, s.staged.value(it, 3))
                    dve.wait_ge(s.loaded.sem, s.loaded.value(it, 80))
                    dve.tensor_scalar(s.f[:], s.s_in[:], s.rest[:, 0:1], s.lb[:, 0:1], ALU.mult, ALU.add).then_inc(s.f_set.sem, 1)
                    dve.tensor_scalar(s.k[:], s.n_in[:], s.rest[:, 0:1], None, ALU.mult).then_inc(s.k_set.sem, 1)
                    dve.wait_ge(s.f_set.sem, s.f_set.value(it, 1))
                    dve.tensor_scalar(s.f[:], s.f[:], F_FLOOR, None, ALU.max).then_inc(s.f_set.sem, 1)
                for s in slots:
                    dve.wait_ge(s.f_ln.sem, s.f_ln.value(it, 1))
                    dve.tensor_tensor_scan(s.cum[:], start[:], s.f[:], 0.0, ALU.mult, ALU.add).then_inc(s.cum_set.sem, 1)
                for s in slots:
                    dve.wait_ge(s.cum_set.sem, s.cum_set.value(it, 1))
                    chunks = s.cum[:].rearrange("p (c t) -> p c t", c=HG_CH)
                    dve.tensor_tensor(s.to_end[:].rearrange("p (c t) -> p c t", c=HG_CH),
                                      chunks[:, :, P - 1:P].to_broadcast([P, HG_CH, P]), chunks,
                                      ALU.subtract).then_inc(s.end_arg.sem, 1)
                for s in slots:
                    exponents(s, it, 0)
                for lev in range(LEVELS):
                    if lev < LEVELS - 1:
                        for s in slots:
                            exponents(s, it, lev + 1)
                    for s in slots:
                        dve.wait_ge(s.exp_set.sem, s.exp_set.value(it, 2 * lev + 1))
                        if lev >= 2:
                            dve.wait_ge(s.scores.sem, s.scores.value(it, lev))
                        dve.tensor_tensor(s.q_lev[:, lev % 2, :], s.q_in[:], s.q_arg[:, lev % 2, :],
                                          ALU.mult).then_inc(s.q_lev_set.sem, 1)
                    for s in slots:
                        masked(s, it, lev)
                    if 3 <= lev < 6:
                        c = lev - 3
                        for s in slots:
                            dve.wait_ge(s.add_ready.sem, s.add_ready.value(it, 3))
                            if c == 0:
                                dve.wait_ge(s.dec_exp.sem, s.dec_exp.value(it, 1))
                                dve.tensor_copy(s.state[:, 0, :], s.misc_bank[:, 0:P]).then_inc(s.state_set.sem, 1)
                            else:
                                dve.wait_ge(s.state_set.sem, s.state_set.value(it, c))
                                dve.scalar_tensor_tensor(s.state[:, c, :], s.state[:, c - 1, :], s.decay_end[:, c:c + 1],
                                                         s.misc_bank[:, c * P:(c + 1) * P], ALU.mult, ALU.add
                                                         ).then_inc(s.state_set.sem, 1)
                for s in slots:
                    masked(s, it, LEVELS)
                for s in slots:
                    dve.wait_ge(s.o_set.sem, s.o_set.value(it, 1))
                    dve.wait_ge(s.inv_set.sem, s.inv_set.value(it, 1))
                    dve.tensor_tensor(s.o[:], s.o[:], s.o_sq[:], ALU.mult).then_inc(s.o_normed.sem, 1)
                for s in slots:
                    dve.wait_ge(s.o_normed.sem, s.o_normed.value(it, 1))
                    dve.wait_ge(s.stored.sem, s.stored.value(it, 0))
                    dve.scalar_tensor_tensor(s.y_out[:], s.o[:], s.nw[:, 0:1], s.z_in[:], ALU.mult,
                                             ALU.mult).then_inc(s.head_done.sem, 1)


ML_H = 8
ML_CH = LAT // P
ML_E = 2
ML_TABS = 8


@stage
def mlstm_gates_stage(nc, consts, ig, fg, bias_i, bias_f, tabs):
    ident, start, last_row = consts["ident"], consts["start"], consts["last"]
    LN_SCALE = float(-0.5 * np.log(P))
    with ExitStack() as ctx:
        def sb(name, *shape):
            return ctx.enter_context(nc.sbuf_tensor("mg_" + name, list(shape), F32))

        def sem(name):
            return nc.alloc_semaphore("mg_" + name)

        li, x, e, lf = sb("li", 8, LAT), sb("x", 8, LAT), sb("e", 8, LAT), sb("lf", 8, LAT)
        cum, m = sb("cum", 8, LAT), sb("m", 8, LAT)
        rows = sb("rows", 8, 3, LAT)
        turned = ctx.enter_context(nc.psum_tensor("mg_turned", [P, 3, ML_CH, 8], F32))
        ends = ctx.enter_context(nc.psum_tensor("mg_ends", [P, 3, ML_CH, 8], F32))
        dve_n, act_n = sem("dve_n"), sem("act_n")
        rows_set, turned_set, cols_set, ends_set = sem("rows_set"), sem("turned_set"), sem("cols_set"), sem("ends_set")
        block = ctx.enter_context(nc.Block())

        @block.vector
        def _(dve):
            done = [0]

            def link(ins):
                done[0] += 1
                ins.then_inc(dve_n, 1)
                dve.wait_ge(dve_n, done[0])

            link(dve.tensor_scalar(li[:], ig, bias_i, None, ALU.add))
            link(dve.tensor_scalar(x[:], fg, bias_f, None, ALU.add))
            dve.wait_ge(act_n, 3)
            link(dve.tensor_scalar(x[:], x[:], 0.0, None, ALU.min))
            link(dve.tensor_tensor(lf[:], x[:], e[:], ALU.subtract))
            link(dve.tensor_tensor_scan(cum[:], start[0:8, :], lf[:], 0.0, ALU.mult, ALU.add))
            link(dve.tensor_tensor_scan(m[:], lf[:], li[:], 0.0, ALU.add, ALU.max))
            link(dve.tensor_tensor(rows[:, 0, :], cum[:], m[:], ALU.subtract))
            link(dve.tensor_tensor(rows[:, 1, :], li[:], cum[:], ALU.subtract))
            dve.tensor_copy(rows[:, 2, :], m[:]).then_inc(rows_set, 1)
            dve.wait_ge(turned_set, 1)
            dve.tensor_copy(tabs[:, 0:3, :, :], turned[:]).then_inc(cols_set, 1)
            dve.wait_ge(cols_set, 1)
            dve.wait_ge(ends_set, 1)
            link(dve.memset(tabs[:, 3, 0, :], 0.0))
            link(dve.tensor_copy(tabs[:, 3, 1:ML_CH, :], ends[:, 2, 0:ML_CH - 1, :]))
            link(dve.tensor_tensor(tabs[:, 4, :, :], tabs[:, 1, :, :], ends[:, 0, :, :], ALU.add))
            link(dve.tensor_tensor(tabs[:, 5, :, :], tabs[:, 3, :, :], ends[:, 0, :, :], ALU.add))
            link(dve.tensor_scalar(tabs[:, 6, :, :], tabs[:, 1, :, :], LN_SCALE, None, ALU.add))
            link(dve.tensor_scalar(tabs[:, 7, :, :], tabs[:, 3, :, :], LN_SCALE, None, ALU.add))

        @block.scalar
        def _(act):
            act.preload_act_table_set(EXP_LN)
            act.wait_ge(dve_n, 2)
            act.activation(e[:], x[:], ACT.Abs).then_inc(act_n, 1)
            act.wait_ge(act_n, 1)
            act.activation(e[:], e[:], ACT.Exp, scale=-1.0).then_inc(act_n, 1)
            act.wait_ge(act_n, 2)
            act.activation(e[:], e[:], ACT.Ln, bias=1.0).then_inc(act_n, 1)
            act.wait_ge(dve_n, 14)
            act.activation(tabs[:, 4:6, :, :], tabs[:, 4:6, :, :], ACT.Exp).then_inc(act_n, 1)

        @block.tensor
        def _(pe):
            pe.wait_ge(rows_set, 1)
            for t in range(3):
                for c in range(ML_CH):
                    last = pe.transpose(turned[:, t, c, :], rows[:, t, c * P:(c + 1) * P], ident[0:8, 0:8])
            last.then_inc(turned_set, 1)
            pe.wait_ge(cols_set, 1)
            pe.matmul(ends[:], last_row[:], tabs[:, 0:3, :, :], start=True, stop=True).then_inc(ends_set, 1)


ML_SLOTS = 2
ML_SW = (ML_E + 1) * P


class MlstmSlot:

    def __init__(self, nc, ctx, g):
        SW = ML_SW

        def sb(name, *shape):
            return ctx.enter_context(nc.sbuf_tensor(f"ml{g}_{name}", [P, *shape], F32))

        def sig(name, per=1, base=0):
            return Sig(nc.alloc_semaphore(f"ml{g}_{name}"), per, base)

        self.bank = [ctx.enter_context(nc.psum_tensor(f"ml{g}_bank{i}", [P, 512], F32)) for i in range(4)]
        self.q_in, self.k_in, self.v_tok = sb("q_in", LAT), sb("k_in", LAT), sb("v_tok", ML_CH, ML_E * P)
        self.og_in, self.z_in, self.gate = sb("og_in", ML_E, LAT), sb("z_in", ML_E, LAT), sb("gate", ML_E, LAT)
        self.tab, self.nw = sb("tab", ML_TABS, ML_CH), sb("nw", ML_E)
        self.grow, self.expo, self.w, self.floor = sb("grow", ML_CH, P), sb("expo", ML_CH, P), sb("w", ML_CH, P), sb("floor", LAT)
        self.q_grow, self.score = sb("q_grow", LAT), sb("score", ML_CH, P)
        self.k_w, self.state = sb("k_w", ML_CH, P), sb("state", ML_CH - 1, SW)
        self.den, self.o, self.o_sq, self.inv, self.y_out = sb("den", LAT), sb("o", ML_E, LAT), sb("o_sq", ML_E, LAT), sb("inv", LAT), sb("y_out", ML_E, LAT)

        self.loaded = sig("loaded", 80)
        self.stored, self.head_done = sig("stored", 16, 16), sig("head_done", 1, 1)
        self.staged = sig("staged", 2)
        self.cum_ready, self.m_ready, self.kq_ready, self.k_turned = sig("cum_ready"), sig("m_ready"), sig("kq_ready"), sig("k_turned")
        self.grow_set, self.floor_set, self.expo_set, self.w_set = sig("grow_set"), sig("floor_set"), sig("expo_set"), sig("w_set")
        self.q_grown, self.gate_set = sig("q_grown"), sig("gate_set")
        self.score_set, self.k_w_set = sig("score_set"), sig("k_w_set")
        self.add_ready, self.state_set = sig("add_ready", 3), sig("state_set", 3)
        self.num_ready, self.den_ready = sig("num_ready", ML_E), sig("den_ready")
        self.den_abs, self.den_max, self.den_inv = sig("den_abs"), sig("den_max"), sig("den_inv")
        self.o_set, self.o_squared, self.sums = sig("o_set", ML_E), sig("o_squared"), sig("sums")
        self.inv_ln, self.inv_set, self.y_normed = sig("inv_ln"), sig("inv_set"), sig("y_normed")


@stage
def mlstm_stage(nc, consts, qkT, v_tok_dram, tabs, norm_w, ogT, zT, yT):
    ident, ones, neg = consts["ident"], consts["ones"], consts["neg"]
    with ExitStack() as ctx:
        slots = [MlstmSlot(nc, ctx, g) for g in range(ML_SLOTS)]
        eps = ctx.enter_context(nc.sbuf_tensor("ml_eps", [P, 1], F32))
        consts_set = nc.alloc_semaphore("ml_consts_set")
        ROUNDS = ML_H // ML_SLOTS
        ADD_BANK = (3, 0, 1)
        block = ctx.enter_context(nc.Block())

        @block.sync
        def _(sp):
            def load(s, h):
                pair_of = bass.ds(h * ML_E, ML_E)
                for dst, src in ((s.k_in[:], qkT[h + ML_H]), (s.q_in[:], qkT[h]),
                                 (s.v_tok[:], v_tok_dram.rearrange("(c p) f -> p c f", p=P)[:, :, bass.ts(h, ML_E * P)]),
                                 (s.og_in[:], ogT[pair_of].rearrange("b p t -> p b t")),
                                 (s.z_in[:], zT[pair_of].rearrange("b p t -> p b t"))):
                    sp.dma_start(dst, src).then_inc(s.loaded.sem, 16)

            def store(s, h):
                sp.dma_start(yT[bass.ds(h * ML_E, ML_E)].rearrange("b p t -> p b t"), s.y_out[:]).then_inc(s.stored.sem, 16)

            for g, s in enumerate(slots):
                load(s, g)
            with sp.Fori(1, ROUNDS) as it:
                for g, s in enumerate(slots):
                    sp.wait_ge(s.head_done.sem, s.head_done.value(it, 0))
                    load(s, it * ML_SLOTS + g)
                    store(s, (it - 1) * ML_SLOTS + g)
            for g, s in enumerate(slots):
                sp.wait_ge(s.head_done.sem, s.head_done.value(ROUNDS, 0))
                store(s, ML_H - ML_SLOTS + g)
            for s in slots:
                sp.wait_ge(s.stored.sem, s.stored.value(ROUNDS, 0))

        @block.tensor
        def _(pe):
            with pe.Fori(0, ROUNDS) as it:
                for s in slots:
                    pe.wait_ge(s.head_done.sem, s.head_done.value(it, 0))
                    pe.wait_ge(s.staged.sem, s.staged.value(it, 2))
                    for i, t, ready in ((0, 0, s.cum_ready), (1, 2, s.m_ready)):
                        for c in range(ML_CH):
                            last = pe.matmul(s.bank[i][:, c * P:(c + 1) * P], s.tab[:, t, c:c + 1].to_broadcast([P, P]),
                                             ident[:], start=True, stop=True)
                        last.then_inc(ready.sem, 1)
                for s in slots:
                    pe.wait_ge(s.loaded.sem, s.loaded.value(it, 80))
                    for c in range(ML_CH):
                        last = pe.transpose(s.bank[3][:, c * P:(c + 1) * P], s.k_in[:, c * P:(c + 1) * P], ident[:])
                    last.then_inc(s.k_turned.sem, 1)
                    for c in range(ML_CH):
                        cols = slice(c * P, (c + 1) * P)
                        last = pe.matmul(s.bank[2][:, cols], s.k_in[:, cols], s.q_in[:, cols], start=True, stop=True)
                    last.then_inc(s.kq_ready.sem, 1)
                for s in slots:
                    pe.wait_ge(s.k_w_set.sem, s.k_w_set.value(it, 1))
                    pe.wait_ge(s.expo_set.sem, s.expo_set.value(it, 1))
                    pe.wait_ge(s.floor_set.sem, s.floor_set.value(it, 1))
                    for c, i in enumerate(ADD_BANK):
                        pe.matmul(s.bank[i][:, 0:ML_E * P], s.k_w[:, c, :], s.v_tok[:, c, :], start=True, stop=True)
                        pe.matmul(s.bank[i][:, ML_E * P:ML_SW], s.k_w[:, c, :], ones[:], start=True, stop=True
                                  ).then_inc(s.add_ready.sem, 1)
                for s in slots:
                    pe.wait_ge(s.score_set.sem, s.score_set.value(it, 1))
                    pe.wait_ge(s.q_grown.sem, s.q_grown.value(it, 1))
                    pe.wait_ge(s.state_set.sem, s.state_set.value(it, 3))
                    for i, e, ready in ((2, ML_E, s.den_ready), (3, 0, s.num_ready), (0, 1, s.num_ready)):
                        for c in range(ML_CH):
                            cols = slice(c * P, (c + 1) * P)
                            if c > 0:
                                pe.matmul(s.bank[i][:, cols], s.state[:, c - 1, e * P:(e + 1) * P], s.q_grow[:, cols],
                                          start=True, stop=False)
                            values = ones[:] if e == ML_E else s.v_tok[:, c, e * P:(e + 1) * P]
                            last = pe.matmul(s.bank[i][:, cols], values, s.score[:, c, :], start=(c == 0), stop=True)
                        last.then_inc(ready.sem, 1)
                for s in slots:
                    pe.wait_ge(s.o_squared.sem, s.o_squared.value(it, 1))
                    for e in range(ML_E):
                        last = pe.matmul(s.bank[1][:, :], ones[:], s.o_sq[:, e, :], start=(e == 0), stop=(e == ML_E - 1))
                    last.then_inc(s.sums.sem, 1)

        @block.scalar
        def _(act):
            act.preload_act_table_set(EXP_LN)
            act.wait_ge(consts_set, 1)
            with act.Fori(0, ROUNDS) as it:
                for s in slots:
                    act.wait_ge(s.head_done.sem, s.head_done.value(it, 0))
                    act.wait_ge(s.cum_ready.sem, s.cum_ready.value(it, 1))
                    for c in range(ML_CH):
                        ins = act.activation(s.grow[:, c, :], s.bank[0][:, c * P:(c + 1) * P], ACT.Exp, bias=s.tab[:, 7, c:c + 1])
                    ins.then_inc(s.grow_set.sem, 1)
                    act.wait_ge(s.m_ready.sem, s.m_ready.value(it, 1))
                    act.activation(s.floor[:], s.bank[1][:, :], ACT.Exp, scale=-1.0).then_inc(s.floor_set.sem, 1)
                for s in slots:
                    act.wait_ge(s.expo_set.sem, s.expo_set.value(it, 1))
                    for c in range(ML_CH):
                        ins = act.activation(s.w[:, c, :], s.expo[:, c, :], ACT.Exp, bias=s.tab[:, 6, c:c + 1])
                    ins.then_inc(s.w_set.sem, 1)
                for s in slots:
                    act.wait_ge(s.den_ready.sem, s.den_ready.value(it, 1))
                    act.activation(s.den[:], s.bank[2][:, :], ACT.Abs).then_inc(s.den_abs.sem, 1)
                for s in slots:
                    act.wait_ge(s.o_set.sem, s.o_set.value(it, ML_E))
                    act.activation(s.o_sq[:], s.o[:], ACT.Square).then_inc(s.o_squared.sem, 1)
                for s in slots:
                    act.wait_ge(s.sums.sem, s.sums.value(it, 1))
                    act.activation(s.inv[:], s.bank[1][:, :], ACT.Ln, scale=1.0 / (ML_E * P), bias=eps[:, 0:1]).then_inc(s.inv_ln.sem, 1)
                for s in slots:
                    act.wait_ge(s.inv_ln.sem, s.inv_ln.value(it, 1))
                    act.activation(s.inv[:], s.inv[:], ACT.Exp, scale=-0.5).then_inc(s.inv_set.sem, 1)

        @block.gpsimd
        def _(pool):
            with pool.Fori(0, ROUNDS) as it:
                for s in slots:
                    pool.wait_ge(s.loaded.sem, s.loaded.value(it, 80))
                    pool.wait_ge(s.grow_set.sem, s.grow_set.value(it, 1))
                    pool.tensor_tensor(s.q_grow[:], s.q_in[:], s.grow[:].rearrange("p c t -> p (c t)"), ALU.mult).then_inc(s.q_grown.sem, 1)
                for s in slots:
                    pool.tensor_tensor(s.gate[:], s.og_in[:], s.z_in[:], ALU.mult).then_inc(s.gate_set.sem, 1)

        @block.vector
        def _(dve):
            dve.memset(eps[:], EPS).then_inc(consts_set, 1)
            for s in slots:
                dve.sem_inc(s.head_done.sem, 1)
                dve.sem_inc(s.stored.sem, 16)
            with dve.Fori(0, ROUNDS) as it:
                for g, s in enumerate(slots):
                    h = it * ML_SLOTS + g
                    dve.wait_ge(s.head_done.sem, s.head_done.value(it, 0))
                    dve.tensor_copy(s.tab[:].rearrange("p t c -> p (t c)"),
                                    tabs[:].rearrange("p t c h -> p (t c) h")[:, :, bass.ds(h, 1)]
                                    .rearrange("p x h -> p (x h)")).then_inc(s.staged.sem, 1)
                    dve.tensor_copy(s.nw[:], norm_w[:, bass.ds(h * ML_E, ML_E)]).then_inc(s.staged.sem, 1)
                for s in slots:
                    dve.wait_ge(s.staged.sem, s.staged.value(it, 2))
                    dve.wait_ge(s.grow_set.sem, s.grow_set.value(it, 1))
                    dve.tensor_tensor(s.expo[:], s.bank[0][:, :].rearrange("p (c t) -> p c t", c=ML_CH),
                                      neg[:, 0, :].unsqueeze(1).to_broadcast([P, ML_CH, P]), ALU.add).then_inc(s.expo_set.sem, 1)
                    dve.wait_ge(s.k_turned.sem, s.k_turned.value(it, 1))
                    dve.tensor_tensor(s.k_w[:], s.bank[3][:, :].rearrange("p (c t) -> p c t", c=ML_CH),
                                      s.tab[:, 4, :].unsqueeze(2).to_broadcast([P, ML_CH, P]), ALU.mult).then_inc(s.k_w_set.sem, 1)
                for s in slots:
                    dve.wait_ge(s.kq_ready.sem, s.kq_ready.value(it, 1))
                    dve.wait_ge(s.w_set.sem, s.w_set.value(it, 1))
                    dve.tensor_tensor(s.score[:], s.bank[2][:, :].rearrange("p (c t) -> p c t", c=ML_CH), s.w[:],
                                      ALU.mult).then_inc(s.score_set.sem, 1)
                for c, i in enumerate(ADD_BANK):
                    for s in slots:
                        dve.wait_ge(s.add_ready.sem, s.add_ready.value(it, c + 1))
                        if c == 0:
                            ins = dve.tensor_copy(s.state[:, 0, :], s.bank[i][:, 0:ML_SW])
                        else:
                            dve.wait_ge(s.state_set.sem, s.state_set.value(it, c))
                            ins = dve.scalar_tensor_tensor(s.state[:, c, :], s.state[:, c - 1, :], s.tab[:, 5, c:c + 1],
                                                           s.bank[i][:, 0:ML_SW], ALU.mult, ALU.add)
                        ins.then_inc(s.state_set.sem, 1)
                for s in slots:
                    dve.wait_ge(s.den_abs.sem, s.den_abs.value(it, 1))
                    dve.tensor_tensor(s.den[:], s.den[:], s.floor[:], ALU.max).then_inc(s.den_max.sem, 1)
                    dve.wait_ge(s.den_max.sem, s.den_max.value(it, 1))
                    dve.reciprocal(s.den[:], s.den[:]).then_inc(s.den_inv.sem, 1)
                for s in slots:
                    dve.wait_ge(s.den_inv.sem, s.den_inv.value(it, 1))
                    for e, i in ((0, 3), (1, 0)):
                        dve.wait_ge(s.num_ready.sem, s.num_ready.value(it, e + 1))
                        dve.tensor_tensor(s.o[:, e, :], s.bank[i][:, :], s.den[:], ALU.mult).then_inc(s.o_set.sem, 1)
                for s in slots:
                    dve.wait_ge(s.inv_set.sem, s.inv_set.value(it, 1))
                    dve.wait_ge(s.stored.sem, s.stored.value(it, 0))
                    for e in range(ML_E):
                        ins = dve.scalar_tensor_tensor(s.y_out[:, e, :], s.o[:, e, :], s.nw[:, e:e + 1], s.inv[:], ALU.mult, ALU.mult)
                    ins.then_inc(s.y_normed.sem, 1)
                for s in slots:
                    dve.wait_ge(s.y_normed.sem, s.y_normed.value(it, 1))
                    dve.wait_ge(s.gate_set.sem, s.gate_set.value(it, 1))
                    dve.tensor_tensor(s.y_out[:], s.y_out[:], s.gate[:], ALU.mult).then_inc(s.head_done.sem, 1)


ROWS = [
    [("b_ada", 48), ("pre_norm_w", 16), ("post_norm_w", 16), ("conv_ssd_b", 12), ("ssd_norm_w", 8), ("gdn_norm_w", 1)],
    [("conv_ssd_w", 60), ("c_conv_w_2", 64)],
    [("conv_gdn_w", 120)],
    [("e_norm_2", 16), ("o_norm_2", 16), ("final_norm_2", 16), ("ple_norm_2", 32), ("a_norm_2", 8), ("c_norm_2", 16),
     ("b_conv_b_2", 8), ("b_b_r_2", 8), ("b_b_i_2", 8)],
    [("b_conv_w_2", 32), ("b_lambda_2", 8), ("a_lb_logits_2", 16), ("c_conv_b_2", 16)],
]
CONSTS = {"ident": (P,), "ones": (P,), "causal": (2, P), "neg": (2, P), "pair": (LEVELS, 2, P),
          "scan": (LEVELS + 1, P), "start": (LAT,), "last": (P,)}
Z_BLOCKS = D // P
XBC_BLOCKS, QKV_BLOCKS = 12, 24
OFF_XBC, OFF_DT = D, D + XBC_BLOCKS * P
OFF_QKV = OFF_DT + 2 * SSD_H
OFF_BETA = OFF_QKV + QKV_BLOCKS * P
GATES = 2 * SSD_H + 4 * GDN_H


def flat(ap):
    names = "abcdef"[:len(ap.shape) - 1]
    return ap if len(names) == 1 else ap.rearrange(f"p {' '.join(names)} -> p ({' '.join(names)})")


def columns(cols, name, lo=0, n=None):
    for t, tile in enumerate(ROWS):
        at = 0
        for key, rows in tile:
            if key == name:
                return cols[:, t, at + lo:at + (rows if n is None else lo + n)]
            at += rows
    raise KeyError(name)


@stage
def setup_stage(nc, a, consts, cols):
    with ExitStack() as ctx:
        def sem(name):
            return nc.alloc_semaphore("set_" + name)

        rows = ctx.enter_context(nc.sbuf_tensor("set_rows", [P, len(ROWS), P], F32))
        cols_p = [ctx.enter_context(nc.psum_tensor(f"set_cols{i}", [P, P], F32)) for i in range(2)]
        ident_in, others_in, rows_in = sem("ident_in"), sem("others_in"), sem("rows_in")
        cleared, cols_ready, cols_set = sem("cleared"), sem("cols_ready"), sem("cols_set")
        n_rows = sum(len(t) for t in ROWS)
        block = ctx.enter_context(nc.Block())

        @block.sync
        def _(sp):
            sp.dma_start(consts["ident"][:], a["c_ident"]).then_inc(ident_in, 16)
            for key in CONSTS:
                if key != "ident":
                    sp.dma_start(flat(consts[key][:]), a["c_" + key]).then_inc(others_in, 16)
            sp.wait_ge(others_in, 16 * (len(CONSTS) - 1))

        @block.tensor
        def _(pe):
            pe.wait_ge(ident_in, 16)
            pe.wait_ge(rows_in, 16 * n_rows)
            for t in range(len(ROWS)):
                if t >= 2:
                    pe.wait_ge(cols_set, t - 1)
                pe.transpose(cols_p[t % 2][:], rows[:, t, :], consts["ident"][:]).then_inc(cols_ready, 1)

        @block.vector
        def _(dve):
            dve.memset(rows[:], 0.0).then_inc(cleared, 1)
            for t in range(len(ROWS)):
                dve.wait_ge(cols_ready, t + 1)
                dve.tensor_copy(cols[:, t, :], cols_p[t % 2][:]).then_inc(cols_set, 1)

        @block.scalar
        def _(act):
            act.wait_ge(cleared, 1)
            for t, tile in enumerate(ROWS):
                at = 0
                for key, n in tile:
                    src = a[key]
                    names = "abcdef"[:len(src.shape)]
                    src = src if len(names) == 1 else src.rearrange(f"{' '.join(names)} -> ({' '.join(names)})")
                    act.dma_start(rows[at:at + n, t, :], src.rearrange("(r f) -> r f", f=P)).then_inc(rows_in, 16)
                    at += n


@stage
def modulation_stage(nc, a, ident, cols, mod, vec, x_all, h_dram):
    MB = 3 * KD
    GROUP = 4
    with ExitStack() as ctx:
        def sb(name, *shape):
            return ctx.enter_context(nc.sbuf_tensor("mod_" + name, [P, *shape], F32))

        def sem(name):
            return nc.alloc_semaphore("mod_" + name)

        TILES = TOK // P
        tok = sb("tok", 2, D)
        turned_p = [ctx.enter_context(nc.psum_tensor(f"mod_turned{i}", [P, 4, P], F32)) for i in range(4)]
        tok_in, turned, copied, h_stored = [sem("tok_in0"), sem("tok_in1")], sem("turned"), sem("copied"), sem("h_stored")
        c_in, c_act = sb("c_in", 2, KD), sb("c_act", KD, 2)
        w = [sb(f"w{i}", KD, GROUP * P) for i in range(2)]
        t0, t1, t2 = sb("t0", 8), sb("t1", 8), sb("t2", 8)
        acc = [ctx.enter_context(nc.psum_tensor(f"mod_acc{i}", [2, GROUP * P], F32)) for i in range(2)]
        mod_p = ctx.enter_context(nc.psum_tensor("mod_p", [P, MB, 2], F32))
        mod_row = ctx.enter_context(nc.sbuf_tensor("mod_row", [2, MB * P], F32))
        c_loaded, c_set, w_in = sem("c_loaded"), sem("c_set"), [sem("w_in0"), sem("w_in1")]
        group_ready, group_used = sem("group_ready"), sem("group_used")
        dve_n, act_n = sem("dve_n"), sem("act_n")
        HALF = MB // GROUP // 2
        ready, used = Sig(group_ready, 2), Sig(group_used, 2, 2)
        loads = [Sig(s, 16) for s in w_in]
        w_v = a["w_ada"].rearrange("l (p k) n -> (l p) k n", k=KD)
        block = ctx.enter_context(nc.Block())

        @block.sync
        def _(sp):
            sp.dma_start(c_in[:, 0, :], a["c"].rearrange("b (p k) -> (b p) k", k=KD)).then_inc(c_loaded, 16)
            sp.dma_start(c_in[:, 1, :], a["c_ctx"].rearrange("(p k) -> p k", k=KD)).then_inc(c_loaded, 16)
            with sp.Fori(0, HALF) as it:
                for s in range(2):
                    sp.wait_ge(used.sem, used.value(it, s - 1))
                    sp.dma_start(w[s][:], w_v[:, :, bass.ds(it * (2 * GROUP * P) + s * GROUP * P, GROUP * P)]
                                 ).then_inc(w_in[s], 16)

        @block.tensor
        def _(pe):
            for i in range(TILES):
                pe.wait_ge(tok_in[i % 2], 16 * (i // 2 + 1))
                for g in range(4):
                    n = 4 * i + g
                    if n >= 4:
                        pe.wait_ge(copied, n - 3)
                    for k in range(4):
                        f = 4 * g + k
                        last = pe.transpose(turned_p[n % 4][:, k, :], tok[:, i % 2, f * P:(f + 1) * P], ident)
                    last.then_inc(turned, 1)
            pe.wait_ge(c_set, 1)
            with pe.Fori(0, HALF) as it:
                for s in range(2):
                    pe.wait_ge(w_in[s], loads[s].value(it, 16))
                    pe.wait_ge(used.sem, used.value(it, s - 1))
                    for k in range(KD):
                        last = pe.matmul(acc[s][:, :], c_act[:, k, :], w[s][:, k, :], start=(k == 0), stop=(k == KD - 1))
                    last.then_inc(ready.sem, 1)
            pe.wait_ge(used.sem, used.value(HALF, 0))
            for b in range(MB):
                last = pe.transpose(mod_p[:, b, :], mod_row[:, b * P:(b + 1) * P], ident[0:2, 0:2])
            last.then_inc(turned, 1)

        @block.scalar
        def _(act):
            for i in range(TILES):
                if i >= 2:
                    act.wait_ge(copied, 4 * (i - 1))
                act.dma_start(tok[:, i % 2, :], a["ctx"][0, i * P:(i + 1) * P, :] if i < CTX_CHUNKS else
                              a["x"][0, (i - CTX_CHUNKS) * P:(i - CTX_CHUNKS + 1) * P, :]).then_inc(tok_in[i % 2], 16)
            for g in range(4):
                act.wait_ge(copied, 4 * TILES - 3 + g)
                act.dma_start(h_dram[4 * g:4 * g + 4].rearrange("k p t -> p k t"),
                              x_all[:, 4 * g:4 * g + 4, CTX:TOK]).then_inc(h_stored, 16)
            act.wait_ge(c_loaded, 32)
            act.activation(c_act[:].rearrange("p k w -> p w k"), c_in[:], ACT.Silu).then_inc(c_set, 1)
            act.preload_act_table_set(EXP_LN)
            act.activation(t0[:], columns(cols, "b_lambda_2"), ACT.Abs).then_inc(act_n, 1)
            act.wait_ge(act_n, 1)
            act.activation(t0[:], t0[:], ACT.Exp, scale=-1.0).then_inc(act_n, 1)
            act.wait_ge(act_n, 2)
            act.activation(t0[:], t0[:], ACT.Ln, bias=1.0).then_inc(act_n, 1)
            act.wait_ge(dve_n, 4)
            act.activation(vec["lower"], t1[:], ACT.Exp).then_inc(act_n, 1)
            act.activation(t2[:], t2[:], ACT.Exp).then_inc(act_n, 1)
            act.wait_ge(h_stored, 64)

        @block.vector
        def _(dve):
            dve.sem_inc(used.sem, 2)
            for n in range(4 * TILES):
                i, g = n // 4, n % 4
                dve.wait_ge(turned, n + 1)
                dve.tensor_copy(x_all[:, 4 * g:4 * g + 4, i * P:(i + 1) * P], turned_p[n % 4][:]).then_inc(copied, 1)
            done = [0]

            def link(ins):
                done[0] += 1
                ins.then_inc(dve_n, 1)
                dve.wait_ge(dve_n, done[0])

            l0, l1 = columns(cols, "a_lb_logits_2", 0, 8), columns(cols, "a_lb_logits_2", 8, 8)
            link(dve.tensor_tensor(t1[:], l0, l1, ALU.max))
            link(dve.tensor_tensor(t2[:], l1, t1[:], ALU.subtract))
            link(dve.tensor_tensor(t1[:], l0, t1[:], ALU.subtract))
            link(dve.tensor_scalar(vec["rate8"], columns(cols, "b_lambda_2"), -1.0, 0.0, ALU.mult, ALU.max))
            dve.wait_ge(act_n, 5)
            link(dve.tensor_tensor(vec["rate8"], vec["rate8"], t0[:], ALU.add))
            link(dve.tensor_scalar(vec["rate8"], vec["rate8"], -8.0, None, ALU.mult))
            link(dve.tensor_scalar(vec["rate16"], vec["rate8"], 2.0, None, ALU.mult))
            link(dve.tensor_tensor(t2[:], t2[:], vec["lower"], ALU.add))
            link(dve.reciprocal(t2[:], t2[:]))
            link(dve.tensor_tensor(vec["lower"], vec["lower"], t2[:], ALU.mult))
            b_ada = columns(cols, "b_ada")
            with dve.Fori(0, HALF) as it:
                for s in range(2):
                    dve.wait_ge(ready.sem, ready.value(it, s + 1))
                    here = bass.ds(it * (2 * GROUP * P) + s * GROUP * P, GROUP * P)
                    dve.tensor_copy(mod_row[:, here], acc[s][:, :]).then_inc(used.sem, 1)
            dve.wait_ge(turned, 4 * TILES + 1)
            link(dve.tensor_tensor(mod[:], mod_p[:], b_ada.unsqueeze(2).to_broadcast([P, MB, 2]), ALU.add))
            pre, post = columns(cols, "pre_norm_w"), columns(cols, "post_norm_w")
            for w_, out in ((0, vec["gain_l"]), (1, vec["gain_c"])):
                link(dve.tensor_scalar(out, mod[:, KD:2 * KD, w_], 1.0, None, ALU.add))
                link(dve.tensor_tensor(out, out, pre, ALU.mult))
                link(dve.tensor_copy(vec["shift_l" if w_ == 0 else "shift_c"], mod[:, 0:KD, w_]))
            link(dve.tensor_tensor(vec["post_gain"], mod[:, 2 * KD:MB, 0], post, ALU.mult))


@stage
def norm_stage(nc, name, ones, src, regions, dst=None, parts=None, add_to=None, add_from=None, inv=None,
               feature_count=D):
    K = feature_count // P
    width = max(t0 + n for t0, n, _, _ in regions)
    RING = 4
    pool_sums = [k for k in range(K) if k % 3 == 2]
    dve_sums = [k for k in range(K) if k % 3 != 2]
    inv_only = inv is not None
    pool_last = [k for k in range(K) if k % 3 != 0] if dst is None and not inv_only else []
    dve_last = [k for k in range(K) if k % 3 == 0] if dst is None and not inv_only else []
    with ExitStack() as ctx:
        def sb(nm, *shape):
            return ctx.enter_context(nc.sbuf_tensor(f"{name}_{nm}", [P, *shape], F32))

        def sem(nm):
            return nc.alloc_semaphore(f"{name}_{nm}")

        sq, sum_sq = sb("sq", RING, width), sb("sum_sq", 2, width)
        if inv is None:
            inv = sb("inv", width)
        ring = sq
        eps = sb("eps", 1)
        sums = [ctx.enter_context(nc.psum_tensor(f"{name}_sums{i}", [P, 512], F32)) for i in range(len(regions))]
        eps_set, sq_set, sums_ready = sem("eps_set"), sem("sq_set"), sem("sums_ready")
        dve_added, pool_added = sem("dve_added"), sem("pool_added")
        ln_set, inv_set, normed, shifted, hi_set = sem("ln_set"), sem("inv_set"), sem("normed"), sem("shifted"), sem("hi_set")
        dve_out, pool_out = sem("dve_out"), sem("pool_out")
        added_in = sem("added_in")
        block = ctx.enter_context(nc.Block())

        if add_from is not None:
            @block.sync
            def _(sp):
                sp.dma_start(add_to[:], add_from.rearrange("b p t -> p b t")).then_inc(added_in, 16)

        def free(eng, k, dve_list, pool_list, dve_sem, pool_sem):
            if k in dve_list:
                eng.wait_ge(dve_sem, dve_list.index(k) + 1)
            else:
                eng.wait_ge(pool_sem, pool_list.index(k) + 1)

        def add_squares(eng, blocks, total, done):
            for n, k in enumerate(blocks):
                eng.wait_ge(sq_set, k + 1)
                if n == 0:
                    eng.sem_inc(done, 1)
                    continue
                eng.wait_ge(done, n)
                eng.tensor_tensor(total, total, sq[:, k % RING, :], ALU.add).then_inc(done, 1)

        def last_step(eng, k, done):
            if parts is not None:
                eng.wait_ge(hi_set, k + 1)
                eng.tensor_tensor(parts[1][:, k, 0:width], ring[:, k % RING, :], parts[0][:, k, 0:width].bitcast(F32),
                                  ALU.subtract).then_inc(done, 1)
            else:
                eng.wait_ge(normed, len(regions) * (k + 1))
                if add_from is not None:
                    eng.wait_ge(added_in, 16)
                eng.tensor_tensor(add_to[:, k, 0:width], add_to[:, k, 0:width], ring[:, k % RING, :],
                                  ALU.add).then_inc(done, 1)

        @block.scalar
        def _(act):
            act.preload_act_table_set(EXP_LN)
            for k in range(K):
                if k == dve_sums[0]:
                    out = sum_sq[:, 0, :]
                elif k == pool_sums[0]:
                    out = sum_sq[:, 1, :]
                else:
                    out = sq[:, k % RING, :]
                    if k >= RING:
                        free(act, k - RING, dve_sums, pool_sums, dve_added, pool_added)
                act.activation(out, src[:, k, 0:width], ACT.Square).then_inc(sq_set, 1)
            act.wait_ge(eps_set, 1)
            act.wait_ge(sums_ready, 1)
            for r, (t0, n, _, _) in enumerate(regions):
                act.activation(inv[:, t0:t0 + n], sums[r][:, 0:n], ACT.Ln, scale=1.0 / feature_count,
                               bias=eps[:, 0:1]).then_inc(ln_set, 1)
            act.wait_ge(ln_set, len(regions))
            act.activation(inv[:], inv[:], ACT.Exp, scale=-0.5).then_inc(inv_set, 1)
            n_shifted = 0
            for k in range(K if parts is not None else 0):
                act.wait_ge(normed, len(regions) * (k + 1))
                for t0, n, _, shift in regions:
                    if shift is not None:
                        value = ring[:, k % RING, t0:t0 + n]
                        act.activation(value, value, ACT.Identity, bias=shift[:, k:k + 1]).then_inc(shifted, 1)
                        n_shifted += 1
                if n_shifted:
                    act.wait_ge(shifted, n_shifted)
                act.activation(parts[0][:, k, 0:width], ring[:, k % RING, :], ACT.Copy).then_inc(hi_set, 1)

        @block.tensor
        def _(pe):
            for i, (done, blocks) in enumerate(((dve_added, dve_sums), (pool_added, pool_sums))):
                pe.wait_ge(done, len(blocks))
                for r, (t0, n, _, _) in enumerate(regions):
                    last = pe.matmul(sums[r][:, 0:n], ones, sum_sq[:, i, t0:t0 + n], start=(i == 0), stop=(i == 1))
            last.then_inc(sums_ready, 1)

        @block.vector
        def _(dve):
            dve.memset(eps[:], EPS).then_inc(eps_set, 1)
            add_squares(dve, dve_sums, sum_sq[:, 0, :], dve_added)
            dve.wait_ge(inv_set, 1)
            for k in range(0 if inv_only else K):
                for t0, n, gain, _ in regions:
                    here = slice(t0, t0 + n)
                    out = dst[:, k, here] if dst is not None else ring[:, k % RING, here]
                    if dst is None and k >= RING:
                        free(dve, k - RING, dve_last, pool_last, dve_out, pool_out)
                    dve.scalar_tensor_tensor(out, src[:, k, here], gain[:, k:k + 1], inv[:, here],
                                             ALU.mult, ALU.mult).then_inc(normed, 1)
                if k > 0 and k - 1 in dve_last:
                    last_step(dve, k - 1, dve_out)
            if K - 1 in dve_last:
                last_step(dve, K - 1, dve_out)

        @block.gpsimd
        def _(pool):
            add_squares(pool, pool_sums, sum_sq[:, 1, :], pool_added)
            for k in pool_last:
                last_step(pool, k, pool_out)


class Segment:

    def __init__(self, w, col0, blocks, kind, dst, func=None, taps=None, bias=None, extra=None):
        self.w, self.col0, self.blocks, self.kind, self.dst = w, col0, blocks, kind, dst
        self.func, self.taps, self.bias, self.extra = func, taps, bias, extra
        self.rounds = blocks // 4


@stage
def project_stage(nc, name, x, segments, lat0=0, kd=KD, small=None, x_from=None):
    has_ctx = lat0 > 0
    has_conv = any(s.kind in ("conv5", "conv4") for s in segments)
    C = min(4, kd)
    KC = kd // C
    R = C
    PAIR = 2 * P
    x_hi, x_lo = x
    x_in_dram = x_from is not None and x_from.shape[0] != P
    with ExitStack() as ctx:
        def sb(nm, *shape, dt=F32):
            return ctx.enter_context(nc.sbuf_tensor(f"{name}_{nm}", [P, *shape], dt))

        def sem(nm):
            return nc.alloc_semaphore(f"{name}_{nm}")

        tokens = lat0 + LAT
        w = [sb(f"w{r}", KC, PAIR) for r in range(R)]
        w_hi, w_lo = ([sb(f"w_{part}{r}", KC, PAIR, dt=F32R) for r in range(R)] for part in ("hi", "lo"))
        out_b = [sb(f"out{b}", 2 if any(s.kind == "sig2" for s in segments) else 1, tokens) for b in range(2)]
        raw = [sb(f"raw{b}", tokens) for b in range(2)] if has_conv else None
        mixed = [sb(f"mixed{b}", tokens) for b in range(2)] if has_conv else None
        banks = 2 if has_ctx or any(s.kind == "tok" for s in segments) else 1
        acc = [[[ctx.enter_context(nc.psum_tensor(f"{name}_acc{q}{i}{r}", [P, 512], F32)) for r in range(banks)]
                for i in range(2)] for q in range(2)]
        w_in = [sem(f"w_in{r}") for r in range(R)]
        hi_s, lo_s, done_s, evac_s = sem("w_hi_set"), sem("w_lo_set"), sem("chunk_done"), sem("evacuated")
        tap_s, out_s = sem("taps"), sem("out_set")
        stored_s = [sem("stored0"), sem("stored1")]
        small_in, small_ready, small_set = sem("small_in"), sem("small_ready"), sem("small_set")
        x_in, x_hi_set, x_lo_set = [sem("x_in0"), sem("x_in1")], sem("x_hi_set"), sem("x_lo_set")
        x_ring = sb("x_ring", 2, KC, LAT) if x_in_dram else None
        if small:
            w_small = sb("w_small", kd, small["cols"] if small["token_major"] else 32 + small["cols"] // 2)

        plan, blocks_done, taps_done, outs_done, stores_done = [], 0, 0, 0, 0
        for g in segments:
            tap_n = {"conv5": 9, "conv4": 4, "gate": 2}.get(g.kind, 0)
            chunk0 = blocks_done // 2 * C
            plan.append(dict(
                hi=Sig(hi_s, 2 * C, chunk0), lo=Sig(lo_s, 2 * C, chunk0 + R), done=Sig(done_s, 2 * C, chunk0),
                evac=Sig(evac_s, 4, blocks_done + 4), taps=Sig(tap_s, 4 * tap_n, taps_done), tap_n=tap_n,
                out=Sig(out_s, 4, outs_done),
                loads=[Sig(s, 16 * 2 * C // R, 16 * chunk0 // R) for s in w_in],
                stores=[Sig(s, 32 * (2 if g.kind == "sig2" else 1), stores_done + 16) for s in stored_s]))
            blocks_done += g.blocks
            taps_done += g.blocks * tap_n
            outs_done += g.blocks if g.kind in ("conv5", "conv4") else 0
            if g.kind in ("act", "tok", "conv5", "conv4"):
                stores_done += 8 * g.blocks
            if g.kind == "sig2":
                stores_done += 16 * g.blocks
        block = ctx.enter_context(nc.Block())

        def x_rows(c):
            return x_ring[:, c % 2] if x_in_dram else x_from[:, c * KC:(c + 1) * KC, :]

        def rounds(eng, body):
            for g, pl in zip(segments, plan):
                last = g is segments[-1]
                if g.rounds - last > 0:
                    with eng.Fori(0, g.rounds - last) as it:
                        body(g, pl, it, False)
                if last:
                    body(g, pl, g.rounds - 1, True)

        @block.sync
        def _(sp):
            for g, pl in zip(segments, plan):
                w_v = g.w.rearrange("(k p) n -> p k n", p=P)
                with sp.Fori(0, g.rounds) as it:
                    for j in range(2 * C):
                        q, c = j // C, j % C
                        sp.wait_ge(lo_s, pl["lo"].value(it, j + 1 - R))
                        sp.dma_start(w[j % R][:], w_v[:, c * KC:(c + 1) * KC, bass.ds(it * (2 * PAIR) + (g.col0 + q * PAIR), PAIR)]
                                     ).then_inc(w_in[j % R], 16)

        @block.tensor
        def _(pe):
            if small:
                pe.wait_ge(small_in, 16 * len(small["parts"]))
                if small["token_major"]:
                    for m in range(tokens // P):
                        for k in range(kd):
                            for part in x:
                                last = pe.matmul(acc[1][0][0][:, m * small["cols"]:(m + 1) * small["cols"]],
                                                 part[:, k, m * P:(m + 1) * P].bitcast(F32), w_small[:, k, :],
                                                 start=(k == 0 and part is x_hi), stop=(k == kd - 1 and part is x_lo))
                else:
                    cols = w_small.shape[-1]
                    for k in range(kd):
                        for part in x:
                            last = pe.matmul(acc[1][0][0][0:cols, :], w_small[:, k, :], part[:, k, lat0:tokens].bitcast(F32),
                                             start=(k == 0 and part is x_hi), stop=(k == kd - 1 and part is x_lo))
                last.then_inc(small_ready, 1)
                pe.wait_ge(small_set, 1 if small["token_major"] else 2)

            def body(g, pl, it, final):
                for j in range(2 * C):
                    q, c = j // C, j % C
                    if c == 0:
                        pe.wait_ge(evac_s, pl["evac"].value(it, 2 * q - 2))
                    pe.wait_ge(lo_s, pl["lo"].value(it, j + 1))
                    if x_from is not None and g is segments[0] and q == 0:
                        pe.wait_ge(x_lo_set, c + 1)
                    hi, lo = w_hi[j % R], w_lo[j % R]
                    for kk in range(KC):
                        k = c * KC + kk
                        first, end = k == 0, k == kd - 1
                        if g.kind == "tok":
                            for m in range(LAT // P):
                                out = acc[q][m // 2][m % 2][:, 0:PAIR]
                                here = slice(lat0 + m * P, lat0 + (m + 1) * P)
                                pe.matmul(out, x_hi[:, k, here], hi[:, kk, :], start=first, stop=False)
                                pe.matmul(out, x_hi[:, k, here], lo[:, kk, :], start=False, stop=False)
                                last = pe.matmul(out, x_lo[:, k, here], hi[:, kk, :], start=False, stop=end)
                            continue
                        for i in range(2):
                            wh, wl = hi[:, kk, i * P:(i + 1) * P], lo[:, kk, i * P:(i + 1) * P]
                            lat = acc[q][i][0][:, :]
                            pe.matmul(lat, wh, x_hi[:, k, lat0:tokens], start=first, stop=False)
                            pe.matmul(lat, wh, x_lo[:, k, lat0:tokens], start=False, stop=False)
                            if g.kind == "conv5":
                                context = acc[q][i][1][:, 0:lat0]
                                pe.matmul(context, wh, x_hi[:, k, 0:lat0], start=first, stop=False)
                                pe.matmul(context, wh, x_lo[:, k, 0:lat0], start=False, stop=False)
                                pe.matmul(context, wl, x_hi[:, k, 0:lat0], start=False, stop=end)
                            last = pe.matmul(lat, wl, x_hi[:, k, lat0:tokens], start=False, stop=end)
                    last.then_inc(done_s, 1)

            rounds(pe, body)

        @block.scalar
        def _(act):
            def store(g, pl, it, s):
                b, blk = s % 2, it * 4 + s
                if g.kind in ("conv5", "conv4"):
                    act.wait_ge(out_s, pl["out"].value(it, s + 1))
                elif g.kind in ("act", "sig2", "tok"):
                    act.wait_ge(evac_s, pl["evac"].value(it, s + 1))
                else:
                    return
                if g.kind == "tok":
                    dst = g.dst.rearrange("(m p) f -> p m f", p=P)
                    m = 2 * (s % 2)
                    act.dma_start(dst[:, m:m + 2, bass.ds(it * 512 + (s // 2) * 256, 256)],
                                  out_b[b][:, 0, 0:512].rearrange("p (m f) -> p m f", m=2)).then_inc(stored_s[b], 16)
                elif g.kind == "sig2":
                    for i in range(2):
                        act.dma_start(g.dst[i][blk], out_b[b][:, i, :]).then_inc(stored_s[b], 16)
                elif g.kind == "conv5":
                    act.dma_start(g.dst[blk], out_b[b][:, 0, :]).then_inc(stored_s[b], 16)
                else:
                    act.dma_start(g.dst[blk], out_b[b][:, 0, lat0:tokens]).then_inc(stored_s[b], 16)

            if small:
                act.wait_ge(small_ready, 1)
                if small["token_major"]:
                    act.activation(small["out"][0], acc[1][0][0][:, 0:(tokens // P) * small["cols"]], ACT.Copy).then_inc(small_set, 1)
                else:
                    half = small["cols"] // 2
                    act.activation(small["out"][0], acc[1][0][0][0:half, :], ACT.Copy)
                    act.activation(small["out"][1], acc[1][0][0][32:32 + half, :], ACT.Copy).then_inc(small_set, 1)
            for c in range(C):
                if x_in_dram:
                    act.wait_ge(x_in[c % 2], 16 * (c // 2 + 1))
                if x_from is not None:
                    act.activation(x_hi[:, c * KC:(c + 1) * KC, :], x_rows(c), ACT.Copy).then_inc(x_hi_set, 1)
                act.wait_ge(w_in[c], 16)
                act.activation(w_hi[c][:], w[c][:], ACT.Copy).then_inc(hi_s, 1)

            def body(g, pl, it, final):
                for q in range(2):
                    for c in range(C if not (final and q == 1) else 0):
                        j = (q + 1) * C + c
                        r = j % R
                        act.wait_ge(w_in[r], pl["loads"][r].value(it, 16 * (j // R + 1)))
                        act.wait_ge(done_s, pl["done"].value(it, j + 1 - R))
                        act.activation(w_hi[r][:], w[r][:], ACT.Copy).then_inc(hi_s, 1)
                    act.wait_ge(done_s, pl["done"].value(it, (q + 1) * C))
                    if g.kind in ("conv5", "conv4"):
                        for b in range(2):
                            if g.kind == "conv5":
                                act.activation(raw[b][:, 0:lat0], acc[q][b][1][:, 0:lat0], ACT.Copy)
                            act.activation(raw[b][:, lat0:tokens], acc[q][b][0][:, :], ACT.Copy).then_inc(evac_s, 1)
                    for b in range(2):
                        s = 2 * q + b
                        blk = it * 4 + s
                        st = pl["stores"][b]
                        per_store = 32 if g.kind == "sig2" else 16
                        if g.kind in ("act", "sig2", "tok", "conv5", "conv4"):
                            act.wait_ge(st.sem, st.value(it, per_store * q))
                        bank = acc[q][b][0]
                        if g.kind == "act":
                            act.activation(out_b[b][:, 0, lat0:tokens], bank[:, :], g.func).then_inc(evac_s, 1)
                        elif g.kind == "sig2":
                            act.activation(out_b[b][:, 0, :], bank[:, :], ACT.Sigmoid)
                            act.activation(out_b[b][:, 1, :], bank[:, :], ACT.Sigmoid, scale=-1.0).then_inc(evac_s, 1)
                        elif g.kind == "tok":
                            act.activation(out_b[b][:, 0, 0:PAIR], bank[:, 0:PAIR], ACT.Copy)
                            act.activation(out_b[b][:, 0, PAIR:2 * PAIR], acc[q][b][1][:, 0:PAIR], ACT.Copy).then_inc(evac_s, 1)
                        elif g.kind in ("conv5", "conv4"):
                            act.wait_ge(tap_s, pl["taps"].value(it, (s + 1) * pl["tap_n"]))
                            bias = g.bias[:, bass.ds(blk, 1)] if g.bias is not None else 0.0
                            act.activation(out_b[b][:, 0, :], mixed[b][:], g.func, bias=bias).then_inc(out_s, 1)
                        elif g.kind == "keep":
                            act.activation(g.dst[:, bass.ds(blk, 1), :].rearrange("p o t -> p (o t)"), bank[:, :],
                                           ACT.Copy).then_inc(evac_s, 1)
                        elif g.kind == "gate":
                            act.wait_ge(out_s, pl["out"].value(it, s - 1) + 2)
                            act.activation(out_b[b][:, 0, :], bank[:, :], ACT.Sigmoid).then_inc(evac_s, 1)
                        store(g, pl, it, s)

            rounds(act, body)
            for b in range(2):
                act.wait_ge(stored_s[b], stores_done + 16)

        @block.vector
        def _(dve):
            dve.sem_inc(lo_s, R)
            dve.sem_inc(evac_s, 4)
            dve.sem_inc(stored_s[0], 16)
            dve.sem_inc(stored_s[1], 16)
            if any(g.kind == "gate" for g in segments):
                dve.sem_inc(out_s, 2)
            for c in range(C):
                if x_from is not None:
                    here = slice(c * KC, (c + 1) * KC)
                    dve.wait_ge(x_hi_set, c + 1)
                    dve.tensor_tensor(x_lo[:, here, :], x_rows(c), x_hi[:, here, :].bitcast(F32),
                                      ALU.subtract).then_inc(x_lo_set, 1)
                dve.wait_ge(hi_s, c + 1)
                dve.tensor_tensor(w_lo[c][:], w[c][:], w_hi[c][:].bitcast(F32), ALU.subtract).then_inc(lo_s, 1)

            def taps(g, pl, it, s):
                b, blk = s % 2, it * 4 + s
                n = s * pl["tap_n"]
                dve.wait_ge(evac_s, pl["evac"].value(it, s + 1))
                main = 2 if g.kind == "conv5" else 3

                def weight(j):
                    return g.taps[:, bass.ds(blk + j * g.extra, 1)]

                dve.tensor_scalar(mixed[b][:], raw[b][:], weight(main), None, ALU.mult).then_inc(tap_s, 1)
                n += 1
                rows = (tokens - lat0) // GRID_W
                for j in (0, 1, 3, 4) if g.kind == "conv5" else (0, 1, 2):
                    off = j - main
                    dve.wait_ge(tap_s, pl["taps"].value(it, n))
                    if g.kind == "conv5":
                        out = slice(max(0, -off), lat0 - max(0, off))
                        src = slice(max(0, off), lat0 - max(0, -off))
                        dve.scalar_tensor_tensor(mixed[b][:, out], raw[b][:, src], weight(j), mixed[b][:, out],
                                                 ALU.mult, ALU.add).then_inc(tap_s, 1)
                        out = slice(max(0, -off), GRID_W - max(0, off))
                        src = slice(max(0, off), GRID_W - max(0, -off))
                        m_v = mixed[b][:, lat0:tokens].rearrange("p (r t) -> p r t", r=rows)
                        r_v = raw[b][:, lat0:tokens].rearrange("p (r t) -> p r t", r=rows)
                        dve.scalar_tensor_tensor(m_v[:, :, out], r_v[:, :, src], weight(j), m_v[:, :, out],
                                                 ALU.mult, ALU.add).then_inc(tap_s, 1)
                        n += 2
                    else:
                        dve.scalar_tensor_tensor(mixed[b][:, -off:LAT], raw[b][:, 0:LAT + off], weight(j),
                                                 mixed[b][:, -off:LAT], ALU.mult, ALU.add).then_inc(tap_s, 1)
                        n += 1

            def body(g, pl, it, final):
                for q in range(2):
                    for c in range(C if not (final and q == 1) else 0):
                        j = (q + 1) * C + c
                        r = j % R
                        dve.wait_ge(hi_s, pl["hi"].value(it, j + 1))
                        dve.tensor_tensor(w_lo[r][:], w[r][:], w_hi[r][:].bitcast(F32), ALU.subtract).then_inc(lo_s, 1)
                    for b in range(2):
                        s = 2 * q + b
                        here = bass.ds(it * 4 + s, 1)
                        if g.kind in ("conv5", "conv4"):
                            taps(g, pl, it, s)
                        elif g.kind == "add":
                            dve.wait_ge(done_s, pl["done"].value(it, (q + 1) * C))
                            here = g.dst[:, here, :].rearrange("p o t -> p (o t)")
                            dve.tensor_tensor(here, here, acc[q][b][0][:, :], ALU.add).then_inc(evac_s, 1)
                        elif g.kind == "gate":
                            values, gain, inv = g.extra
                            dve.wait_ge(evac_s, pl["evac"].value(it, s + 1))
                            dve.scalar_tensor_tensor(out_b[b][:, 0, :], out_b[b][:, 0, :], gain[:, here], inv[:],
                                                     ALU.mult, ALU.mult).then_inc(tap_s, 1)
                            dve.wait_ge(tap_s, pl["taps"].value(it, 2 * s + 1))
                            dve.tensor_tensor(out_b[b][:, 0, :], out_b[b][:, 0, :],
                                              values[:, here, :].rearrange("p o t -> p (o t)"), ALU.mult).then_inc(tap_s, 1)
                            dve.wait_ge(tap_s, pl["taps"].value(it, 2 * s + 2))
                            here = g.dst[:, here, :].rearrange("p o t -> p (o t)")
                            dve.tensor_tensor(here, here, out_b[b][:, 0, :], ALU.add).then_inc(out_s, 1)

            rounds(dve, body)

        @block.gpsimd
        def _(pool):
            for c in range(C if x_in_dram else 0):
                if c >= 2:
                    pool.wait_ge(x_lo_set, c - 1)
                pool.dma_start(x_ring[:, c % 2], x_from[c * KC:(c + 1) * KC].rearrange("b p t -> p b t")).then_inc(x_in[c % 2], 16)
            if small:
                at = 0
                if not small["token_major"]:
                    pool.memset(w_small[:], 0.0).then_inc(small_set, 1)
                    pool.wait_ge(small_set, 1)
                for part in small["parts"]:
                    n = part.shape[1]
                    pool.dma_start(w_small[:, :, at:at + n], part.rearrange("(k p) n -> p k n", p=P)).then_inc(small_in, 16)
                    at += n if small["token_major"] else 32


@stage
def first_gates_stage(nc, consts, a, raw, gdn_tabs, ssd_tabs):
    NS, NG = 2 * SSD_H, 2 * GDN_H
    N = NS + NG
    with ExitStack() as ctx:
        def sb(name, *shape):
            return ctx.enter_context(nc.sbuf_tensor("fg_" + name, [P, *shape], F32))

        def sem(name):
            return nc.alloc_semaphore("fg_" + name)

        bias, rate = sb("bias", N), sb("rate", N)
        x, e, soft, log_a = sb("x", CHUNKS, N), sb("e", CHUNKS, N), sb("soft", CHUNKS, N), sb("log_a", CHUNKS, N)
        beta = sb("beta", CHUNKS, NG)
        cum, total, to_end = sb("cum", CHUNKS, N), sb("total", CHUNKS, N), sb("to_end", CHUNKS, N)
        cum_p = ctx.enter_context(nc.psum_tensor("fg_cum_p", [P, CHUNKS, N], F32))
        total_p = ctx.enter_context(nc.psum_tensor("fg_total_p", [P, CHUNKS, N], F32))
        loaded, dve_n, act_n, sums_ready = sem("loaded"), sem("dve_n"), sem("act_n"), sem("sums_ready")
        block = ctx.enter_context(nc.Block())

        @block.sync
        def _(sp):
            for dst, ssd, gdn in ((bias, "ssd_dt_bias", "gdn_dt_bias"), (rate, "ssd_a_log", "gdn_a_log")):
                sp.dma_start(dst[:, 0:NS], a[ssd].rearrange("l d h -> l (d h)").to_broadcast([P, NS])).then_inc(loaded, 16)
                sp.dma_start(dst[:, NS:N], a[gdn].rearrange("l d h -> l (d h)").to_broadcast([P, NG])).then_inc(loaded, 16)

        @block.vector
        def _(dve):
            done = [0]

            def link(ins):
                done[0] += 1
                ins.then_inc(dve_n, 1)
                dve.wait_ge(dve_n, done[0])

            dve.wait_ge(loaded, 64)
            link(dve.tensor_tensor(x[:, :, 0:NS], raw[:, :, 0:NS],
                                   bias[:, 0:NS].unsqueeze(1).to_broadcast([P, CHUNKS, NS]), ALU.add))
            link(dve.tensor_tensor(x[:, :, NS:N], raw[:, :, NS + NG:GATES],
                                   bias[:, NS:N].unsqueeze(1).to_broadcast([P, CHUNKS, NG]), ALU.add))
            link(dve.tensor_scalar(soft[:], x[:], 0.0, None, ALU.max))
            dve.wait_ge(act_n, 5)
            link(dve.tensor_tensor(soft[:], soft[:], e[:], ALU.add))
            link(dve.tensor_tensor(log_a[:], soft[:], rate[:].unsqueeze(1).to_broadcast([P, CHUNKS, N]), ALU.mult))
            link(dve.tensor_scalar(log_a[:], log_a[:], -1.0, None, ALU.mult))
            link(dve.tensor_scalar(beta[:], beta[:], 1.0, None, ALU.add))
            link(dve.reciprocal(beta[:], beta[:]))
            dve.wait_ge(sums_ready, 1)
            link(dve.tensor_copy(cum[:], cum_p[:]))
            link(dve.tensor_copy(total[:], total_p[:]))
            link(dve.tensor_tensor(to_end[:], total[:], cum[:], ALU.subtract))
            dve.wait_ge(act_n, 7)

            def ssd(t):
                return ssd_tabs[:, t].rearrange("p c d h -> p c (d h)")

            def gdn(t):
                return gdn_tabs[:, t].rearrange("p c d h -> p c (d h)")

            link(dve.tensor_copy(ssd(0), soft[:, :, 0:NS]))
            link(dve.tensor_tensor(ssd(1), soft[:, :, 0:NS], to_end[:, :, 0:NS], ALU.mult))
            link(dve.tensor_copy(ssd(2), total[:, :, 0:NS]))
            link(dve.tensor_copy(ssd(3), cum[:, :, 0:NS]))
            link(dve.tensor_copy(gdn(0), beta[:]))
            link(dve.tensor_copy(gdn(2), to_end[:, :, NS:N]))
            link(dve.tensor_copy(gdn(3), total[:, :, NS:N]))
            link(dve.tensor_copy(gdn(4), cum[:, :, NS:N]))

        @block.scalar
        def _(act):
            act.preload_act_table_set(EXP_LN)
            act.wait_ge(loaded, 64)
            act.activation(rate[:], rate[:], ACT.Exp).then_inc(act_n, 1)
            act.activation(beta[:], raw[:, :, NS:NS + NG], ACT.Exp, scale=-1.0).then_inc(act_n, 1)
            act.wait_ge(dve_n, 2)
            act.activation(e[:], x[:], ACT.Abs).then_inc(act_n, 1)
            act.wait_ge(act_n, 3)
            act.activation(e[:], e[:], ACT.Exp, scale=-1.0).then_inc(act_n, 1)
            act.wait_ge(act_n, 4)
            act.activation(e[:], e[:], ACT.Ln, bias=1.0).then_inc(act_n, 1)
            act.wait_ge(dve_n, 11)
            act.activation(to_end[:], to_end[:], ACT.Exp).then_inc(act_n, 1)
            act.activation(total[:], total[:], ACT.Exp).then_inc(act_n, 1)
            act.wait_ge(dve_n, 19)
            act.activation(gdn_tabs[:, 1].rearrange("p c d h -> p c (d h)"), cum[:, :, NS:N], ACT.Exp).then_inc(act_n, 1)

        @block.tensor
        def _(pe):
            pe.wait_ge(dve_n, 6)
            for lo, n in ((0, SSD_H), (NS, GDN_H)):
                for d in range(2):
                    cols = slice(lo + d * n, lo + (d + 1) * n)
                    pe.matmul(cum_p[:, :, cols], consts["causal"][:, d, :], log_a[:, :, cols], start=True, stop=True)
            pe.matmul(total_p[:], consts["ones"][:], log_a[:], start=True, stop=True).then_inc(sums_ready, 1)


@stage
def lru_stage(nc, a, cols, vec, xT, zT, yT):
    B = 8
    with ExitStack() as ctx:
        def sb(name, *shape):
            return ctx.enter_context(nc.sbuf_tensor("lru_" + name, [P, *shape], F32))

        def sem(name):
            return nc.alloc_semaphore("lru_" + name)

        x, z, r, i, dec = sb("x", B, LAT), sb("z", B, LAT), sb("r", B, LAT), sb("i", B, LAT), sb("dec", B, LAT)
        sq = sb("sq", B, LAT)
        wr, wi = sb("wr", B, P), sb("wi", B, P)
        acc = [ctx.enter_context(nc.psum_tensor(f"lru_acc{n}", [P, LAT], F32)) for n in range(4)]
        loaded, z_loaded, ready, evacuated = sem("loaded"), sem("z_loaded"), sem("ready"), sem("evacuated")
        a_set, sq_exp, th_set = sem("a_set"), sem("sq_exp"), sem("th_set")
        gap, root, ix, u_set, hs, y_set = sem("gap"), sem("root"), sem("ix"), sem("u_set"), sem("hs"), sem("y_set")
        stored = sem("stored")
        block = ctx.enter_context(nc.Block())

        @block.sync
        def _(sp):
            sp.dma_start(x[:], xT.rearrange("b p t -> p b t")).then_inc(loaded, 16)
            sp.dma_start(wr[:], a["b_w_r_2"].rearrange("l n c d -> c (l n) d")).then_inc(loaded, 16)
            sp.dma_start(wi[:], a["b_w_i_2"].rearrange("l n c d -> c (l n) d")).then_inc(loaded, 16)
            sp.dma_start(z[:], zT.rearrange("b p t -> p b t")).then_inc(z_loaded, 16)
            for b in range(B):
                sp.wait_ge(y_set, b + 1)
                sp.dma_start(yT[b], r[:, b, :]).then_inc(stored, 16)
            sp.wait_ge(stored, 16 * B)

        @block.tensor
        def _(pe):
            pe.wait_ge(loaded, 48)
            for b in range(B):
                for j, w in enumerate((wr, wi)):
                    n = 2 * b + j
                    if n >= 4:
                        pe.wait_ge(evacuated, n - 3)
                    pe.matmul(acc[n % 4][:], w[:, b, :], x[:, b, :], start=True, stop=True).then_inc(ready, 1)

        @block.scalar
        def _(act):
            b_r, b_i = columns(cols, "b_b_r_2"), columns(cols, "b_b_i_2")
            for b in range(B):
                for j, (bias, dst) in enumerate(((b_r, r), (b_i, i))):
                    n = 2 * b + j
                    act.wait_ge(ready, n + 1)
                    act.activation(dst[:, b, :], acc[n % 4][:], ACT.Sigmoid, bias=bias[:, b:b + 1]).then_inc(evacuated, 1)
            act.wait_ge(evacuated, 2 * B)
            for b in range(B):
                act.activation(dec[:, b, :], r[:, b, :], ACT.Exp, scale=vec["rate8"][:, b:b + 1]).then_inc(a_set, 1)
                act.activation(sq[:, b, :], r[:, b, :], ACT.Exp, scale=vec["rate16"][:, b:b + 1]).then_inc(sq_exp, 1)
                act.activation(r[:, b, :], r[:, b, :], ACT.Tanh, scale=vec["rate8"][:, b:b + 1]).then_inc(th_set, 1)
            for b in range(B):
                act.wait_ge(gap, b + 1)
                act.activation(sq[:, b, :], sq[:, b, :], ACT.Sqrt, scale=-1.0).then_inc(root, 1)

        @block.gpsimd
        def _(pool):
            for b in range(B):
                pool.wait_ge(evacuated, 2 * b + 2)
                pool.tensor_tensor(i[:, b, :], i[:, b, :], x[:, b, :], ALU.mult).then_inc(ix, 1)

        @block.vector
        def _(dve):
            for b in range(B):
                dve.wait_ge(sq_exp, b + 1)
                dve.wait_ge(th_set, b + 1)
                dve.scalar_tensor_tensor(sq[:, b, :], sq[:, b, :], 1.0, r[:, b, :], ALU.add, ALU.mult).then_inc(gap, 1)
            dve.wait_ge(z_loaded, 16)
            for b in range(B):
                dve.wait_ge(root, b + 1)
                dve.wait_ge(ix, b + 1)
                dve.tensor_tensor(i[:, b, :], i[:, b, :], sq[:, b, :], ALU.mult).then_inc(u_set, 1)
                dve.wait_ge(u_set, b + 1)
                dve.tensor_tensor_scan(x[:, b, :], dec[:, b, :], i[:, b, :], 0.0, ALU.mult, ALU.add).then_inc(hs, 1)
                dve.wait_ge(hs, b + 1)
                dve.tensor_tensor(r[:, b, :], x[:, b, :], z[:, b, :], ALU.mult).then_inc(y_set, 1)


@stage
def turn_in_stage(nc, name, ident, dst, src):
    F = src.shape[1]
    with ExitStack() as ctx:
        tok = ctx.enter_context(nc.sbuf_tensor(name + "_tok", [P, LAT // P, F], F32))
        turned_p = [ctx.enter_context(nc.psum_tensor(f"{name}_p{i}", [P, LAT], F32)) for i in range(2)]
        loaded, turned, copied = (nc.alloc_semaphore(f"{name}_{s}") for s in ("in", "turned", "copied"))
        block = ctx.enter_context(nc.Block())

        @block.sync
        def _(sp):
            sp.dma_start(tok[:], src.rearrange("(m p) f -> p m f", p=P)).then_inc(loaded, 16)

        @block.tensor
        def _(pe):
            pe.wait_ge(loaded, 16)
            for f in range(F // P):
                if f >= 2:
                    pe.wait_ge(copied, f - 1)
                for m in range(LAT // P):
                    last = pe.transpose(turned_p[f % 2][:, m * P:(m + 1) * P], tok[:, m, f * P:(f + 1) * P], ident)
                last.then_inc(turned, 1)

        @block.vector
        def _(dve):
            for f in range(F // P):
                dve.wait_ge(turned, f + 1)
                dve.tensor_copy(dst[:, f, :], turned_p[f % 2][:]).then_inc(copied, 1)


@stage
def turn_out_stage(nc, ident, src, out):
    with ExitStack() as ctx:
        tok = ctx.enter_context(nc.sbuf_tensor("to_tok", [P, 2, D], F32))
        turned_p = [ctx.enter_context(nc.psum_tensor(f"to_p{i}", [P, 4, P], F32)) for i in range(4)]
        turned, copied = nc.alloc_semaphore("to_turned"), nc.alloc_semaphore("to_copied")
        stored = [nc.alloc_semaphore(f"to_stored{i}") for i in range(2)]
        block = ctx.enter_context(nc.Block())

        @block.tensor
        def _(pe):
            for m in range(LAT // P):
                for g in range(4):
                    n = 4 * m + g
                    if n >= 4:
                        pe.wait_ge(copied, n - 3)
                    for k in range(4):
                        last = pe.transpose(turned_p[n % 4][:, k, :], src[:, 4 * g + k, m * P:(m + 1) * P], ident)
                    last.then_inc(turned, 1)

        @block.vector
        def _(dve):
            for m in range(LAT // P):
                if m >= 2:
                    dve.wait_ge(stored[m % 2], 16 * (m // 2))
                for g in range(4):
                    n = 4 * m + g
                    dve.wait_ge(turned, n + 1)
                    dve.tensor_copy(tok[:, m % 2, g * 512:(g + 1) * 512].rearrange("p (k f) -> p k f", k=4),
                                    turned_p[n % 4][:]).then_inc(copied, 1)

        @block.sync
        def _(sp):
            for m in range(LAT // P):
                sp.wait_ge(copied, 4 * m + 4)
                sp.dma_start(out[m * P:(m + 1) * P, :], tok[:, m % 2, :]).then_inc(stored[m % 2], 16)
            for i in range(2):
                sp.wait_ge(stored[i], 32)


@stage
def bias_stage(nc, a, bias):
    loaded = nc.alloc_semaphore("ml_bias_in")
    with nc.Block() as block:
        @block.sync
        def _(sp):
            sp.dma_start(bias[:, 0:1], a["c_b_i_2"].rearrange("l h -> h l")).then_inc(loaded, 16)
            sp.dma_start(bias[:, 1:2], a["c_b_f_2"].rearrange("l h -> h l")).then_inc(loaded, 16)
            sp.wait_ge(loaded, 32)


@stage
def skip_stage(nc, a, skip):
    loaded, made = nc.alloc_semaphore("skip_in"), nc.alloc_semaphore("skip_set")
    with nc.sbuf_tensor("skip_row", [P, SSD_H], F32) as row, nc.Block() as block:
        @block.sync
        def _(sp):
            sp.dma_start(row[:], a["ssd_d"].to_broadcast([P, SSD_H])).then_inc(loaded, 16)

        @block.vector
        def _(dve):
            dve.wait_ge(loaded, 16)
            for s in range(2):
                part = slice(s * SSD_P, (s + 1) * SSD_P)
                dve.tensor_copy(skip[part, :], row[part, :].rearrange("p (b s) -> p s b", s=2)[:, s, :]).then_inc(made, 1)


def kernel_program(nc, a, out):
    def scratch(name, *shape):
        return nc.dram_tensor("s_" + name, shape, F32).ap()

    w_in = a["w_in"].rearrange("l k n -> (l k) n")
    e_in = a["e_w_in_2"].rearrange("l k n -> (l k) n")
    o_in = a["o_w_in_2"].rearrange("l k n -> (l k) n")

    with ExitStack() as ctx:
        def sb(name, *shape):
            return ctx.enter_context(nc.sbuf_tensor(name, [P, *shape], F32))

        consts = {key: sb("k_" + key, *shape) for key, shape in CONSTS.items()}
        cols = sb("cols", len(ROWS), P)
        vec_t = sb("vec", 5 * KD + 3 * 8)
        vec = {}
        for n, key in enumerate(("gain_l", "shift_l", "gain_c", "shift_c", "post_gain")):
            vec[key] = vec_t[:, n * KD:(n + 1) * KD]
        for n, key in enumerate(("rate8", "rate16", "lower")):
            vec[key] = vec_t[:, 5 * KD + 8 * n:5 * KD + 8 * (n + 1)]

        def split_pair(owner, name, *shape):
            return [owner.enter_context(nc.sbuf_tensor(f"{name}_{part}", [P, *shape], F32R)) for part in ("hi", "lo")]

        h_dram = scratch("h", KD, P, LAT)
        z1, y1 = scratch("z1", KD, P, LAT), scratch("y1", KD, P, LAT)
        xbc, qkv = scratch("xbc", XBC_BLOCKS, P, TOK), scratch("qkv", QKV_BLOCKS, P, TOK)
        with ExitStack() as first:
            gdn_tabs = first.enter_context(nc.sbuf_tensor("gdn_tabs", [P, GDN_TABS, CHUNKS, 2, GDN_H], F32))
            ssd_tabs = first.enter_context(nc.sbuf_tensor("ssd_tabs", [P, SSD_TABS, CHUNKS, 2, SSD_H], F32))
            raw_gates = first.enter_context(nc.sbuf_tensor("raw_gates", [P, CHUNKS, GATES], F32))
            skip = first.enter_context(nc.sbuf_tensor("skip", [P, 8], F32))
            setup_stage(nc, a, consts, cols)
            with ExitStack() as inner:
                with nc.sbuf_tensor("x1", [P, KD, TOK], F32, side="right") as x_all:
                    with nc.sbuf_tensor("mod", [P, 3 * KD, 2], F32) as mod:
                        modulation_stage(nc, a, consts["ident"][:], cols, mod, vec, x_all, h_dram)
                    u = split_pair(inner, "u1", KD, TOK)
                    norm_stage(nc, "pre", consts["ones"][:], x_all, [
                        (0, CTX, vec["gain_c"], vec["shift_c"]),
                        (CTX, LAT, vec["gain_l"], vec["shift_l"])], parts=u)
                project_stage(nc, "p1", u, [
                    Segment(w_in, OFF_QKV, QKV_BLOCKS, "conv5", qkv, ACT.Silu, columns(cols, "conv_gdn_w"), None, QKV_BLOCKS),
                    Segment(w_in, OFF_XBC, XBC_BLOCKS, "conv5", xbc, ACT.Silu, columns(cols, "conv_ssd_w"),
                            columns(cols, "conv_ssd_b"), XBC_BLOCKS),
                    Segment(w_in, 0, Z_BLOCKS, "act", z1, ACT.Silu),
                ], lat0=CTX, small=dict(cols=GATES, token_major=True, out=[flat(raw_gates[:])],
                                        parts=[w_in[:, OFF_DT:OFF_QKV], w_in[:, OFF_BETA:OFF_BETA + 4 * GDN_H]]))
            first_gates_stage(nc, consts, a, raw_gates, gdn_tabs, ssd_tabs)
            skip_stage(nc, a, skip)
            gdn_stage(nc, consts, qkv, gdn_tabs, columns(cols, "gdn_norm_w"), z1[8:16], y1[8:16])
            ssd_stage(nc, consts, xbc, ssd_tabs, skip, columns(cols, "ssd_norm_w"), z1[0:8], y1[0:8])
        with nc.sbuf_tensor("mix1", [P, KD, LAT], F32, side="right") as mix:
            with ExitStack() as inner:
                y = split_pair(inner, "y_in1", KD, LAT)
                project_stage(nc, "o1", y, [Segment(a["w_out"].rearrange("l k n -> (l k) n"), 0, KD, "keep", mix)],
                              x_from=y1)
            h = sb("h", KD, LAT)
            norm_stage(nc, "post", consts["ones"][:], mix, [(0, LAT, vec["post_gain"], None)], add_to=h, add_from=h_dram)

        q2, s2, n2 = (scratch(n, 8, P, LAT) for n in ("q2", "s2", "n2"))
        v2, za2, xb2, zb2 = scratch("v2", LAT, 1024), scratch("za2", 8, P, LAT), scratch("xb2", 8, P, LAT), scratch("zb2", 8, P, LAT)
        y2 = scratch("y2", KD, P, LAT)
        with ExitStack() as inner:
            u = split_pair(inner, "u2", KD, LAT)
            norm_stage(nc, "en", consts["ones"][:], h, [(0, LAT, columns(cols, "e_norm_2"), None)], parts=u)
            project_stage(nc, "p2", u, [
                Segment(e_in, 0, 8, "act", q2, ACT.Silu),
                Segment(e_in, 1024, 8, "sig2", (s2, n2)),
                Segment(e_in, 2048, 8, "tok", v2),
                Segment(e_in, 3072, 8, "act", za2, ACT.Silu),
                Segment(e_in, 4096, 8, "conv4", xb2, ACT.Identity, columns(cols, "b_conv_w_2"), columns(cols, "b_conv_b_2"), 8),
                Segment(e_in, 5120, 8, "act", zb2, ACT.Silu),
            ])
        hgrn_stage(nc, consts, q2, s2, n2, v2, vec["lower"], columns(cols, "a_norm_2"), za2, y2[0:8])
        lru_stage(nc, a, cols, vec, xb2, zb2, y2[8:16])
        with ExitStack() as inner:
            y = split_pair(inner, "y_in2", KD, LAT)
            project_stage(nc, "o2", y, [Segment(a["e_w_out_2"].rearrange("l k n -> (l k) n"), 0, KD, "add", h)], x_from=y2)
        embed_stages(nc, a, consts, cols, h, 0)

        qk3, v3 = scratch("qk3", 16, P, LAT), scratch("v3", LAT, D)
        og3, z3, y3 = scratch("og3", 16, P, LAT), scratch("z3", 16, P, LAT), scratch("y3", 16, P, LAT)
        with ExitStack() as last:
            tabs = last.enter_context(nc.sbuf_tensor("ml_tabs", [P, ML_TABS, ML_CH, ML_H], F32))
            gates = last.enter_context(nc.sbuf_tensor("ml_raw", [ML_H, 2, LAT], F32))
            with ExitStack() as inner:
                u = split_pair(inner, "u3", KD, LAT)
                norm_stage(nc, "on", consts["ones"][:], h, [(0, LAT, columns(cols, "o_norm_2"), None)], parts=u)
                project_stage(nc, "p3", u, [
                    Segment(o_in, 0, 16, "conv4", qk3, ACT.Silu, columns(cols, "c_conv_w_2"), columns(cols, "c_conv_b_2"), 16),
                    Segment(o_in, 2048, 16, "tok", v3),
                    Segment(o_in, 4096, 16, "act", og3, ACT.Sigmoid),
                    Segment(o_in, 6144, 16, "act", z3, ACT.Silu),
                ], small=dict(cols=2 * ML_H, token_major=False, out=[gates[:, 0, :], gates[:, 1, :]],
                              parts=[o_in[:, 8192:8192 + ML_H], o_in[:, 8192 + ML_H:8192 + 2 * ML_H]]))
            bias = last.enter_context(nc.sbuf_tensor("ml_bias", [ML_H, 2], F32))
            bias_stage(nc, a, bias)
            mlstm_gates_stage(nc, consts, gates[:, 0, :], gates[:, 1, :], bias[:, 0:1], bias[:, 1:2], tabs)
            mlstm_stage(nc, consts, qk3, v3, tabs, columns(cols, "c_norm_2"), og3, z3, y3)
        with ExitStack() as inner:
            y = split_pair(inner, "y_in3", KD, LAT)
            project_stage(nc, "o3", y, [Segment(a["o_w_out_2"].rearrange("l k n -> (l k) n"), 0, KD, "add", h)], x_from=y3)
        embed_stages(nc, a, consts, cols, h, 1)
        with nc.sbuf_tensor("u4", [P, KD, LAT], F32) as u:
            norm_stage(nc, "fn", consts["ones"][:], h, [(0, LAT, columns(cols, "final_norm_2"), None)], dst=u)
            turn_out_stage(nc, consts["ident"][:], u, out.rearrange("b t f -> (b t) f"))


def embed_stages(nc, a, consts, cols, h, i):
    with ExitStack() as ctx:
        def split_pair(owner, name, blocks):
            return [owner.enter_context(nc.sbuf_tensor(f"{name}{i}_{part}", [P, blocks, LAT], F32R)) for part in ("hi", "lo")]

        pl = ctx.enter_context(nc.sbuf_tensor(f"pl{i}", [P, KD, LAT], F32))
        with ExitStack() as inner:
            p_t = inner.enter_context(nc.sbuf_tensor(f"p_t{i}", [P, 2, LAT], F32))
            p_parts = split_pair(inner, "p", 2)
            turn_in_stage(nc, f"ti{i}", consts["ident"][:], p_t, a["p_2"][i, 0])
            project_stage(nc, f"e{i}", p_parts, [Segment(a["ple_w_2"][i], 0, KD, "keep", pl)], kd=2,
                          x_from=p_t)
        gain = columns(cols, "ple_norm_2", 16 * i, 16)
        pl_inv = ctx.enter_context(nc.sbuf_tensor(f"pl_inv{i}", [P, LAT], F32))
        norm_stage(nc, f"pn{i}", consts["ones"][:], pl, [(0, LAT, gain, None)], inv=pl_inv)
        h_parts = split_pair(ctx, "h", KD)
        project_stage(nc, f"g{i}", h_parts, [Segment(a["ple_gate_w_2"][i], 0, KD, "gate", h,
                                                     extra=(pl, gain, pl_inv))], x_from=h)


_INS = ["x", "c", "ctx", "c_ctx", "w_ada", "b_ada", "pre_norm_w", "post_norm_w", "w_in", "conv_ssd_w", "conv_ssd_b",
        "conv_gdn_w", "ssd_a_log", "ssd_dt_bias", "ssd_d", "ssd_norm_w", "gdn_a_log", "gdn_dt_bias", "gdn_norm_w",
        "w_out", "p_2", "e_norm_2", "e_w_in_2", "a_lb_logits_2", "a_norm_2", "b_conv_w_2", "b_conv_b_2", "b_w_r_2",
        "b_b_r_2", "b_w_i_2", "b_b_i_2", "b_lambda_2", "e_w_out_2", "o_norm_2", "o_w_in_2", "c_conv_w_2",
        "c_conv_b_2", "c_b_i_2", "c_b_f_2", "c_norm_2", "o_w_out_2", "ple_w_2", "ple_norm_2", "ple_gate_w_2",
        "final_norm_2"]


def kernel(**inputs):
    import numpy as _np
    import concourse.bacc as _bacc
    from concourse import mybir as _mybir
    from concourse.bass_utils import run_bass_kernel_spmd as _run

    nc = _bacc.Bacc("TRN2", target_bir_lowering=False, num_devices=1)
    arrays, args = {}, {}
    for name, value in [(n, inputs[n]) for n in _INS] + list(constants().items()):
        value = _np.ascontiguousarray(value)
        arrays[f"in_{name}_dram"] = value
        args[name] = nc.dram_tensor(f"in_{name}_dram", value.shape, _mybir.dt.from_np(value.dtype), kind="ExternalInput").ap()
    out = nc.dram_tensor("out_0_dram", (1, LAT, D), _mybir.dt.float32, kind="ExternalOutput").ap()
    kernel_program(nc, args, out)
    return _run(nc, [arrays], core_ids=[0]).results[0]["out_0_dram"]
```
